# Optimizing a Trainium2 kernel written in Bass

```python
import math
import jax, jax.numpy as jnp
from jax import lax
import numpy as np

D_MODEL = 1024
BATCH = 1
SEQ = 1024
DEPTH = 1
DEC_BATCH = 1
DEC_SEQ = 32
PAST_LEN = 256

CHUNK = 64
Q_BLOCK = 128
SB_HEADS = 8
SB_HEAD_DIM = 64
DIFF_HEADS = 4
DIFF_HEAD_DIM = 64
SB_WIDTH = SB_HEADS * SB_HEAD_DIM
DIFF_WIDTH = DIFF_HEADS * 2 * DIFF_HEAD_DIM
MIX_WIDTH = SB_WIDTH + DIFF_WIDTH
IN_WIDTH = 3 * SB_WIDTH + 3 * DIFF_WIDTH
D_FF = 2816
RMS_EPS = 1e-6
LAMBDA_STD = 0.1

kernel_name = 'hymba_stickbreak_diffattn_macaron_step'

def rms_norm(x, g):
    xf = x.astype(jnp.float32)
    y = xf * lax.rsqrt(jnp.mean(xf * xf, axis=-1, keepdims=True) + RMS_EPS)
    return (y * g.astype(jnp.float32)).astype(x.dtype)

def swiglu(x, w_gate, w_up, w_down):
    return (jax.nn.silu(x @ w_gate) * (x @ w_up)) @ w_down

def alibi_slopes(n):
    return 2.0 ** (-8.0 * jnp.arange(1, n + 1, dtype=jnp.float32) / n)

def stick_breaking(q, k, v, q_pos, k_pos):
    z = jnp.einsum('bqhd,bkhd->bhqk', q, k).astype(jnp.float32) * (SB_HEAD_DIM ** -0.5)
    mask = k_pos[None, :] < q_pos[:, None]
    log_stay = jnp.where(mask, jax.nn.log_sigmoid(-z), 0.0)
    between = lax.cumsum(log_stay, axis=3, reverse=True) - log_stay
    w = jnp.where(mask, jnp.exp(jax.nn.log_sigmoid(z) + between), 0.0)
    return jnp.einsum('bhqk,bkhd->bqhd', w, v.astype(jnp.float32))

def diff_attention(q, k, v, q_pos, k_pos, lam):
    scale = DIFF_HEAD_DIM ** -0.5
    q1, q2 = q[..., :DIFF_HEAD_DIM], q[..., DIFF_HEAD_DIM:]
    k1, k2 = k[..., :DIFF_HEAD_DIM], k[..., DIFF_HEAD_DIM:]
    dist = jnp.abs(q_pos[:, None] - k_pos[None, :]).astype(jnp.float32)
    bias = -alibi_slopes(DIFF_HEADS)[:, None, None] * dist
    mask = (k_pos // CHUNK)[None, :] <= (q_pos // CHUNK)[:, None]

    def attn_map(qc, kc):
        s = jnp.einsum('bqhd,bkhd->bhqk', qc, kc).astype(jnp.float32) * scale + bias
        return jax.nn.softmax(jnp.where(mask, s, -jnp.inf), axis=-1)

    w = attn_map(q1, k1) - lam * attn_map(q2, k2)
    return jnp.einsum('bhqk,bkhd->bqhd', w, v.astype(jnp.float32))

def sweep_query_blocks(fn, q, q_pos):
    b, s = q.shape[:2]
    nb = s // Q_BLOCK
    qb = jnp.swapaxes(q.reshape((b, nb, Q_BLOCK) + q.shape[2:]), 0, 1)
    pb = q_pos.reshape(nb, Q_BLOCK)
    ob = lax.map(lambda a: fn(a[0], a[1]), (qb, pb))
    return jnp.swapaxes(ob, 0, 1).reshape((b, s) + ob.shape[3:])

def run_attention(fn, q, q_pos):
    n = q.shape[1]
    if n % Q_BLOCK == 0 and n > Q_BLOCK:
        return sweep_query_blocks(fn, q, q_pos)
    return fn(q, q_pos)

def token_mixer(hn, past, w_in, lam_q1, lam_k1, lam_q2, lam_k2, subln_g, w_out, lam_init):
    b, n, _ = hn.shape
    p = hn @ w_in
    cuts = [SB_WIDTH, 2 * SB_WIDTH, 3 * SB_WIDTH, 3 * SB_WIDTH + DIFF_WIDTH, 3 * SB_WIDTH + 2 * DIFF_WIDTH]
    sb_q, sb_k, sb_v, d_q, d_k, d_v = jnp.split(p, cuts, axis=-1)
    sb_shape = (b, n, SB_HEADS, SB_HEAD_DIM)
    d_shape = (b, n, DIFF_HEADS, 2 * DIFF_HEAD_DIM)
    sb_q, sb_k, sb_v = sb_q.reshape(sb_shape), sb_k.reshape(sb_shape), sb_v.reshape(sb_shape)
    d_q, d_k, d_v = d_q.reshape(d_shape), d_k.reshape(d_shape), d_v.reshape(d_shape)
    if past is None:
        offset = 0
        sb_k_all, sb_v_all, d_k_all, d_v_all = sb_k, sb_v, d_k, d_v
    else:
        c_sb_k, c_sb_v, c_d_k, c_d_v = past
        offset = c_sb_k.shape[1]
        sb_k_all = jnp.concatenate([c_sb_k.astype(sb_k.dtype), sb_k], axis=1)
        sb_v_all = jnp.concatenate([c_sb_v.astype(sb_v.dtype), sb_v], axis=1)
        d_k_all = jnp.concatenate([c_d_k.astype(d_k.dtype), d_k], axis=1)
        d_v_all = jnp.concatenate([c_d_v.astype(d_v.dtype), d_v], axis=1)
    q_pos = offset + jnp.arange(n, dtype=jnp.int32)
    k_pos = jnp.arange(offset + n, dtype=jnp.int32)
    lam = (jnp.exp(jnp.sum(lam_q1.astype(jnp.float32) * lam_k1.astype(jnp.float32)))
           - jnp.exp(jnp.sum(lam_q2.astype(jnp.float32) * lam_k2.astype(jnp.float32))) + lam_init)
    sb_o = run_attention(lambda qb, pb: stick_breaking(qb, sb_k_all, sb_v_all, pb, k_pos), sb_q, q_pos)
    d_o = run_attention(lambda qb, pb: diff_attention(qb, d_k_all, d_v_all, pb, k_pos, lam), d_q, q_pos)
    d_o = rms_norm(d_o, subln_g) * (1.0 - lam_init)
    o = jnp.concatenate([sb_o.reshape(b, n, SB_WIDTH), d_o.reshape(b, n, DIFF_WIDTH)], axis=-1)
    return o.astype(hn.dtype) @ w_out, (sb_k, sb_v, d_k, d_v)

def encoder_layer(x, past, ff1_pre_g, ff1_w_gate, ff1_w_up, ff1_w_down, ff1_post_g,
                  mix_pre_g, w_in, lam_q1, lam_k1, lam_q2, lam_k2, subln_g, w_out, mix_post_g,
                  ff2_pre_g, ff2_w_gate, ff2_w_up, ff2_w_down, ff2_post_g, final_g, lam_init):
    h = x + 0.5 * rms_norm(swiglu(rms_norm(x, ff1_pre_g), ff1_w_gate, ff1_w_up, ff1_w_down), ff1_post_g)
    mix, rows = token_mixer(rms_norm(h, mix_pre_g), past, w_in, lam_q1, lam_k1, lam_q2, lam_k2,
                            subln_g, w_out, lam_init)
    h = h + rms_norm(mix, mix_post_g)
    h = h + 0.5 * rms_norm(swiglu(rms_norm(h, ff2_pre_g), ff2_w_gate, ff2_w_up, ff2_w_down), ff2_post_g)
    return rms_norm(h, final_g), rows

def setup_inputs(seed: int = 0) -> dict:
    key = jax.random.key(seed)
    ks = iter(jax.random.split(key, 40))
    f32 = jnp.float32

    def nrm(shape, scale=1.0):
        return jax.random.normal(next(ks), shape, f32) * scale

    def gain(shape):
        return 1.0 + 0.05 * nrm(shape)

    L = DEPTH
    sb_c = (L, DEC_BATCH, PAST_LEN, SB_HEADS, SB_HEAD_DIM)
    d_c = (L, DEC_BATCH, PAST_LEN, DIFF_HEADS, 2 * DIFF_HEAD_DIM)
    return {
        'x_prompt': nrm((BATCH, SEQ, D_MODEL)),
        'x_sample': nrm((DEC_BATCH, DEC_SEQ, D_MODEL)),
        'cache_sb_k': nrm(sb_c),
        'cache_sb_v': nrm(sb_c),
        'cache_diff_k': nrm(d_c),
        'cache_diff_v': nrm(d_c),
        'ff1_pre_g': gain((L, D_MODEL)),
        'ff1_w_gate': nrm((L, D_MODEL, D_FF), D_MODEL ** -0.5),
        'ff1_w_up': nrm((L, D_MODEL, D_FF), D_MODEL ** -0.5),
        'ff1_w_down': nrm((L, D_FF, D_MODEL), D_FF ** -0.5),
        'ff1_post_g': gain((L, D_MODEL)),
        'mix_pre_g': gain((L, D_MODEL)),
        'w_in': nrm((L, D_MODEL, IN_WIDTH), D_MODEL ** -0.5),
        'lam_q1': nrm((L, DIFF_HEAD_DIM), LAMBDA_STD),
        'lam_k1': nrm((L, DIFF_HEAD_DIM), LAMBDA_STD),
        'lam_q2': nrm((L, DIFF_HEAD_DIM), LAMBDA_STD),
        'lam_k2': nrm((L, DIFF_HEAD_DIM), LAMBDA_STD),
        'subln_g': gain((L, 2 * DIFF_HEAD_DIM)),
        'w_out': nrm((L, MIX_WIDTH, D_MODEL), MIX_WIDTH ** -0.5),
        'mix_post_g': gain((L, D_MODEL)),
        'ff2_pre_g': gain((L, D_MODEL)),
        'ff2_w_gate': nrm((L, D_MODEL, D_FF), D_MODEL ** -0.5),
        'ff2_w_up': nrm((L, D_MODEL, D_FF), D_MODEL ** -0.5),
        'ff2_w_down': nrm((L, D_FF, D_MODEL), D_FF ** -0.5),
        'ff2_post_g': gain((L, D_MODEL)),
        'final_g': gain((L, D_MODEL)),
    }

def reference(x_prompt, x_sample, cache_sb_k, cache_sb_v, cache_diff_k, cache_diff_v,
              ff1_pre_g, ff1_w_gate, ff1_w_up, ff1_w_down, ff1_post_g,
              mix_pre_g, w_in, lam_q1, lam_k1, lam_q2, lam_k2, subln_g, w_out, mix_post_g,
              ff2_pre_g, ff2_w_gate, ff2_w_up, ff2_w_down, ff2_post_g, final_g):
    yp, ys = x_prompt, x_sample
    rows_p = [[], [], [], []]
    rows_s = [[], [], [], []]
    for l in range(DEPTH):
        lam_init = 0.8 - 0.6 * math.exp(-0.3 * l)
        w = (ff1_pre_g[l], ff1_w_gate[l], ff1_w_up[l], ff1_w_down[l], ff1_post_g[l],
             mix_pre_g[l], w_in[l], lam_q1[l], lam_k1[l], lam_q2[l], lam_k2[l], subln_g[l], w_out[l],
             mix_post_g[l], ff2_pre_g[l], ff2_w_gate[l], ff2_w_up[l], ff2_w_down[l], ff2_post_g[l],
             final_g[l])
        yp, rp = encoder_layer(yp, None, *w, lam_init)
        past = (cache_sb_k[l], cache_sb_v[l], cache_diff_k[l], cache_diff_v[l])
        ys, rs = encoder_layer(ys, past, *w, lam_init)
        for i in range(4):
            rows_p[i].append(rp[i])
            rows_s[i].append(rs[i])
    sb_k_p, sb_v_p, d_k_p, d_v_p = [jnp.stack(r, axis=0) for r in rows_p]
    sb_k_s, sb_v_s, d_k_s, d_v_s = [jnp.stack(r, axis=0) for r in rows_s]
    return (yp, ys, sb_k_p, sb_v_p, d_k_p, d_v_p, sb_k_s, sb_v_s, d_k_s, d_v_s)


_drawn_inputs = setup_inputs


def setup_inputs(seed=0):
    import zlib

    import numpy as np

    out = dict(_drawn_inputs(seed))
    spreads = {}
    factors = {'lam_k1': 2.672, 'ff2_post_g': 3.592}
    for name, (base, spread) in spreads.items():
        noise = np.random.default_rng([zlib.crc32(name.encode()), seed]).standard_normal(out[name].shape)
        drawn = base * np.exp(spread * noise) if base else spread * noise
        out[name] = __import__('jax').numpy.asarray(drawn.astype(out[name].dtype))
    for name, factor in factors.items():
        out[name] = (out[name] * factor).astype(out[name].dtype)
    return out
```

```python
import math
from contextlib import ExitStack

import numpy as np

import concourse.bass as bass
from concourse import mybir

P = 128
D_MODEL, SEQ, DEC_SEQ, PAST = 1024, 1024, 32, 256
D_FF = 2816
HEADS_SB, HEADS_DIFF, HD = 8, 4, 64
EPS = 1e-6
LAM_INIT = 0.8 - 0.6 * math.exp(-0.3 * 0)

T = SEQ + DEC_SEQ
NT, TT = 3, T // 3
KC = D_MODEL // P
FF_ITERS = D_FF // P // 2
FF_PIECES = 6
SB_UNITS = HEADS_SB * HD // P
DIFF_UNITS = HEADS_DIFF
UNITS = SB_UNITS + DIFF_UNITS
RING = 3
TP = SEQ + P
KCOLS = TP + PAST
KBLK = KCOLS // P
VW = 192
U_CLAMP = 30.0

F32, F32R = mybir.dt.float32, mybir.dt.float32r
ALU, ACT = mybir.AluOpType, mybir.ActivationFunctionType

PIECE_FF1 = 0
PIECE_IN = PIECE_FF1 + FF_PIECES * FF_ITERS
PIECE_OUT = PIECE_IN + 3 * UNITS
PIECE_FF2 = PIECE_OUT + KC
PIECES = PIECE_FF2 + FF_PIECES * FF_ITERS

G_FF1_PRE, G_FF1_POST, G_MIX_PRE, G_MIX_POST, G_FF2_PRE, G_FF2_POST, G_FINAL = range(7)
G_SUBLN = 7 * KC


def sb_steps():
    steps = []
    for g in range(SEQ // 512):
        for kb in range(4 * g + 3, -1, -1):
            for h in range(2):
                c0 = max(kb * P, g * 512)
                steps.append(dict(g=g, h=h, kb=kb, c0=c0, w=(g + 1) * 512 - c0, off=c0 - g * 512,
                                  diag=kb >= 4 * g, first=kb == 4 * g + 3, last=kb == 0, bank=h))
    for kb in (8, 10, 9):
        steps.append(dict(g=SEQ // 512, h=None, kb=kb, c0=SEQ, w=2 * DEC_SEQ, off=0, diag=kb == 8,
                          first=kb == 8, last=kb == 9, bank=0))
    return steps


def diff_tiles():
    tiles = [dict(q0=SEQ, nq=DEC_SEQ, k0=SEQ, nk=KCOLS - SEQ, t0=SEQ)]
    for i in range(SEQ // P):
        nk = (i + 1) * P
        tiles.append(dict(q0=i * P, nq=P, k0=0, nk=nk, t0=SEQ - nk))
    for n, t in enumerate(tiles):
        t["i"] = n
        blocks = list(range(t["nk"] // P))
        t["groups"] = [blocks[b:b + 4] for b in range(0, len(blocks), 4)]
    return tiles


STEPS = sb_steps()
NSTEP = len(STEPS)
NMASKED = sum(s["diag"] for s in STEPS)
NCARRY = sum(not s["last"] for s in STEPS)
TILES = diff_tiles()
NTILE = len(TILES)
NGRP = sum(len(t["groups"]) for t in TILES)

T_SPLIT_FF1, T_POST_FF1, T_SPLIT_MIX, T_SUB = 0, KC, 2 * KC, 3 * KC
T_POST_MIX = T_SUB + DIFF_UNITS
T_SPLIT_FF2, T_POST_FF2, T_FINAL = T_POST_MIX + KC, T_POST_MIX + 2 * KC, T_POST_MIX + 3 * KC


def v_pair(t, b, n):
    return t.rearrange("p (b x d) -> p b x d", x=3, d=HD)[:, b:b + n, 0:3:2, :]


def v_one(t, b, n):
    return t[:, b * P:(b + n) * P]


def sample_q(t, h):
    return t[HD * h:HD * h + HD, DEC_SEQ * h:DEC_SEQ * h + DEC_SEQ]


def v_in(layout, src, n):
    return src.rearrange("p (b x d) -> p b x d", x=2, d=HD) if layout is v_pair else src


def build(nc, xT, wg1, wu1, wd1, w_mix, wg2, wu2, wd2, k_cache, v_cache, gains_d, lam_d, consts_d, dist_d,
          yT_out, kv_out):
    ctx = ExitStack()
    with ctx:
        where = [1152]

        def at(name, shape, dt, offset=None):
            size = 4 * int(np.prod(shape[1:]))
            if offset is None:
                offset = where[0]
                where[0] += -(-size // 32) * 32
            return nc.alloc_sbuf_tensor_at(name, shape, dt, offset=offset)

        xh = at("xh", [P, KC, T], F32R)
        xl = at("xl", [P, KC, T], F32R)
        y = at("y", [P, KC, T], F32)
        raw = at("raw", [P, RING, KC, P], F32)
        wh = at("wh", [P, RING, KC, P], F32R)
        wl = at("wl", [P, RING, KC, P], F32R)
        cst = at("cst", [P, 6, P], F32)
        tri = at("tri", [P, 2, P], F32R)
        gains = at("gains", [P, 7 * KC + 1], F32)
        lamv = at("lamv", [HD, 4], F32)
        lamp = at("lamp", [HD, 2], F32)
        lame = at("lame", [P, 2], F32)
        neglam = at("neglam", [P, 1], F32)
        mx = at("mx", [P, 2, 2], F32)
        nm = at("nm", [P, 2, 2], F32)
        ls = at("ls", [P, 2, 2], F32)
        rl = at("rl", [P, 2, 2], F32)
        c2 = at("c2", [P, 2, 1], F32)
        ident, ones, m01, mneg = cst[:, 0, :], cst[:, 1, :], cst[:, 4, :], cst[:, 5, :]
        shared = where[0]

        resid = at("resid", [P, KC, T], F32)
        rstd = at("rstd", [P, T], F32)
        sq = at("sq", [P, 2, T], F32)
        tmp = at("tmp", [P, 2, T], F32)
        hh = at("hh", [P, 2, T], F32R)
        hl = at("hl", [P, 2, T], F32R)

        where[0] = shared
        kh = at("kh", [P, KCOLS], F32R)
        kl = at("kl", [P, KCOLS], F32R)
        qh = at("qh", [P, TP], F32R)
        ql = at("ql", [P, TP], F32R)
        vh = at("vh", [P, KBLK * VW], F32R)
        vl = at("vl", [P, KBLK * VW], F32R)
        qkv = at("qkv", [P, 3, TP], F32)
        kvc = at("kvc", [P, 2, PAST], F32)
        qsh = at("qsh", [P, 2 * DEC_SEQ], F32R)
        qsl = at("qsl", [P, 2 * DEC_SEQ], F32R)
        temps = where[0]
        zs = at("zs", [P, 3, 512], F32)
        u = at("u", [P, 2, 512], F32)
        sph = at("sph", [P, 2, 512], F32R)
        spl = at("spl", [P, 2, 512], F32R)
        wt = at("wt", [P, 2, 512], F32)
        wth = at("wth", [P, 2, 512], F32R)
        wtl = at("wtl", [P, 2, 512], F32R)
        where[0] = temps
        maps = at("maps", [P, 2, 2, SEQ], F32)
        dist = at("dist", [P, SEQ + KCOLS - SEQ], F32)
        dwh = at("dwh", [P, 2, 512], F32R)
        dwl = at("dwl", [P, 2, 512], F32R)

        resid_dram = nc.dram_tensor("resid_scratch", [KC, P, T], F32).ap()

        psA = ctx.enter_context(nc.psum_tensor("psA", [P, 3, 512], F32))
        psB = ctx.enter_context(nc.psum_tensor("psB", [P, 3, 512], F32))
        psC = ctx.enter_context(nc.psum_tensor("psC", [P, 2, 512], F32))
        Z = [psA[:, 2, :], psB[:, 0, :]]
        S = [psB[:, 1, :], psB[:, 2, :]]
        O = psC[:, 0, :]
        DS = [psB[:, 0:2, :], psC[:, 0:2, :]]
        DT, DO = psA[:, 2, :], psB[:, 2, :]

        def sem(name):
            return ctx.enter_context(nc.semaphore(name))

        const_in, x_in, lam_in = sem("const_in"), sem("x_in"), sem("lam_in")
        raw_in = [sem(f"raw_in{s}") for s in range(RING)]
        cache_in, dist_in, resid_in = sem("cache_in"), sem("dist_in"), sem("resid_in")
        spilled, kv_stored, y_stored = sem("spilled"), sem("kv_stored"), sem("y_stored")
        w_hi, w_ready = sem("w_hi"), sem("w_ready")
        setup_v, lam_prod, lam_sum, lam_exp, lam_half = (
            sem("setup_v"), sem("lam_prod"), sem("lam_sum"), sem("lam_exp"), sem("lam_half"))
        zeroed, y_zero = sem("zeroed"), sem("y_zero")
        sq_ready, sums, ln_done, rstd_ready = sem("sq_ready"), sem("sums"), sem("ln_done"), sem("rstd_ready")
        t_ready, xh_ready, x_ready, r_ready = sem("t_ready"), sem("xh_ready"), sem("x_ready"), sem("r_ready")
        fullA, fullB, silu_done, h_done, hh_done, hl_done, y_done = (
            sem("fullA"), sem("fullB"), sem("silu_done"), sem("h_done"), sem("hh_done"), sem("hl_done"), sem("y_done"))
        proj_full, proj_out, vt_full, bound_hi, bound_lo, unit_done = (
            sem("proj_full"), sem("proj_out"), sem("vt_full"), sem("bound_hi"), sem("bound_lo"), sem("unit_done"))
        z_full, zs_ready, u_ready, e_ready, l_ready, diag_v, sp_ready, sph_ready, spl_ready = (
            sem("z_full"), sem("zs_ready"), sem("u_ready"), sem("e_ready"), sem("l_ready"), sem("diag_v"),
            sem("sp_ready"), sem("sph_ready"), sem("spl_ready"))
        s_full, arg_ready, carried, wt_ready, wth_ready, wtl_ready, av_done, o_full, o_done = (
            sem("s_full"), sem("arg_ready"), sem("carried"), sem("wt_ready"), sem("wth_ready"), sem("wtl_ready"),
            sem("av_done"), sem("o_full"), sem("o_done"))
        dist_ready, ds_full, ds_read, nm_ready, de_done, rl_ready, c2_ready, e2_ready, dw_ready = (
            sem("dist_ready"), sem("ds_full"), sem("ds_read"), sem("nm_ready"), sem("de_done"), sem("rl_ready"),
            sem("c2_ready"), sem("e2_ready"), sem("dw_ready"))
        dt_full, dwh_ready, dwl_ready, dav_done, do_done = (
            sem("dt_full"), sem("dwh_ready"), sem("dwl_ready"), sem("dav_done"), sem("do_done"))
        sub_sq, sub_sum, sub_ln, sub_rstd, sub_t = (
            sem("sub_sq"), sem("sub_sum"), sem("sub_ln"), sem("sub_rstd"), sem("sub_t"))
        wo_full, wo_out = sem("wo_full"), sem("wo_out")
        held = sem("held")

        block = ctx.enter_context(nc.Block())

        def bank3(ps):
            return ps[:, :, 0:TT]

        def tiles3(ap):
            return ap.rearrange("p (t c) -> p t c", t=NT)

        class Piece:
            def __init__(self, n, i=0, per=0):
                self.slot = n % RING
                self.landed = 16 * (n // RING + 1) + (16 * (per // RING)) * i
                self.count = n + 1 + per * i

        @block.sync
        def _(sp):
            def load_piece(src, piece, n_static=None):
                if n_static is None or n_static >= RING:
                    sp.wait_ge(w_ready, piece.count - RING)
                sp.dma_start(raw[:, piece.slot, :, :].rearrange("p k c -> p (k c)"), src).then_inc(raw_in[piece.slot], 16)

            def ff_sources(gate, up, down, i):
                for j in range(2):
                    yield gate, 2 * i + j
                    yield up, 2 * i + j
                for j in range(2):
                    yield down, 2 * i + j

            def one(w, n):
                return w[bass.ds(n, 1), :, :].rearrange("o p c -> (o p) c")

            sp.dma_start(cst[:].rearrange("p a b -> p (a b)"), consts_d).then_inc(const_in, 16)
            sp.dma_start(gains[:], gains_d).then_inc(const_in, 16)
            for k in range(KC):
                sp.dma_start(resid[:, k, :], xT[k, :, :]).then_inc(x_in, 16)
            for j, (w, n) in enumerate(ff_sources(wg1, wu1, wd1, 0)):
                load_piece(w[n, :, :], Piece(PIECE_FF1 + j), j)
            sp.dma_start(lamv[:], lam_d).then_inc(lam_in, 16)
            with sp.Fori(1, FF_ITERS) as i:
                for j, (w, n) in enumerate(ff_sources(wg1, wu1, wd1, i)):
                    load_piece(one(w, n), Piece(PIECE_FF1 + j, i, FF_PIECES))
            for j in range(6):
                load_piece(w_mix[j, :, :], Piece(PIECE_IN + j))
            sp.wait_ge(x_ready, 2 * KC)
            for k in range(KC):
                sp.dma_start(resid_dram[k, :, :], resid[:, k, :]).then_inc(spilled, 16)
            sp.wait_ge(spilled, 16 * KC)

            def load_cache(unit):
                sp.dma_start(kvc[:, 0, :], k_cache[bass.ds(unit, 1), :, :].rearrange("o p c -> (o p) c")).then_inc(cache_in, 16)
                sp.dma_start(kvc[:, 1, :], v_cache[bass.ds(unit, 1), :, :].rearrange("o p c -> (o p) c")).then_inc(cache_in, 16)

            def unit_dmas(unit, last=False):
                for j in range(3):
                    load_piece(one(w_mix, 3 * unit + 6 + j), Piece(PIECE_IN + 6 + j, unit, 3))
                sp.wait_ge(proj_out, 9 * unit + 9)
                for j in range(2):
                    sp.dma_start(kv_out[bass.ds(2 * unit + j, 1), :, :].rearrange("o p c -> (o p) c"),
                                 qkv[:, 1 + j, 0:T]).then_inc(kv_stored, 16)
                if not last:
                    sp.wait_ge(bound_lo, 6 * unit + 6)
                    load_cache(unit + 1)

            load_cache(0)
            with sp.Fori(0, SB_UNITS) as i:
                unit_dmas(i)
            sp.wait_ge(unit_done, 1 + SB_UNITS)
            sp.dma_start(dist[:], dist_d).then_inc(dist_in, 16)
            with sp.Fori(SB_UNITS, UNITS - 1) as i:
                unit_dmas(i)
            unit_dmas(UNITS - 1, last=True)
            sp.wait_ge(unit_done, 1 + UNITS)
            for k in range(KC):
                sp.dma_start(resid[:, k, :], resid_dram[k, :, :]).then_inc(resid_in, 16)
            for j in range(6, KC):
                load_piece(w_mix[3 * UNITS + j, :, :], Piece(PIECE_OUT + j))
            with sp.Fori(0, FF_ITERS) as i:
                for j, (w, n) in enumerate(ff_sources(wg2, wu2, wd2, i)):
                    load_piece(one(w, n), Piece(PIECE_FF2 + j, i, FF_PIECES))
            for k in range(KC):
                sp.wait_ge(t_ready, T_FINAL + k + 1)
                sp.dma_start(yT_out[k, :, :], y[:, k, :]).then_inc(y_stored, 16)
            sp.wait_ge(y_stored, 16 * KC)
            sp.wait_ge(kv_stored, 32 * UNITS)

        def split3(pe, out, wa, wb, xa, xb, start, stop, group=True):
            pe.matmul(out, wa, xa, start=start, stop=False, skip_group_check=not group)
            pe.matmul(out, wa, xb, start=False, stop=False, skip_group_check=not group)
            return pe.matmul(out, wb, xa, start=False, stop=stop, skip_group_check=not group)

        @block.tensor
        def _(pe):
            pe.sem_inc(unit_done, 1)

            def dense(ps, piece, rh, rl_, x_base=None):
                pe.wait_ge(w_ready, piece.count)
                for k in range(KC):
                    if x_base is not None:
                        pe.wait_ge(x_ready, x_base + k + 1)
                    for wa, ra in ((wh, rh), (wh, rl_), (wl, rh)):
                        for t in range(NT):
                            last = pe.matmul(ps[:, t, 0:TT], wa[:, piece.slot, k, :], ra[:, k, t * TT:(t + 1) * TT],
                                             start=(k == 0 and wa is wh and ra is rh),
                                             stop=(k == KC - 1 and wa is wl))
                return last

            def stats(norm):
                for k in range(KC):
                    pe.wait_ge(sq_ready, KC * norm + k + 1)
                    for t in range(NT):
                        last = pe.matmul(psA[:, t, 0:TT], ones, sq[:, k % 2, t * TT:(t + 1) * TT],
                                         start=k == 0, stop=k == KC - 1)
                    last.then_inc(sums, 1)

            def ffn(base, i, n_it, x_base):
                ii = i + n_it
                piece = [Piece(base + j, i, FF_PIECES) for j in range(FF_PIECES)]
                for j in range(2):
                    if j == 0:
                        pe.wait_ge(y_done, 8 * ii + 7)
                    else:
                        pe.wait_ge(silu_done, 6 * ii + 3)
                    dense(psA, piece[2 * j], xh, xl, x_base if j == 0 else None).then_inc(fullA, 1)
                    if j == 0:
                        pe.wait_ge(y_done, 8 * ii + 8)
                    else:
                        pe.wait_ge(h_done, 6 * ii + 3)
                    dense(psB, piece[2 * j + 1], xh, xl).then_inc(fullB, 1)
                for d in range(KC):
                    ps, full = ((psA, fullA), (psB, fullB))[d % 2]
                    if d == 0:
                        pe.wait_ge(silu_done, 6 * ii + 6)
                        pe.wait_ge(hl_done, 6 * ii + 3)
                        pe.wait_ge(w_ready, piece[5].count)
                    elif d == 1:
                        pe.wait_ge(h_done, 6 * ii + 6)
                    else:
                        pe.wait_ge(y_done, 8 * ii + 8 + d - 1)
                    for j in range(2):
                        for t in range(NT):
                            if d == 0 and j == 1:
                                pe.wait_ge(hl_done, 6 * ii + 3 + t + 1)
                            s = piece[4 + j].slot
                            c = slice(t * TT, (t + 1) * TT)
                            last = split3(pe, ps[:, t, 0:TT], wh[:, s, d, :], wl[:, s, d, :], hh[:, j, c], hl[:, j, c],
                                          start=j == 0, stop=j == 1)
                    last.then_inc(full, 1)

            def proj_part(unit, f, part, parts, x_base=None):
                piece = Piece(PIECE_IN + f // 3, unit, 3)
                bank = psA[:, f % 2, 0:TT]
                if part == 0:
                    if f % 3 == 0:
                        pe.wait_ge(w_ready, piece.count)
                    if not (isinstance(unit, int) and unit == 0 and f < 2):
                        pe.wait_ge(proj_out, 9 * unit + f - 1)
                todo = [(k, n) for k in range(KC) for n in range(3)]
                for k, n in todo[part * len(todo) // parts:(part + 1) * len(todo) // parts]:
                    if x_base is not None and f == 0 and n == 0:
                        pe.wait_ge(x_ready, x_base + k + 1)
                    wa, xa = ((wh, xh), (wh, xl), (wl, xh))[n]
                    last = pe.matmul(bank, wa[:, piece.slot, k, :], xa[:, k, (f % 3) * TT:(f % 3 + 1) * TT],
                                     start=(k, n) == todo[0], stop=(k, n) == todo[-1])
                if part == parts - 1:
                    last.then_inc(proj_full, 1)

            def boundary(unit):
                pe.wait_ge(proj_out, 9 * unit + 9)
                pe.wait_ge(bound_lo, 6 * unit + 1)
                for b in range(SEQ // P):
                    last = pe.transpose(psC[:, b // 4, (b % 4) * P:(b % 4 + 1) * P], qkv[:, 2, b * P:(b + 1) * P], ident)
                last.then_inc(vt_full, 1)
                pe.transpose(psB[:, 0, 0:P], qkv[:, 2, SEQ:TP], ident).then_inc(vt_full, 1)
                pe.wait_ge(bound_lo, 6 * unit + 6)

            def sb_unit(unit):
                boundary(unit)
                carry = [0]

                def scores(n):
                    s = STEPS[n]
                    if n >= 2:
                        pe.wait_ge(zs_ready, NSTEP * unit + n - 1)
                    kc = slice(s["kb"] * P, (s["kb"] + 1) * P)
                    out = Z[n % 2][:, 0:s["w"]]
                    if s["h"] is None:
                        last = split3(pe, out, kh[:, kc], kl[:, kc], qsh[:], qsl[:], start=True, stop=True)
                    else:
                        r = slice(HD * s["h"], HD * s["h"] + HD)
                        qc = slice(s["c0"], s["c0"] + s["w"])
                        last = split3(pe, out, kh[r, kc], kl[r, kc], qh[r, qc], ql[r, qc], start=True, stop=True)
                    last.then_inc(z_full, 1)

                def add_tri(n, which, start):
                    s = STEPS[n]
                    out = S[s["bank"]][:, s["off"]:s["off"] + s["w"]]
                    pe.matmul(out, tri[:, which, :], sph[:, n % 2, 0:s["w"]], start=start, stop=False,
                              skip_group_check=True)
                    return pe.matmul(out, tri[:, which, :], spl[:, n % 2, 0:s["w"]], start=False, stop=False,
                                     skip_group_check=True)

                def suffix(n):
                    pe.wait_ge(spl_ready, NSTEP * unit + n + 1)
                    add_tri(n, 0, STEPS[n]["first"]).then_inc(s_full, 1)

                def carry_on(n):
                    pe.wait_ge(arg_ready, NSTEP * unit + n + 1)
                    if not STEPS[n]["last"]:
                        add_tri(n, 1, False).then_inc(carried, 1)

                def values(n):
                    s = STEPS[n]
                    pe.wait_ge(wtl_ready, NSTEP * unit + n + 1)
                    if s["first"] and s["h"] != 1 and s["g"] > 0:
                        pe.wait_ge(o_done, 3 * unit + s["g"])
                    heads = (s["h"],) if s["h"] is not None else (0, 1)
                    for x, h in enumerate(heads):
                        w = s["w"] // len(heads)
                        vc = slice(s["kb"] * VW + HD * h, s["kb"] * VW + HD * h + P)
                        wc = slice(x * w, (x + 1) * w)
                        last = split3(pe, O[:, s["off"]:s["off"] + w], vh[:, vc], vl[:, vc],
                                      wth[:, n % 2, wc], wtl[:, n % 2, wc],
                                      start=s["first"] and h == 0, stop=False, group=False)
                    last.then_inc(av_done, 1)

                for tick in range(NSTEP + 3):
                    if tick < NSTEP:
                        scores(tick)
                    if 2 <= tick < NSTEP + 2:
                        suffix(tick - 2)
                    if tick < NSTEP:
                        proj_part(unit + 1, tick // 3, tick % 3, 3)
                    if 2 <= tick < NSTEP + 2:
                        carry_on(tick - 2)
                    if tick >= 3:
                        values(tick - 3)
                pe.drain().then_inc(unit_done, 1)

            def diff_unit(unit, head, filler):
                boundary(unit)
                group = [0]

                def scores(t):
                    for m in range(2):
                        if t["i"] >= 1:
                            pe.wait_ge(ds_read, 2 * NTILE * head + 2 * (t["i"] - 1) + m + 1)
                        r = slice(HD * m, HD * m + HD)
                        for c in range(0, t["nk"], 512):
                            w = min(512, t["nk"] - c)
                            qc, kc = slice(t["q0"], t["q0"] + P), slice(t["k0"] + c, t["k0"] + c + w)
                            last = split3(pe, DS[m][:, c // 512, 0:w], qh[r, qc], ql[r, qc], kh[r, kc], kl[r, kc],
                                          start=True, stop=True)
                        last.then_inc(ds_full, 1)

                def turn(t, g, gn):
                    if g == 0:
                        pe.wait_ge(dw_ready, NTILE * head + t["i"] + 1)
                    if gn >= 1:
                        pe.wait_ge(dwl_ready, NGRP * head + gn)
                    for x, b in enumerate(t["groups"][g]):
                        last = pe.transpose(DT[:, x * P:(x + 1) * P], maps[:, t["i"] % 2, 0, b * P:(b + 1) * P], ident)
                    last.then_inc(dt_full, 1)

                def values(t, g, gn):
                    pe.wait_ge(dwl_ready, NGRP * head + gn + 1)
                    if g == 0 and t["i"] >= 2:
                        pe.wait_ge(do_done, NTILE * head + t["i"] - 1)
                    out = DO[:, (t["i"] % 2) * P:(t["i"] % 2) * P + t["nq"]]
                    for x, b in enumerate(t["groups"][g]):
                        kb = t["k0"] // P + b
                        vc, wc = slice(kb * P, (kb + 1) * P), slice(x * P, x * P + t["nq"])
                        last = split3(pe, out, vh[:, vc], vl[:, vc], dwh[:, gn % 2, wc], dwl[:, gn % 2, wc],
                                      start=g == 0 and x == 0, stop=b == t["groups"][-1][-1])
                    last.then_inc(dav_done, 1)

                gn = 0
                for tick in range(NTILE + 1):
                    if tick < NTILE:
                        scores(TILES[tick])
                    t = TILES[tick - 1] if tick else None
                    if t:
                        turn(t, 0, gn)
                    if filler and tick < NTILE:
                        proj_part(unit + 1, tick, 0, 2)
                    if t:
                        values(t, 0, gn)
                        gn += 1
                        if len(t["groups"]) > 1:
                            turn(t, 1, gn)
                    if filler and tick < NTILE:
                        proj_part(unit + 1, tick, 1, 2)
                    if t and len(t["groups"]) > 1:
                        values(t, 1, gn)
                        gn += 1
                pe.drain().then_inc(unit_done, 1)

            pe.wait_ge(const_in, 32)
            stats(0)
            with pe.Fori(0, FF_ITERS) as i:
                ffn(PIECE_FF1, i, 0, 0)
            pe.wait_ge(y_done, 8 * FF_ITERS + 7)
            stats(1)
            pe.wait_ge(lam_prod, 1)
            pe.matmul(psC[:, 0, 0:2], ones[0:HD, :], lamp[:], start=True, stop=True).then_inc(lam_sum, 1)
            stats(2)
            for f in range(9):
                proj_part(0, f, 0, 1, KC)
            with pe.Fori(0, SB_UNITS) as i:
                sb_unit(i)
            with pe.Fori(0, DIFF_UNITS - 1) as i:
                diff_unit(i + SB_UNITS, i, True)
            diff_unit(UNITS - 1, DIFF_UNITS - 1, False)
            for d in range(DIFF_UNITS):
                pe.wait_ge(sub_sq, d + 1)
                if d >= 2:
                    pe.wait_ge(sub_ln, d - 1)
                ps = (psA, psB)[d % 2]
                for t in range(NT):
                    last = pe.matmul(ps[:, t, 0:TT], ones, sq[:, d % 2, t * TT:(t + 1) * TT], start=True, stop=True)
                last.then_inc(sub_sum, 1)
            pe.wait_ge(x_ready, 3 * KC)
            for d in range(KC):
                if d >= 2:
                    pe.wait_ge(wo_out, d - 1)
                dense((psA, psB)[d % 2], Piece(PIECE_OUT + d), xh, xl).then_inc(wo_full, 1)
            pe.wait_ge(wo_out, KC)
            stats(3)
            stats(4)
            with pe.Fori(0, FF_ITERS) as i:
                ffn(PIECE_FF2, i, FF_ITERS, 3 * KC)
            pe.wait_ge(y_done, 8 * 2 * FF_ITERS + 7)
            stats(5)
            stats(6)

        @block.scalar
        def _(act):
            def split_hi(piece):
                act.wait_ge(raw_in[piece.slot], piece.landed)
                act.activation(wh[:, piece.slot, :, :], raw[:, piece.slot, :, :], ACT.Copy).then_inc(w_hi, 1)

            def stats(norm, src, ready, base):
                for k in range(KC):
                    act.wait_ge(ready, base + k + 1 if ready is not x_in else 16 * KC)
                    if norm > 0 or k >= 2:
                        act.wait_ge(sums, KC * norm + k - 1)
                    act.activation(sq[:, k % 2, :], src[:, k, :], ACT.Square).then_inc(sq_ready, 1)
                act.preload_act_table_set("natural_log_exp_and_others")
                act.wait_ge(sums, KC * (norm + 1))
                act.activation(tiles3(rstd[:]), bank3(psA), ACT.Ln, scale=1.0 / D_MODEL, bias=EPS).then_inc(ln_done, 1)
                act.wait_ge(ln_done, norm + 1)
                act.activation(rstd[:], rstd[:], ACT.Exp, scale=-0.5).then_inc(rstd_ready, 1)

            def x_hi(t_base):
                for k in range(KC):
                    act.wait_ge(t_ready, t_base + k + 1)
                    act.activation(xh[:, k, :], tmp[:, k % 2, :], ACT.Copy).then_inc(xh_ready, 1)

            def ffn(base, i, n_it, last=False):
                ii = i + n_it
                piece = [Piece(base + j, i, FF_PIECES) for j in range(2 * FF_PIECES)]

                def silu(j):
                    act.wait_ge(fullA, 6 * ii + j + 1)
                    for t in range(NT):
                        c = slice(t * TT, (t + 1) * TT)
                        act.activation(tmp[:, j, c], psA[:, t, 0:TT], ACT.Silu).then_inc(silu_done, 1)

                def hidden_hi(j):
                    for t in range(NT):
                        c = slice(t * TT, (t + 1) * TT)
                        act.wait_ge(h_done, 6 * ii + 3 * j + t + 1)
                        act.activation(hh[:, j, c], tmp[:, j, c], ACT.Copy).then_inc(hh_done, 1)

                silu(0)
                split_hi(piece[3])
                hidden_hi(0)
                split_hi(piece[4])
                silu(1)
                split_hi(piece[5])
                hidden_hi(1)
                if not last:
                    split_hi(piece[6])
                    act.wait_ge(fullB, 6 * ii + 6)
                    split_hi(piece[7])
                    split_hi(piece[8])

            stats(0, resid, x_in, 0)
            for n in range(RING):
                split_hi(Piece(n))
            x_hi(T_SPLIT_FF1)
            act.preload_act_table_set("silu_and_others")
            with act.Fori(0, FF_ITERS) as i:
                ffn(PIECE_FF1, i, 0)
            stats(1, y, y_done, 8 * FF_ITERS)
            stats(2, resid, r_ready, 0)
            act.wait_ge(lam_sum, 1)
            act.activation(lame[:], psC[:, 0, 0:2], ACT.Exp).then_inc(lam_exp, 1)
            x_hi(T_SPLIT_MIX)

            def proj_evac(unit, f):
                act.wait_ge(proj_full, 9 * unit + f + 1)
                act.activation(qkv[:, f // 3, (f % 3) * TT:(f % 3 + 1) * TT], psA[:, f % 2, 0:TT], ACT.Copy,
                               scale=HD ** -0.5 if f < 3 else 1.0).then_inc(proj_out, 1)

            def boundary(unit, v_out):
                act.wait_ge(proj_out, 9 * unit + 9)
                act.wait_ge(unit_done, unit + 1)
                if v_out is v_pair:
                    for h in range(2):
                        act.activation(sample_q(qsh, h), qkv[HD * h:HD * h + HD, 0, SEQ:T], ACT.Copy)
                act.activation(qh[:], qkv[:, 0, :], ACT.Copy).then_inc(bound_hi, 1)
                act.activation(kh[:, 0:TP], qkv[:, 1, :], ACT.Copy).then_inc(bound_hi, 1)
                act.wait_ge(cache_in, 32 * unit + 32)
                act.activation(kh[:, TP:KCOLS], kvc[:, 0, :], ACT.Copy).then_inc(bound_hi, 1)
                o, i = v_out(vh, SEQ // P + 1, 2), v_in(v_out, kvc[:, 1, :], 2)
                act.activation(o, i, ACT.Copy).then_inc(bound_hi, 1)
                act.wait_ge(vt_full, 2 * unit + 1)
                for c in range(2):
                    last = act.activation(v_out(vh, 4 * c, 4), v_in(v_out, psC[:, c, :], 4), ACT.Copy)
                last.then_inc(bound_hi, 1)
                act.wait_ge(vt_full, 2 * unit + 2)
                act.activation(v_out(vh, SEQ // P, 1), v_in(v_out, psB[:, 0, 0:P], 1), ACT.Copy).then_inc(bound_hi, 1)

            def staging_free(unit):
                act.wait_ge(kv_stored, 32 * unit + 32)
                act.wait_ge(bound_lo, 6 * unit + 6)

            def sb_unit(unit):
                boundary(unit, v_pair)
                base = NSTEP * unit
                carries = [sum(not s["last"] for s in STEPS[:n]) for n in range(NSTEP)]

                def sp_hi(n):
                    w = STEPS[n]["w"]
                    act.wait_ge(sp_ready, base + n + 1)
                    if n >= 2:
                        if STEPS[n - 2]["last"]:
                            act.wait_ge(s_full, base + n - 1)
                        else:
                            act.wait_ge(carried, NCARRY * unit + carries[n - 2] + 1)
                    act.activation(sph[:, n % 2, 0:w], u[:, n % 2, 0:w], ACT.Copy).then_inc(sph_ready, 1)

                def weight_exp(n):
                    w = STEPS[n]["w"]
                    act.wait_ge(arg_ready, base + n + 1)
                    act.activation(wt[:, n % 2, 0:w], wt[:, n % 2, 0:w], ACT.Exp).then_inc(wt_ready, 1)

                def soft_exp(n):
                    w = STEPS[n]["w"]
                    act.wait_ge(u_ready, base + n + 1)
                    act.activation(u[:, n % 2, 0:w], u[:, n % 2, 0:w], ACT.Exp).then_inc(e_ready, 1)

                def weight_hi(n):
                    w = STEPS[n]["w"]
                    act.wait_ge(wt_ready, base + n + 1)
                    if n >= 2:
                        act.wait_ge(av_done, base + n - 1)
                    act.activation(wth[:, n % 2, 0:w], wt[:, n % 2, 0:w], ACT.Copy).then_inc(wth_ready, 1)

                def soft_ln(n):
                    w = STEPS[n]["w"]
                    act.wait_ge(e_ready, base + n + 1)
                    act.activation(u[:, n % 2, 0:w], u[:, n % 2, 0:w], ACT.Ln, bias=1.0).then_inc(l_ready, 1)

                for tick in range(NSTEP + 2):
                    if 1 <= tick <= NSTEP:
                        sp_hi(tick - 1)
                    if tick >= 2:
                        weight_exp(tick - 2)
                    if tick < NSTEP:
                        soft_exp(tick)
                    if tick >= 2:
                        weight_hi(tick - 2)
                    if tick < NSTEP:
                        soft_ln(tick)
                    if tick == 3:
                        staging_free(unit)
                    if tick % 3 == 0 and 0 < tick <= NSTEP:
                        proj_evac(unit + 1, tick // 3 - 1)
                    if tick % 9 == 0 and 0 < tick <= NSTEP:
                        split_hi(Piece(PIECE_IN + 3 + tick // 9 - 1, unit + 1, 3))

            def diff_unit(unit, head, filler):
                boundary(unit, v_one)

                def exps(t):
                    s = t["i"] % 2
                    act.wait_ge(nm_ready, NTILE * head + t["i"] + 1)
                    for m in range(2):
                        act.activation(maps[:, s, m, 0:t["nk"]], maps[:, s, m, 0:t["nk"]], ACT.Exp, bias=nm[:, s, m:m + 1],
                                       accum_out=ls[:, s, m:m + 1]).then_inc(de_done, 1)

                def turned_hi(t, g, gn):
                    w = P * len(t["groups"][g])
                    act.wait_ge(dt_full, NGRP * head + gn + 1)
                    if gn >= 2:
                        act.wait_ge(dav_done, NGRP * head + gn - 1)
                    act.activation(dwh[:, gn % 2, 0:w], DT[:, 0:w], ACT.Copy).then_inc(dwh_ready, 1)

                gn = 0
                for tick in range(NTILE + 1):
                    t = TILES[tick - 1] if tick else None
                    if t:
                        turned_hi(t, 0, gn)
                        gn += 1
                    if tick < NTILE:
                        exps(TILES[tick])
                    if t and len(t["groups"]) > 1:
                        turned_hi(t, 1, gn)
                        gn += 1
                    if filler and tick == 1:
                        staging_free(unit)
                    if filler and tick:
                        proj_evac(unit + 1, tick - 1)
                        if tick % 3 == 0:
                            split_hi(Piece(PIECE_IN + 3 + tick // 3 - 1, unit + 1, 3))

            for f in range(9):
                proj_evac(0, f)
                if f % 3 == 2:
                    split_hi(Piece(PIECE_IN + 3 + f // 3))
            act.wait_ge(spilled, 16 * KC)
            act.wait_ge(zeroed, 5)
            with act.Fori(0, SB_UNITS) as i:
                sb_unit(i)
            with act.Fori(0, DIFF_UNITS - 1) as i:
                diff_unit(i + SB_UNITS, i, True)
            diff_unit(UNITS - 1, DIFF_UNITS - 1, False)
            act.wait_ge(do_done, NTILE * DIFF_UNITS)
            act.wait_ge(kv_stored, 32 * UNITS)

            def sub_square(e):
                act.activation(sq[:, e % 2, :], y[:, SB_UNITS + e, :], ACT.Square).then_inc(sub_sq, 1)

            sub_square(0)
            sub_square(1)
            for d in range(SB_UNITS):
                act.activation(xh[:, d, :], y[:, d, :], ACT.Copy).then_inc(xh_ready, 1)
            for e in range(DIFF_UNITS):
                act.wait_ge(sub_sum, e + 1)
                if e >= 1:
                    act.wait_ge(t_ready, T_SUB + e)
                act.activation(tiles3(rstd[:]), bank3((psA, psB)[e % 2]), ACT.Ln, scale=1.0 / P, bias=EPS).then_inc(sub_ln, 1)
                if e + 2 < DIFF_UNITS:
                    sub_square(e + 2)
                act.wait_ge(sub_ln, e + 1)
                act.activation(rstd[:], rstd[:], ACT.Exp, scale=-0.5).then_inc(sub_rstd, 1)
                act.wait_ge(t_ready, T_SUB + e + 1)
                act.activation(xh[:, SB_UNITS + e, :], tmp[:, e % 2, :], ACT.Copy).then_inc(xh_ready, 1)
            for d in range(KC):
                act.wait_ge(wo_full, d + 1)
                split_hi(Piece(PIECE_OUT + 3 + d))
            stats(3, y, wo_out, 0)
            stats(4, resid, r_ready, KC)
            x_hi(T_SPLIT_FF2)
            act.preload_act_table_set("silu_and_others")
            with act.Fori(0, FF_ITERS - 1) as i:
                ffn(PIECE_FF2, i, FF_ITERS)
            ffn(PIECE_FF2, FF_ITERS - 1, FF_ITERS, last=True)
            stats(5, y, y_done, 8 * 2 * FF_ITERS)
            stats(6, resid, r_ready, 2 * KC)

        @block.vector
        def _(dve):
            dve.sem_inc(y_done, 8)

            def split_lo(piece):
                dve.wait_ge(w_hi, piece.count)
                dve.tensor_tensor(wl[:, piece.slot, :, :], raw[:, piece.slot, :, :], wh[:, piece.slot, :, :].bitcast(F32),
                                  ALU.subtract).then_inc(w_ready, 1)

            def x_split(norm, g, x_base):
                dve.wait_ge(rstd_ready, norm + 1)

                def scaled(k):
                    if k >= 2:
                        dve.wait_ge(x_ready, x_base + k - 1)
                    dve.scalar_tensor_tensor(tmp[:, k % 2, :], resid[:, k, :], gains[:, KC * g + k:KC * g + k + 1],
                                             rstd[:], ALU.mult, ALU.mult).then_inc(t_ready, 1)

                def low(k):
                    dve.wait_ge(xh_ready, x_base + k + 1)
                    dve.tensor_tensor(xl[:, k, :], tmp[:, k % 2, :], xh[:, k, :].bitcast(F32), ALU.subtract).then_inc(x_ready, 1)

                for k in range(KC):
                    scaled(k)
                    if k >= 1:
                        low(k - 1)
                low(KC - 1)

            def post(norm, g, t_base, r_base):
                dve.wait_ge(rstd_ready, norm + 1)

                def add(k):
                    dve.wait_ge(t_ready, t_base + k + 1)
                    dve.scalar_tensor_tensor(resid[:, k, :], tmp[:, k % 2, :], gains[:, KC * g + k:KC * g + k + 1],
                                             resid[:, k, :], ALU.mult, ALU.add).then_inc(r_ready, 1)

                for k in range(KC):
                    if k >= 2:
                        dve.wait_ge(r_ready, r_base + k - 1)
                    dve.tensor_tensor(tmp[:, k % 2, :], y[:, k, :], rstd[:], ALU.mult).then_inc(t_ready, 1)
                    if k >= 1:
                        add(k - 1)
                add(KC - 1)

            def ffn(base, i, n_it, last=False):
                ii = i + n_it
                piece = [Piece(base + j, i, FF_PIECES) for j in range(2 * FF_PIECES)]

                def hidden(j):
                    dve.wait_ge(fullB, 6 * ii + j + 1)
                    for t in range(NT):
                        c = slice(t * TT, (t + 1) * TT)
                        dve.wait_ge(silu_done, 6 * ii + 3 * j + t + 1)
                        dve.tensor_tensor(tmp[:, j, c], psB[:, t, 0:TT], tmp[:, j, c], ALU.mult).then_inc(h_done, 1)
                    for t in range(NT):
                        c = slice(t * TT, (t + 1) * TT)
                        dve.wait_ge(hh_done, 6 * ii + 3 * j + t + 1)
                        dve.tensor_tensor(hl[:, j, c], tmp[:, j, c], hh[:, j, c].bitcast(F32), ALU.subtract).then_inc(hl_done, 1)

                split_lo(piece[3])
                hidden(0)
                split_lo(piece[4])
                split_lo(piece[5])
                hidden(1)
                if not last:
                    split_lo(piece[6])
                for d in range(KC):
                    ps, full = ((psA, fullA), (psB, fullB))[d % 2]
                    dve.wait_ge(full, 6 * ii + 2 + d // 2 + 1)
                    dve.wait_ge(y_done, 8 * ii + d + 1)
                    if d == 0:
                        dve.wait_ge(y_zero, 1 if n_it == 0 else 2)
                    dve.tensor_tensor(tiles3(y[:, d, :]), bank3(ps), tiles3(y[:, d, :]), ALU.add).then_inc(y_done, 1)
                if not last:
                    split_lo(piece[7])
                    split_lo(piece[8])

            dve.wait_ge(const_in, 32)
            dve.tensor_copy(tri[:], cst[:, 2:4, :]).then_inc(setup_v, 1)
            for g in (G_FF1_POST, G_FF2_POST):
                dve.tensor_scalar(gains[:, KC * g:KC * g + KC], gains[:, KC * g:KC * g + KC], 0.5, None, ALU.mult).then_inc(setup_v, 1)
            dve.tensor_scalar(gains[:, G_SUBLN:G_SUBLN + 1], gains[:, G_SUBLN:G_SUBLN + 1], 1.0 - LAM_INIT, None,
                              ALU.mult).then_inc(setup_v, 1)
            dve.wait_ge(setup_v, 4)
            for n in range(RING):
                split_lo(Piece(n))
            dve.wait_ge(lam_in, 16)
            dve.tensor_tensor(lamp[:], lamv[:, 0:2], lamv[:, 2:4], ALU.mult).then_inc(lam_prod, 1)
            x_split(0, G_FF1_PRE, 0)
            with dve.Fori(0, FF_ITERS) as i:
                ffn(PIECE_FF1, i, 0)
            post(1, G_FF1_POST, T_POST_FF1, 0)
            x_split(2, G_MIX_PRE, KC)
            dve.wait_ge(lam_exp, 1)
            dve.scalar_tensor_tensor(neglam[:], lame[:, 1:2], LAM_INIT, lame[:, 0:1], ALU.subtract, ALU.subtract).then_inc(lam_half, 1)

            def boundary(unit, v_out):
                def low(n, o, raw_in_, hi):
                    dve.wait_ge(bound_hi, 6 * unit + n + 1)
                    return dve.tensor_tensor(o, raw_in_, hi.bitcast(F32), ALU.subtract)

                if v_out is v_pair:
                    for h in range(2):
                        low(0, sample_q(qsl, h), qkv[HD * h:HD * h + HD, 0, SEQ:T], sample_q(qsh, h))
                low(0, ql[:], qkv[:, 0, :], qh[:]).then_inc(bound_lo, 1)
                low(1, kl[:, 0:TP], qkv[:, 1, :], kh[:, 0:TP]).then_inc(bound_lo, 1)
                low(2, kl[:, TP:KCOLS], kvc[:, 0, :], kh[:, TP:KCOLS]).then_inc(bound_lo, 1)
                low(3, v_out(vl, SEQ // P + 1, 2), v_in(v_out, kvc[:, 1, :], 2), v_out(vh, SEQ // P + 1, 2)).then_inc(bound_lo, 1)
                for c in range(2):
                    last = low(4, v_out(vl, 4 * c, 4), v_in(v_out, psC[:, c, :], 4), v_out(vh, 4 * c, 4))
                last.then_inc(bound_lo, 1)
                low(5, v_out(vl, SEQ // P, 1), v_in(v_out, psB[:, 0, 0:P], 1), v_out(vh, SEQ // P, 1)).then_inc(bound_lo, 1)

            def sb_unit(unit):
                boundary(unit, v_pair)
                base = NSTEP * unit
                diag = [0]

                def masked(s, first, out, table, op, sem_last):
                    if not s["diag"]:
                        first.then_inc(sem_last, 1)
                        return
                    first.then_inc(diag_v, 1)
                    diag[0] += 1
                    dve.wait_ge(diag_v, 2 * NMASKED * unit + diag[0])
                    heads = 1 if s["h"] is not None else 2
                    w = P if heads == 1 else DEC_SEQ
                    for x in range(heads):
                        last = dve.tensor_tensor(out[:, x * w:(x + 1) * w], out[:, x * w:(x + 1) * w], table[:, 0:w], op)
                    last.then_inc(sem_last, 1)

                def scores_out(n):
                    w = STEPS[n]["w"]
                    dve.wait_ge(z_full, base + n + 1)
                    if n >= 3:
                        dve.wait_ge(arg_ready, base + n - 2)
                    dve.tensor_copy(zs[:, n % 3, 0:w], Z[n % 2][:, 0:w]).then_inc(zs_ready, 1)

                def softplus(n):
                    s = STEPS[n]
                    o = u[:, n % 2, 0:s["w"]]
                    dve.wait_ge(l_ready, base + n + 1)
                    masked(s, dve.tensor_tensor(o, zs[:, n % 3, 0:s["w"]], o, ALU.max), o, m01, ALU.mult, sp_ready)

                def argument(n):
                    s = STEPS[n]
                    o = wt[:, n % 2, 0:s["w"]]
                    if n >= 2:
                        dve.wait_ge(wtl_ready, base + n - 1)
                    dve.wait_ge(s_full, base + n + 1)
                    masked(s, dve.tensor_tensor(o, zs[:, n % 3, 0:s["w"]], S[s["bank"]][:, s["off"]:s["off"] + s["w"]],
                                                ALU.subtract), o, mneg, ALU.min, arg_ready)

                def sp_lo(n):
                    w = STEPS[n]["w"]
                    dve.wait_ge(sph_ready, base + n + 1)
                    dve.tensor_tensor(spl[:, n % 2, 0:w], u[:, n % 2, 0:w], sph[:, n % 2, 0:w].bitcast(F32),
                                      ALU.subtract).then_inc(spl_ready, 1)

                def weight_lo(n):
                    s = STEPS[n]
                    w = s["w"]
                    dve.wait_ge(wth_ready, base + n + 1)
                    dve.tensor_tensor(wtl[:, n % 2, 0:w], wt[:, n % 2, 0:w], wth[:, n % 2, 0:w].bitcast(F32),
                                      ALU.subtract).then_inc(wtl_ready, 1)

                def output(n):
                    s = STEPS[n]
                    if s["last"] and s["h"] != 0:
                        dve.wait_ge(av_done, base + n + 1)
                        w = 512 if s["h"] is not None else DEC_SEQ
                        dve.tensor_copy(y[:, bass.ds(unit, 1), s["g"] * 512:s["g"] * 512 + w],
                                        O[:, 0:w].rearrange("p (o c) -> p o c", o=1)).then_inc(o_done, 1)

                for tick in range(NSTEP + 4):
                    if 3 <= tick < NSTEP + 3:
                        weight_lo(tick - 3)
                    if 1 <= tick <= NSTEP:
                        softplus(tick - 1)
                    if tick < NSTEP:
                        scores_out(tick)
                    if 2 <= tick < NSTEP + 2:
                        argument(tick - 2)
                    if 1 <= tick <= NSTEP:
                        sp_lo(tick - 1)
                    if tick % 9 == 0 and 0 < tick <= NSTEP:
                        split_lo(Piece(PIECE_IN + 3 + tick // 9 - 1, unit + 1, 3))
                    if tick >= 4:
                        output(tick - 4)

            def diff_unit(unit, head, filler):
                boundary(unit, v_one)
                dve.wait_ge(dist_in, 16)
                dve.wait_ge(bound_lo, 6 * unit + 6)
                dve.tensor_scalar(dist[:], dist[:], 0.25, None, ALU.mult).then_inc(dist_ready, 1)
                dve.wait_ge(dist_ready, head + 1)

                def biased(t):
                    s = t["i"] % 2
                    if t["i"] >= 2:
                        dve.wait_ge(dw_ready, NTILE * head + t["i"] - 1)
                    for m in range(2):
                        dve.wait_ge(ds_full, 2 * NTILE * head + 2 * t["i"] + m + 1)
                        dve.sem_inc(held, 1)
                        dve.tensor_tensor_reduce(maps[:, s, m, 0:t["nk"]],
                                                 DS[m].rearrange("p a b -> p (a b)")[:, 0:t["nk"]],
                                                 dist[:, t["t0"]:t["t0"] + t["nk"]], 1.0, -3.0e38, ALU.add, ALU.max,
                                                 mx[:, s, m:m + 1]).then_inc(ds_read, 1)
                    dve.wait_ge(ds_read, 2 * NTILE * head + 2 * t["i"] + 2)
                    dve.tensor_scalar(nm[:, s, :], mx[:, s, :], -1.0, None, ALU.mult).then_inc(nm_ready, 1)

                def turned_lo(t, g, gn):
                    w = P * len(t["groups"][g])
                    dve.wait_ge(dwh_ready, NGRP * head + gn + 1)
                    dve.tensor_tensor(dwl[:, gn % 2, 0:w], DT[:, 0:w], dwh[:, gn % 2, 0:w].bitcast(F32),
                                      ALU.subtract).then_inc(dwl_ready, 1)

                def weights(t):
                    s, i = t["i"] % 2, t["i"]
                    dve.wait_ge(de_done, 2 * NTILE * head + 2 * i + 2)
                    dve.reciprocal(rl[:, s, :], ls[:, s, :]).then_inc(rl_ready, 1)
                    dve.wait_ge(rl_ready, NTILE * head + i + 1)
                    dve.tensor_tensor(c2[:, s, :], rl[:, s, 1:2], neglam[:], ALU.mult).then_inc(c2_ready, 1)
                    dve.wait_ge(c2_ready, NTILE * head + i + 1)
                    dve.tensor_scalar(maps[:, s, 1, 0:t["nk"]], maps[:, s, 1, 0:t["nk"]], c2[:, s, :], None,
                                      ALU.mult).then_inc(e2_ready, 1)
                    dve.wait_ge(e2_ready, NTILE * head + i + 1)
                    dve.scalar_tensor_tensor(maps[:, s, 0, 0:t["nk"]], maps[:, s, 0, 0:t["nk"]], rl[:, s, 0:1],
                                             maps[:, s, 1, 0:t["nk"]], ALU.mult, ALU.add).then_inc(dw_ready, 1)

                def output(t, gn):
                    dve.wait_ge(dav_done, NGRP * head + gn)
                    dve.tensor_copy(y[:, bass.ds(unit, 1), t["q0"]:t["q0"] + t["nq"]],
                                    DO[:, (t["i"] % 2) * P:(t["i"] % 2) * P + t["nq"]].rearrange("p (o c) -> p o c", o=1)
                                    ).then_inc(do_done, 1)

                gn = 0
                for tick in range(NTILE + 2):
                    if tick >= 2:
                        output(TILES[tick - 2], gn)
                    if tick < NTILE:
                        biased(TILES[tick])
                    if 1 <= tick <= NTILE:
                        t = TILES[tick - 1]
                        for g in range(len(t["groups"])):
                            turned_lo(t, g, gn)
                            gn += 1
                    if tick < NTILE:
                        weights(TILES[tick])
                    if filler and tick and tick % 3 == 0:
                        split_lo(Piece(PIECE_IN + 3 + tick // 3 - 1, unit + 1, 3))

            dve.wait_ge(lam_half, 1)
            for j in range(3):
                split_lo(Piece(PIECE_IN + 3 + j))
            with dve.Fori(0, SB_UNITS) as i:
                sb_unit(i)
            with dve.Fori(0, DIFF_UNITS - 1) as i:
                diff_unit(i + SB_UNITS, i, True)
            diff_unit(UNITS - 1, DIFF_UNITS - 1, False)
            for d in range(SB_UNITS):
                dve.wait_ge(xh_ready, 2 * KC + d + 1)
                dve.tensor_tensor(xl[:, d, :], y[:, d, :], xh[:, d, :].bitcast(F32), ALU.subtract).then_inc(x_ready, 1)
            for e in range(DIFF_UNITS):
                d = SB_UNITS + e
                dve.wait_ge(sub_rstd, e + 1)
                if e >= 2:
                    dve.wait_ge(x_ready, 2 * KC + d - 1)
                dve.scalar_tensor_tensor(tmp[:, e % 2, :], y[:, d, :], gains[:, G_SUBLN:G_SUBLN + 1], rstd[:],
                                         ALU.mult, ALU.mult).then_inc(t_ready, 1)
                dve.wait_ge(xh_ready, 2 * KC + d + 1)
                dve.tensor_tensor(xl[:, d, :], tmp[:, e % 2, :], xh[:, d, :].bitcast(F32), ALU.subtract).then_inc(x_ready, 1)
            for d in range(KC):
                dve.wait_ge(wo_full, d + 1)
                dve.tensor_copy(tiles3(y[:, d, :]), bank3((psA, psB)[d % 2])).then_inc(wo_out, 1)
                split_lo(Piece(PIECE_OUT + 3 + d))
            dve.wait_ge(resid_in, 16 * KC)
            post(3, G_MIX_POST, T_POST_MIX, KC)
            x_split(4, G_FF2_PRE, 3 * KC)
            with dve.Fori(0, FF_ITERS - 1) as i:
                ffn(PIECE_FF2, i, FF_ITERS)
            ffn(PIECE_FF2, FF_ITERS - 1, FF_ITERS, last=True)
            post(5, G_FF2_POST, T_POST_FF2, 2 * KC)
            dve.wait_ge(rstd_ready, 7)
            for k in range(KC):
                dve.scalar_tensor_tensor(y[:, k, :], resid[:, k, :], gains[:, KC * G_FINAL + k:KC * G_FINAL + k + 1],
                                         rstd[:], ALU.mult, ALU.mult).then_inc(t_ready, 1)

        @block.gpsimd
        def _(pool):
            pool.memset(y[:], 0.0).then_inc(y_zero, 1)
            pool.wait_ge(spilled, 16 * KC)
            pool.memset(qkv[:, :, T:TP], 0.0).then_inc(zeroed, 1)
            for v in (vh, vl):
                gap = v[:, :].bitcast(F32).rearrange("p (b x d) -> p b x d", x=3, d=HD)[:, :, 1, :]
                pool.memset(gap, 0.0).then_inc(zeroed, 1)

            for q in (qsh, qsl):
                pool.memset(q[:].bitcast(F32), 0.0).then_inc(zeroed, 1)

            def sb_unit(unit):
                for n, s in enumerate(STEPS):
                    w = s["w"]
                    if n >= 2:
                        pool.wait_ge(spl_ready, NSTEP * unit + n - 1)
                    pool.wait_ge(zs_ready, NSTEP * unit + n + 1)
                    pool.sem_inc(held, 1)
                    pool.tensor_scalar(u[:, n % 2, 0:w], zs[:, n % 3, 0:w], U_CLAMP, -3.0e38, ALU.min, ALU.max).then_inc(u_ready, 1)

            with pool.Fori(0, SB_UNITS) as i:
                sb_unit(i)
            pool.wait_ge(t_ready, T_POST_MIX + KC)
            pool.memset(y[:], 0.0).then_inc(y_zero, 1)


def consts():
    i = np.arange(P)
    k, q = i[:, None], i[None, :]
    before = k < q
    c = np.stack([k == q, np.ones((P, P)), k >= q, k < q, before, before], axis=1).astype(np.float32)
    c[:, 5, :] = np.where(before, 3.0e38, -1.0e30)
    huge = -1.0e30
    dist = np.zeros((P, KCOLS), np.float32)
    x = np.arange(SEQ)[None, :] - (SEQ - P)
    dist[:, :SEQ] = np.where(x // HD <= k // HD, -np.abs(k - x), huge)
    dist[:, SEQ:TP] = np.where(q < DEC_SEQ, -np.abs(k - q), huge)
    dist[:, TP:] = -(PAST + k - np.arange(PAST)[None, :])
    return c.reshape(P, 6 * P), dist


def kernel(**inputs):
    import concourse.bacc as bacc
    from concourse.bass_utils import run_bass_kernel_spmd

    a = {n: np.asarray(v) for n, v in inputs.items()}
    f32 = np.float32

    def in_pieces(w):
        return w.reshape(KC, P, -1, P).transpose(2, 1, 0, 3).reshape(-1, P, KC * P)

    c, dist = consts()
    w_in = in_pieces(a["w_in"][0])
    n_sb, n_d = SB_UNITS, DIFF_UNITS
    order = [j * n_sb + n for n in range(n_sb) for j in range(3)]
    order += [3 * n_sb + j * n_d + n for n in range(n_d) for j in range(3)]
    names = ["ff1_pre_g", "ff1_post_g", "mix_pre_g", "mix_post_g", "ff2_pre_g", "ff2_post_g", "final_g"]
    kc = np.concatenate([a["cache_sb_k"][0, 0].reshape(PAST, -1), a["cache_diff_k"][0, 0].reshape(PAST, -1)], axis=1)
    vc = np.concatenate([a["cache_sb_v"][0, 0].reshape(PAST, -1), a["cache_diff_v"][0, 0].reshape(PAST, -1)], axis=1)
    arrays = {
        "xT": np.concatenate([a["x_prompt"][0], a["x_sample"][0]]).T.reshape(KC, P, T),
        "wg1": in_pieces(a["ff1_w_gate"][0]),
        "wu1": in_pieces(a["ff1_w_up"][0]),
        "wd1": a["ff1_w_down"][0].reshape(-1, P, D_MODEL),
        "w_mix": np.concatenate([w_in[order], in_pieces(a["w_out"][0])]),
        "wg2": in_pieces(a["ff2_w_gate"][0]),
        "wu2": in_pieces(a["ff2_w_up"][0]),
        "wd2": a["ff2_w_down"][0].reshape(-1, P, D_MODEL),
        "k_cache": kc.T.reshape(UNITS, P, PAST),
        "v_cache": vc.reshape(PAST // P, P, UNITS, P).transpose(2, 1, 0, 3).reshape(UNITS, P, PAST),
        "gains": np.concatenate([a[n][0].reshape(KC, P).T for n in names] + [a["subln_g"][0].reshape(P, 1)], axis=1),
        "lam": np.stack([a[n][0] for n in ("lam_q1", "lam_q2", "lam_k1", "lam_k2")], axis=1),
        "consts": c,
        "dist_table": dist,
    }
    outs = {"yT": (KC, P, T), "kv": (2 * UNITS, P, T)}

    nc = bacc.Bacc("TRN2", target_bir_lowering=False, num_devices=1, dynamic_dma_scratch_size=1024)
    arrays = {f"in_{n}": np.ascontiguousarray(v) for n, v in arrays.items()}
    args = [nc.dram_tensor(n, v.shape, mybir.dt.from_np(v.dtype), kind="ExternalInput").ap() for n, v in arrays.items()]
    args += [nc.dram_tensor(f"out_{n}", s, F32, kind="ExternalOutput").ap() for n, s in outs.items()]
    build(nc, *args)
    r = run_bass_kernel_spmd(nc, [arrays], core_ids=[0]).results[0]

    yt = r["out_yT"].reshape(D_MODEL, T).T
    kv = r["out_kv"].reshape(UNITS, 2, P, T)

    def rows(units, which, tokens, heads, width):
        t = kv[units, which].reshape(-1, T).T[tokens]
        return np.ascontiguousarray(t).reshape(1, 1, -1, heads, width)

    sb, df = slice(0, SB_UNITS), slice(SB_UNITS, UNITS)
    out = [np.ascontiguousarray(yt[:SEQ])[None], np.ascontiguousarray(yt[SEQ:])[None]]
    for tokens in (slice(0, SEQ), slice(SEQ, T)):
        out += [rows(sb, 0, tokens, HEADS_SB, HD), rows(sb, 1, tokens, HEADS_SB, HD),
                rows(df, 0, tokens, HEADS_DIFF, 2 * HD), rows(df, 1, tokens, HEADS_DIFF, 2 * HD)]
    return tuple(out)
```

```python
import math
from contextlib import ExitStack

import numpy as np

import concourse.bass as bass
from concourse import mybir

P = 128
D_MODEL, SEQ, DEC_SEQ, PAST = 1024, 1024, 32, 256
D_FF = 2816
HEADS_SB, HEADS_DIFF, HD = 8, 4, 64
EPS = 1e-6
LAM_INIT = 0.8 - 0.6 * math.exp(-0.3 * 0)

T = SEQ + DEC_SEQ
NT, TT = 3, T // 3
KC = D_MODEL // P
FF_ITERS = D_FF // P // 2
FF_PIECES = 6
SB_UNITS = HEADS_SB * HD // P
DIFF_UNITS = HEADS_DIFF
UNITS = SB_UNITS + DIFF_UNITS
RING = 3
TP = SEQ + P
KCOLS = TP + PAST
KBLK = KCOLS // P
VW = 192
U_CLAMP = 30.0

F32, F32R = mybir.dt.float32, mybir.dt.float32r
ALU, ACT = mybir.AluOpType, mybir.ActivationFunctionType

PIECE_FF1 = 0
PIECE_IN = PIECE_FF1 + FF_PIECES * FF_ITERS
PIECE_OUT = PIECE_IN + 3 * UNITS
PIECE_FF2 = PIECE_OUT + KC
PIECES = PIECE_FF2 + FF_PIECES * FF_ITERS

G_FF1_PRE, G_FF1_POST, G_MIX_PRE, G_MIX_POST, G_FF2_PRE, G_FF2_POST, G_FINAL = range(7)
G_SUBLN = 7 * KC


def sb_steps():
    steps = []
    for g in range(SEQ // 512):
        for kb in range(4 * g + 3, -1, -1):
            for h in range(2):
                c0 = max(kb * P, g * 512)
                steps.append(dict(g=g, h=h, kb=kb, c0=c0, w=(g + 1) * 512 - c0, off=c0 - g * 512,
                                  diag=kb >= 4 * g, first=kb == 4 * g + 3, last=kb == 0, bank=h))
    for kb in (8, 10, 9):
        steps.append(dict(g=SEQ // 512, h=None, kb=kb, c0=SEQ, w=2 * DEC_SEQ, off=0, diag=kb == 8,
                          first=kb == 8, last=kb == 9, bank=0))
    return steps


def diff_tiles():
    order = list(range(1, SEQ // P, 2)) + list(range(SEQ // P - 2, -1, -2))
    tiles = []
    for i in order:
        nk = (i + 1) * P
        tiles.append(dict(q0=i * P, nq=P, k0=0, nk=nk, t0=SEQ - nk))
    tiles.append(dict(q0=SEQ, nq=DEC_SEQ, k0=SEQ, nk=KCOLS - SEQ, t0=SEQ))
    for n, t in enumerate(tiles):
        t["i"] = n
        blocks = list(range(t["nk"] // P))
        t["groups"] = [blocks[b:b + 4] for b in range(0, len(blocks), 4)]
    return tiles


STEPS = sb_steps()
NSTEP = len(STEPS)
ZS, US = 5, 3
NBIG = sum(s["h"] is not None for s in STEPS)
NMASKED = sum(s["diag"] for s in STEPS)
MASKED = [sum(s["diag"] for s in STEPS[:n]) for n in range(NSTEP)]
NCARRY = sum(not s["last"] for s in STEPS)
CARRIES = [sum(not s["last"] for s in STEPS[:n]) for n in range(NSTEP)]
LAG = 5
FIRST, MIDDLE, TAIL = range(3)


def stage(unit, mode, tick, lag):
    back = tick < lag
    if (back and mode == FIRST) or (not back and mode == TAIL):
        return []
    return [(unit - 1 if back else unit, (tick - lag) % NSTEP)]


def ticks(mode):
    return range(LAG if mode == TAIL else NSTEP)


NQK, NV, NVT = 5, 4, 3
Q_PROMPT, K_PROMPT, Q_SAMPLE, K_SAMPLE, K_CACHE = range(NQK)
V_LOW, V_HIGH, V_SAMPLE, V_CACHE = range(NV)


TILES = diff_tiles()
NTILE = len(TILES)
NGRP = sum(len(t["groups"]) for t in TILES)

T_SPLIT_FF1, T_POST_FF1, T_SPLIT_MIX, T_SUB = 0, KC, 2 * KC, 3 * KC
T_POST_MIX = T_SUB + DIFF_UNITS
T_SPLIT_FF2, T_POST_FF2, T_FINAL = T_POST_MIX + KC, T_POST_MIX + 2 * KC, T_POST_MIX + 3 * KC


def v_pair(t, b, n):
    return t.rearrange("p (b x d) -> p b x d", x=3, d=HD)[:, b:b + n, 0:3:2, :]


def v_one(t, b, n):
    return t[:, b * P:(b + n) * P]


def sample_q(t, h):
    return t[HD * h:HD * h + HD, DEC_SEQ * h:DEC_SEQ * h + DEC_SEQ]


def v_in(layout, src, n):
    return src.rearrange("p (b x d) -> p b x d", x=2, d=HD) if layout is v_pair else src


def build(nc, xT, wg1, wu1, wd1, w_mix, wg2, wu2, wd2, k_cache, v_cache, gains_d, lam_d, consts_d, dist_d,
          yT_out, kv_out):
    ctx = ExitStack()
    with ctx:
        where = [1152]

        def at(name, shape, dt, offset=None):
            size = 4 * int(np.prod(shape[1:]))
            if offset is None:
                offset = where[0]
                where[0] += -(-size // 32) * 32
            return nc.alloc_sbuf_tensor_at(name, shape, dt, offset=offset)

        xh = at("xh", [P, KC, T], F32R)
        xl = at("xl", [P, KC, T], F32R)
        y_at = where[0]
        y = at("y", [P, KC, T], F32)
        raw = at("raw", [P, RING, KC, P], F32)
        wh = at("wh", [P, RING, KC, P], F32R)
        wl = at("wl", [P, RING, KC, P], F32R)
        cst = at("cst", [P, 6, P], F32)
        tri_in = where[0] - 4 * 4 * P
        qsh = at("qsh", [P, 2 * DEC_SEQ], F32R, tri_in)
        qsl = at("qsl", [P, 2 * DEC_SEQ], F32R, tri_in + 8 * DEC_SEQ)
        tri = at("tri", [P, 2, P], F32R)
        gains = at("gains", [P, 7 * KC + 1], F32)
        lamv = at("lamv", [HD, 4], F32)
        lamp = at("lamp", [HD, 2], F32)
        lame = at("lame", [P, 2], F32)
        neglam = at("neglam", [P, 1], F32)
        mx = at("mx", [P, 2, 2], F32)
        nm = at("nm", [P, 2, 2], F32)
        ls = at("ls", [P, 2, 2], F32)
        rl = at("rl", [P, 2, 2], F32)
        c2 = at("c2", [P, 2, 1], F32)
        ident, ones, m01, mneg = cst[:, 0, :], cst[:, 1, :], cst[:, 4, :], cst[:, 5, :]
        shared = where[0]

        resid = at("resid", [P, KC, T], F32)
        rstd = at("rstd", [P, T], F32)
        sq = at("sq", [P, 2, T], F32)
        tmp = at("tmp", [P, 2, T], F32)
        hh = at("hh", [P, 2, T], F32R)
        hl = at("hl", [P, 2, T], F32R)

        where[0] = shared
        kh = at("kh", [P, KCOLS], F32R)
        kl = at("kl", [P, KCOLS], F32R)
        qh = at("qh", [P, TP], F32R)
        ql = at("ql", [P, TP], F32R)
        vh = at("vh", [P, KBLK * VW], F32R)
        vl = at("vl", [P, KBLK * VW], F32R)
        qkv = at("qkv", [P, 3, TP], F32)
        kvc = at("kvc", [P, 2, PAST], F32, y_at + 4 * (KC - 1) * T)
        temps = where[0]
        zs = at("zs", [P, ZS, 512], F32)
        u = at("u", [P, US, 512], F32)
        sph = at("sph", [P, 2, 512], F32R)
        spl = at("spl", [P, 2, 512], F32R)
        wth = at("wth", [P, 2, 512], F32R)
        wtl = at("wtl", [P, 2, 512], F32R)
        small = 4 * 2 * DEC_SEQ
        small_at = y_at + 4 * (KC - 3) * T

        def with_small(big, slots, index, dt):
            little = at(f"small{index}", [P, NSTEP - NBIG, 2 * DEC_SEQ], dt, small_at + (NSTEP - NBIG) * small * index)
            return lambda n: (big[:, n % slots, 0:STEPS[n]["w"]] if n < NBIG else little[:, n - NBIG, :])

        zs_of = with_small(zs, ZS, 0, F32)
        u_of = with_small(u, US, 1, F32)
        sph_of, spl_of = with_small(sph, 2, 2, F32R), with_small(spl, 2, 3, F32R)
        wth_of, wtl_of = with_small(wth, 2, 4, F32R), with_small(wtl, 2, 5, F32R)
        where[0] = temps
        maps = at("maps", [P, 2, 2, SEQ], F32)
        dist = at("dist", [P, SEQ + KCOLS - SEQ], F32)
        dwh = at("dwh", [P, 2, 512], F32R)
        dwl = at("dwl", [P, 2, 512], F32R)

        resid_dram = nc.dram_tensor("resid_scratch", [KC, P, T], F32).ap()

        psA = ctx.enter_context(nc.psum_tensor("psA", [P, 3, 512], F32))
        psB = ctx.enter_context(nc.psum_tensor("psB", [P, 3, 512], F32))
        psC = ctx.enter_context(nc.psum_tensor("psC", [P, 2, 512], F32))
        Z = [psA[:, 2, :], psB[:, 0, :]]
        S = [psB[:, 1, :], psB[:, 2, :]]
        O = psC[:, 0, :]
        VT = psC[:, 1, :]
        DS = [psB[:, 0:2, :], psC[:, 0:2, :]]
        DT, DO = psA[:, 2, :], psB[:, 2, :]
        DVT = psB[:, 1, 0:P]

        def sem(name):
            return ctx.enter_context(nc.semaphore(name))

        const_in, x_in, lam_in = sem("const_in"), sem("x_in"), sem("lam_in")
        raw_in = [sem(f"raw_in{s}") for s in range(RING)]
        cache_in, dist_in, resid_in = sem("cache_in"), sem("dist_in"), sem("resid_in")
        spilled, kv_stored, y_stored = sem("spilled"), sem("kv_stored"), sem("y_stored")
        w_hi, w_ready = sem("w_hi"), sem("w_ready")
        setup_v, lam_prod, lam_sum, lam_exp, lam_half = (
            sem("setup_v"), sem("lam_prod"), sem("lam_sum"), sem("lam_exp"), sem("lam_half"))
        zeroed, y_zero = sem("zeroed"), sem("y_zero")
        sq_ready, sums, ln_done, rstd_ready = sem("sq_ready"), sem("sums"), sem("ln_done"), sem("rstd_ready")
        t_ready, xh_ready, x_ready, r_ready = sem("t_ready"), sem("xh_ready"), sem("x_ready"), sem("r_ready")
        fullA, fullB, silu_done, h_done, hh_done, hl_done, y_done = (
            sem("fullA"), sem("fullB"), sem("silu_done"), sem("h_done"), sem("hh_done"), sem("hl_done"), sem("y_done"))
        proj_full, proj_out, vt_full, unit_done = (
            sem("proj_full"), sem("proj_out"), sem("vt_full"), sem("unit_done"))
        qk_hi, qk_lo, v_hi, v_lo = sem("qk_hi"), sem("qk_lo"), sem("v_hi"), sem("v_lo")
        z_full, zs_ready, u_ready, e_ready, l_ready, sp_whole, arg_whole, sp_ready, sph_ready, spl_ready = (
            sem("z_full"), sem("zs_ready"), sem("u_ready"), sem("e_ready"), sem("l_ready"), sem("sp_whole"),
            sem("arg_whole"),
            sem("sp_ready"), sem("sph_ready"), sem("spl_ready"))
        s_full, arg_ready, carried, wt_ready, wth_ready, wtl_ready, av_done, o_full, o_done = (
            sem("s_full"), sem("arg_ready"), sem("carried"), sem("wt_ready"), sem("wth_ready"), sem("wtl_ready"),
            sem("av_done"), sem("o_full"), sem("o_done"))
        dist_ready, ds_full, ds_read, nm_ready, de_done, rl_ready, c2_ready, e2_ready, dw_ready = (
            sem("dist_ready"), sem("ds_full"), sem("ds_read"), sem("nm_ready"), sem("de_done"), sem("rl_ready"),
            sem("c2_ready"), sem("e2_ready"), sem("dw_ready"))
        dt_full, dwh_ready, dwl_ready, dav_done, do_done = (
            sem("dt_full"), sem("dwh_ready"), sem("dwl_ready"), sem("dav_done"), sem("do_done"))
        sub_sq, sub_sum, sub_ln, sub_rstd, sub_t = (
            sem("sub_sq"), sem("sub_sum"), sem("sub_ln"), sem("sub_rstd"), sem("sub_t"))
        wo_full, wo_out = sem("wo_full"), sem("wo_out")
        held = sem("held")

        block = ctx.enter_context(nc.Block())

        def v_part(part, bank):
            if part == V_CACHE:
                return SEQ // P + 1, 2, kvc[:, 1, :]
            n = 1 if part == V_SAMPLE else 4
            return 4 * part, n, bank[:, 0:n * P]

        def bank3(ps):
            return ps[:, :, 0:TT]

        def tiles3(ap):
            return ap.rearrange("p (t c) -> p t c", t=NT)

        class Piece:
            def __init__(self, n, i=0, per=0):
                self.slot = n % RING
                self.landed = 16 * (n // RING + 1) + (16 * (per // RING)) * i
                self.count = n + 1 + per * i

        @block.sync
        def _(sp):
            def load_piece(src, piece, n_static=None):
                if n_static is None or n_static >= RING:
                    sp.wait_ge(w_ready, piece.count - RING)
                sp.dma_start(raw[:, piece.slot, :, :].rearrange("p k c -> p (k c)"), src).then_inc(raw_in[piece.slot], 16)

            def ff_sources(gate, up, down, i):
                for j in range(2):
                    yield gate, 2 * i + j
                    yield up, 2 * i + j
                for j in range(2):
                    yield down, 2 * i + j

            def one(w, n):
                return w[bass.ds(n, 1), :, :].rearrange("o p c -> (o p) c")

            sp.dma_start(cst[:].rearrange("p a b -> p (a b)"), consts_d).then_inc(const_in, 16)
            sp.dma_start(gains[:], gains_d).then_inc(const_in, 16)
            for k in range(KC):
                sp.dma_start(resid[:, k, :], xT[k, :, :]).then_inc(x_in, 16)
            for j, (w, n) in enumerate(ff_sources(wg1, wu1, wd1, 0)):
                load_piece(w[n, :, :], Piece(PIECE_FF1 + j), j)
            sp.dma_start(lamv[:], lam_d).then_inc(lam_in, 16)
            with sp.Fori(1, FF_ITERS) as i:
                for j, (w, n) in enumerate(ff_sources(wg1, wu1, wd1, i)):
                    load_piece(one(w, n), Piece(PIECE_FF1 + j, i, FF_PIECES))
            for j in range(6):
                load_piece(w_mix[j, :, :], Piece(PIECE_IN + j))
            sp.wait_ge(x_ready, 2 * KC)
            for k in range(KC):
                sp.dma_start(resid_dram[k, :, :], resid[:, k, :]).then_inc(spilled, 16)
            sp.wait_ge(spilled, 16 * KC)

            def load_cache(unit):
                sp.dma_start(kvc[:, 0, :], k_cache[bass.ds(unit, 1), :, :].rearrange("o p c -> (o p) c")).then_inc(cache_in, 16)
                sp.dma_start(kvc[:, 1, :], v_cache[bass.ds(unit, 1), :, :].rearrange("o p c -> (o p) c")).then_inc(cache_in, 16)

            def unit_dmas(unit, last=False):
                for j in range(2):
                    load_piece(one(w_mix, 3 * unit + 6 + j), Piece(PIECE_IN + 6 + j, unit, 3))
                sp.wait_ge(proj_out, 9 * unit + 9)
                for j in range(2):
                    sp.dma_start(kv_out[bass.ds(2 * unit + j, 1), :, :].rearrange("o p c -> (o p) c"),
                                 qkv[:, 1 + j, 0:T]).then_inc(kv_stored, 16)
                load_piece(one(w_mix, 3 * unit + 8), Piece(PIECE_IN + 8, unit, 3))
                if not last:
                    sp.wait_ge(qk_lo, NQK * unit + K_CACHE + 1)
                    sp.wait_ge(v_lo, NV * unit + V_CACHE + 1)
                    load_cache(unit + 1)

            load_cache(0)
            with sp.Fori(0, SB_UNITS) as i:
                unit_dmas(i)
            sp.wait_ge(unit_done, 1)
            sp.dma_start(dist[:], dist_d).then_inc(dist_in, 16)
            with sp.Fori(SB_UNITS, UNITS - 1) as i:
                unit_dmas(i)
            unit_dmas(UNITS - 1, last=True)
            sp.wait_ge(unit_done, 1 + DIFF_UNITS)
            for k in range(KC):
                sp.dma_start(resid[:, k, :], resid_dram[k, :, :]).then_inc(resid_in, 16)
            for j in range(6, KC):
                load_piece(w_mix[3 * UNITS + j, :, :], Piece(PIECE_OUT + j))
            with sp.Fori(0, FF_ITERS) as i:
                for j, (w, n) in enumerate(ff_sources(wg2, wu2, wd2, i)):
                    load_piece(one(w, n), Piece(PIECE_FF2 + j, i, FF_PIECES))
            for k in range(KC):
                sp.wait_ge(t_ready, T_FINAL + k + 1)
                sp.dma_start(yT_out[k, :, :], y[:, k, :]).then_inc(y_stored, 16)
            sp.wait_ge(y_stored, 16 * KC)
            sp.wait_ge(kv_stored, 32 * UNITS)

        def split3(pe, out, wa, wb, xa, xb, start, stop, group=True):
            pe.matmul(out, wa, xa, start=start, stop=False, skip_group_check=not group)
            pe.matmul(out, wa, xb, start=False, stop=False, skip_group_check=not group)
            return pe.matmul(out, wb, xa, start=False, stop=stop, skip_group_check=not group)

        @block.tensor
        def _(pe):
            def dense(ps, piece, rh, rl_, x_base=None):
                pe.wait_ge(w_ready, piece.count)
                for k in range(KC):
                    if x_base is not None:
                        pe.wait_ge(x_ready, x_base + k + 1)
                    for wa, ra in ((wh, rh), (wh, rl_), (wl, rh)):
                        for t in range(NT):
                            last = pe.matmul(ps[:, t, 0:TT], wa[:, piece.slot, k, :], ra[:, k, t * TT:(t + 1) * TT],
                                             start=(k == 0 and wa is wh and ra is rh),
                                             stop=(k == KC - 1 and wa is wl))
                return last

            def stats(norm):
                for k in range(KC):
                    pe.wait_ge(sq_ready, KC * norm + k + 1)
                    for t in range(NT):
                        last = pe.matmul(psA[:, t, 0:TT], ones, sq[:, k % 2, t * TT:(t + 1) * TT],
                                         start=k == 0, stop=k == KC - 1)
                    last.then_inc(sums, 1)

            def ffn(base, i, n_it, x_base):
                ii = i + n_it
                piece = [Piece(base + j, i, FF_PIECES) for j in range(FF_PIECES)]
                for j in range(2):
                    if j == 0:
                        pe.wait_ge(y_done, 8 * ii + 7)
                    else:
                        pe.wait_ge(silu_done, 6 * ii + 3)
                    dense(psA, piece[2 * j], xh, xl, x_base if j == 0 else None).then_inc(fullA, 1)
                    if j == 0:
                        pe.wait_ge(y_done, 8 * ii + 8)
                    else:
                        pe.wait_ge(h_done, 6 * ii + 3)
                    dense(psB, piece[2 * j + 1], xh, xl).then_inc(fullB, 1)
                for d in range(KC):
                    ps, full = ((psA, fullA), (psB, fullB))[d % 2]
                    if d == 0:
                        pe.wait_ge(silu_done, 6 * ii + 6)
                        pe.wait_ge(hl_done, 6 * ii + 3)
                        pe.wait_ge(w_ready, piece[5].count)
                    elif d == 1:
                        pe.wait_ge(h_done, 6 * ii + 6)
                    else:
                        pe.wait_ge(y_done, 8 * ii + 8 + d - 1)
                    for j in range(2):
                        for t in range(NT):
                            if d == 0 and j == 1:
                                pe.wait_ge(hl_done, 6 * ii + 3 + t + 1)
                            s = piece[4 + j].slot
                            c = slice(t * TT, (t + 1) * TT)
                            last = split3(pe, ps[:, t, 0:TT], wh[:, s, d, :], wl[:, s, d, :], hh[:, j, c], hl[:, j, c],
                                          start=j == 0, stop=j == 1)
                    last.then_inc(full, 1)

            def proj_part(unit, f, part, parts, x_base=None):
                piece = Piece(PIECE_IN + f // 3, unit, 3)
                bank = psA[:, f % 2, 0:TT]
                if part == 0:
                    if f % 3 == 0:
                        pe.wait_ge(w_ready, piece.count)
                    if f >= 2:
                        pe.wait_ge(proj_out, 9 * unit + f - 1)
                    elif f == 0 and not (isinstance(unit, int) and unit == 0):
                        pe.wait_ge(proj_out, 9 * unit)
                todo = [(k, n) for k in range(KC) for n in range(3)]
                for k, n in todo[part * len(todo) // parts:(part + 1) * len(todo) // parts]:
                    if x_base is not None and f == 0 and n == 0:
                        pe.wait_ge(x_ready, x_base + k + 1)
                    wa, xa = ((wh, xh), (wh, xl), (wl, xh))[n]
                    last = pe.matmul(bank, wa[:, piece.slot, k, :], xa[:, k, (f % 3) * TT:(f % 3 + 1) * TT],
                                     start=(k, n) == todo[0], stop=(k, n) == todo[-1])
                if part == parts - 1:
                    last.then_inc(proj_full, 1)

            def turn_values(bank, unit, b0, n):
                for b in range(n):
                    last = pe.transpose(bank[:, b * P:(b + 1) * P], qkv[:, 2, (b0 + b) * P:(b0 + b + 1) * P], ident)
                last.then_inc(vt_full, 1)

            def sb_unit(unit, mode):
                def scores(unit, n):
                    s = STEPS[n]
                    if n >= 2:
                        pe.wait_ge(zs_ready, NSTEP * unit + n - 1)
                    elif n == 0 and mode != FIRST:
                        pe.wait_ge(zs_ready, NSTEP * unit)
                    if n == 0:
                        pe.wait_ge(qk_lo, NQK * unit + K_PROMPT + 1)
                    elif n == NBIG:
                        pe.wait_ge(qk_lo, NQK * unit + K_CACHE + 1)
                    kc = slice(s["kb"] * P, (s["kb"] + 1) * P)
                    out = Z[n % 2][:, 0:s["w"]]
                    if s["h"] is None:
                        last = split3(pe, out, kh[:, kc], kl[:, kc], qsh[:], qsl[:], start=True, stop=True)
                    else:
                        r = slice(HD * s["h"], HD * s["h"] + HD)
                        qc = slice(s["c0"], s["c0"] + s["w"])
                        last = split3(pe, out, kh[r, kc], kl[r, kc], qh[r, qc], ql[r, qc], start=True, stop=True)
                    last.then_inc(z_full, 1)

                def add_tri(n, which, start):
                    s = STEPS[n]
                    out = S[s["bank"]][:, s["off"]:s["off"] + s["w"]]
                    pe.matmul(out, tri[:, which, :], sph_of(n), start=start, stop=False, skip_group_check=True)
                    return pe.matmul(out, tri[:, which, :], spl_of(n), start=False, stop=False, skip_group_check=True)

                def suffix(unit, n):
                    pe.wait_ge(spl_ready, NSTEP * unit + n + 1)
                    add_tri(n, 0, STEPS[n]["first"]).then_inc(s_full, 1)

                def carry_on(unit, n):
                    pe.wait_ge(arg_ready, NSTEP * unit + n + 1)
                    if not STEPS[n]["last"]:
                        add_tri(n, 1, False).then_inc(carried, 1)

                def values(unit, n):
                    s = STEPS[n]
                    pe.wait_ge(wtl_ready, NSTEP * unit + n + 1)
                    if s["first"] and s["h"] != 1:
                        pe.wait_ge(v_lo, NV * unit + (V_LOW, V_HIGH, V_CACHE)[s["g"]] + 1)
                        if s["g"] > 0:
                            pe.wait_ge(o_done, 3 * unit + s["g"])
                        elif mode != FIRST:
                            pe.wait_ge(o_done, 3 * unit)
                    heads = (s["h"],) if s["h"] is not None else (0, 1)
                    wt_hi, wt_lo = wth_of(n), wtl_of(n)
                    for x, h in enumerate(heads):
                        w = s["w"] // len(heads)
                        vc = slice(s["kb"] * VW + HD * h, s["kb"] * VW + HD * h + P)
                        wc = slice(x * w, (x + 1) * w)
                        last = split3(pe, O[:, s["off"]:s["off"] + w], vh[:, vc], vl[:, vc], wt_hi[:, wc], wt_lo[:, wc],
                                      start=s["first"] and h == 0, stop=False, group=False)
                    last.then_inc(av_done, 1)

                for tick in ticks(mode):
                    for a in stage(unit, mode, tick, 3):
                        suffix(*a)
                    for a in stage(unit, mode, tick, 0):
                        scores(*a)
                    for a in stage(unit, mode, tick, 5):
                        values(*a)
                    if mode != TAIL:
                        if tick == 1:
                            pe.wait_ge(proj_out, 9 * unit + 9)
                            turn_values(VT, unit, 0, 4)
                        elif tick == 3:
                            pe.wait_ge(v_lo, NV * unit + V_LOW + 1)
                            turn_values(VT, unit, 4, 4)
                        elif tick == 5:
                            pe.wait_ge(v_lo, NV * unit + V_HIGH + 1)
                            turn_values(VT, unit, SEQ // P, 1)
                        proj_part(unit + 1, tick // 3, tick % 3, 3)
                    for a in stage(unit, mode, tick, 3):
                        carry_on(*a)

            def diff_unit(unit, head, filler):
                def scores(t):
                    if t["i"] == 0:
                        pe.wait_ge(qk_lo, NQK * unit + K_PROMPT + 1)
                    elif t["k0"]:
                        pe.wait_ge(qk_lo, NQK * unit + K_CACHE + 1)
                    for m in range(2):
                        if t["i"] >= 1:
                            pe.wait_ge(ds_read, 2 * NTILE * head + 2 * (t["i"] - 1) + m + 1)
                        r = slice(HD * m, HD * m + HD)
                        for c in range(0, t["nk"], 512):
                            w = min(512, t["nk"] - c)
                            qc, kc = slice(t["q0"], t["q0"] + P), slice(t["k0"] + c, t["k0"] + c + w)
                            last = split3(pe, DS[m][:, c // 512, 0:w], qh[r, qc], ql[r, qc], kh[r, kc], kl[r, kc],
                                          start=True, stop=True)
                        last.then_inc(ds_full, 1)

                def turn(t, g, gn):
                    if g == 0:
                        pe.wait_ge(dw_ready, NTILE * head + t["i"] + 1)
                    if gn >= 1:
                        pe.wait_ge(dwl_ready, NGRP * head + gn)
                    else:
                        pe.wait_ge(v_lo, NV * unit + V_HIGH + 1)
                    for x, b in enumerate(t["groups"][g]):
                        last = pe.transpose(DT[:, x * P:(x + 1) * P], maps[:, t["i"] % 2, 0, b * P:(b + 1) * P], ident)
                    last.then_inc(dt_full, 1)

                def values(t, g, gn):
                    pe.wait_ge(dwl_ready, NGRP * head + gn + 1)
                    if t["k0"]:
                        pe.wait_ge(v_lo, NV * unit + V_CACHE + 1)
                    if g == 0 and t["i"] >= 2:
                        pe.wait_ge(do_done, NTILE * head + t["i"] - 1)
                    out = DO[:, (t["i"] % 2) * P:(t["i"] % 2) * P + t["nq"]]
                    for x, b in enumerate(t["groups"][g]):
                        kb = t["k0"] // P + b
                        vc, wc = slice(kb * P, (kb + 1) * P), slice(x * P, x * P + t["nq"])
                        last = split3(pe, out, vh[:, vc], vl[:, vc], dwh[:, gn % 2, wc], dwl[:, gn % 2, wc],
                                      start=g == 0 and x == 0, stop=b == t["groups"][-1][-1])
                    last.then_inc(dav_done, 1)

                gn = 0
                for tick in range(NTILE + 1):
                    if tick < NTILE:
                        scores(TILES[tick])
                    if tick == 0:
                        pe.wait_ge(proj_out, 9 * unit + 9)
                        turn_values(VT, unit, 0, 4)
                        turn_values(DT, unit, 4, 4)
                        turn_values(DVT, unit, SEQ // P, 1)
                    t = TILES[tick - 1] if tick else None
                    if t:
                        turn(t, 0, gn)
                    if filler and tick < NTILE:
                        proj_part(unit + 1, tick, 0, 2)
                    if t:
                        values(t, 0, gn)
                        gn += 1
                        if len(t["groups"]) > 1:
                            turn(t, 1, gn)
                    if filler and tick < NTILE:
                        proj_part(unit + 1, tick, 1, 2)
                    if t and len(t["groups"]) > 1:
                        values(t, 1, gn)
                        gn += 1
                pe.drain().then_inc(unit_done, 1)

            pe.wait_ge(const_in, 32)
            stats(0)
            with pe.Fori(0, FF_ITERS) as i:
                ffn(PIECE_FF1, i, 0, 0)
            pe.wait_ge(y_done, 8 * FF_ITERS + 7)
            stats(1)
            pe.wait_ge(lam_prod, 1)
            pe.matmul(psC[:, 0, 0:2], ones[0:HD, :], lamp[:], start=True, stop=True).then_inc(lam_sum, 1)
            stats(2)
            for f in range(9):
                proj_part(0, f, 0, 1, KC)
            sb_unit(0, FIRST)
            with pe.Fori(1, SB_UNITS) as i:
                sb_unit(i, MIDDLE)
            sb_unit(SB_UNITS, TAIL)
            pe.drain().then_inc(unit_done, 1)
            pe.wait_ge(o_done, 3 * SB_UNITS)
            with pe.Fori(0, DIFF_UNITS - 1) as i:
                diff_unit(i + SB_UNITS, i, True)
            diff_unit(UNITS - 1, DIFF_UNITS - 1, False)
            for d in range(DIFF_UNITS):
                pe.wait_ge(sub_sq, d + 1)
                if d >= 2:
                    pe.wait_ge(sub_ln, d - 1)
                ps = (psA, psB)[d % 2]
                for t in range(NT):
                    last = pe.matmul(ps[:, t, 0:TT], ones, sq[:, d % 2, t * TT:(t + 1) * TT], start=True, stop=True)
                last.then_inc(sub_sum, 1)
            pe.wait_ge(x_ready, 3 * KC)
            for d in range(KC):
                if d >= 2:
                    pe.wait_ge(wo_out, d - 1)
                dense((psA, psB)[d % 2], Piece(PIECE_OUT + d), xh, xl).then_inc(wo_full, 1)
            pe.wait_ge(wo_out, KC)
            stats(3)
            stats(4)
            with pe.Fori(0, FF_ITERS) as i:
                ffn(PIECE_FF2, i, FF_ITERS, 3 * KC)
            pe.wait_ge(y_done, 8 * 2 * FF_ITERS + 7)
            stats(5)
            stats(6)

        @block.scalar
        def _(act):
            def split_hi(piece):
                act.wait_ge(raw_in[piece.slot], piece.landed)
                act.activation(wh[:, piece.slot, :, :], raw[:, piece.slot, :, :], ACT.Copy).then_inc(w_hi, 1)

            def stats(norm, src, ready, base):
                for k in range(KC):
                    act.wait_ge(ready, base + k + 1 if ready is not x_in else 16 * KC)
                    if norm > 0 or k >= 2:
                        act.wait_ge(sums, KC * norm + k - 1)
                    act.activation(sq[:, k % 2, :], src[:, k, :], ACT.Square).then_inc(sq_ready, 1)
                act.preload_act_table_set("natural_log_exp_and_others")
                act.wait_ge(sums, KC * (norm + 1))
                act.activation(tiles3(rstd[:]), bank3(psA), ACT.Ln, scale=1.0 / D_MODEL, bias=EPS).then_inc(ln_done, 1)
                act.wait_ge(ln_done, norm + 1)
                act.activation(rstd[:], rstd[:], ACT.Exp, scale=-0.5).then_inc(rstd_ready, 1)

            def x_hi(t_base):
                for k in range(KC):
                    act.wait_ge(t_ready, t_base + k + 1)
                    act.activation(xh[:, k, :], tmp[:, k % 2, :], ACT.Copy).then_inc(xh_ready, 1)

            def ffn(base, i, n_it, last=False):
                ii = i + n_it
                piece = [Piece(base + j, i, FF_PIECES) for j in range(2 * FF_PIECES)]

                def silu(j):
                    act.wait_ge(fullA, 6 * ii + j + 1)
                    for t in range(NT):
                        c = slice(t * TT, (t + 1) * TT)
                        act.activation(tmp[:, j, c], psA[:, t, 0:TT], ACT.Silu).then_inc(silu_done, 1)

                def hidden_hi(j):
                    for t in range(NT):
                        c = slice(t * TT, (t + 1) * TT)
                        act.wait_ge(h_done, 6 * ii + 3 * j + t + 1)
                        act.activation(hh[:, j, c], tmp[:, j, c], ACT.Copy).then_inc(hh_done, 1)

                silu(0)
                split_hi(piece[3])
                hidden_hi(0)
                split_hi(piece[4])
                silu(1)
                split_hi(piece[5])
                hidden_hi(1)
                if not last:
                    split_hi(piece[6])
                    act.wait_ge(fullB, 6 * ii + 6)
                    split_hi(piece[7])
                    split_hi(piece[8])

            stats(0, resid, x_in, 0)
            for n in range(RING):
                split_hi(Piece(n))
            x_hi(T_SPLIT_FF1)
            act.preload_act_table_set("silu_and_others")
            with act.Fori(0, FF_ITERS) as i:
                ffn(PIECE_FF1, i, 0)
            stats(1, y, y_done, 8 * FF_ITERS)
            stats(2, resid, r_ready, 0)
            act.wait_ge(lam_sum, 1)
            act.activation(lame[:], psC[:, 0, 0:2], ACT.Exp).then_inc(lam_exp, 1)
            x_hi(T_SPLIT_MIX)

            def proj_evac(unit, f):
                act.wait_ge(proj_full, 9 * unit + f + 1)
                act.activation(qkv[:, f // 3, (f % 3) * TT:(f % 3 + 1) * TT], psA[:, f % 2, 0:TT], ACT.Copy,
                               scale=HD ** -0.5 if f < 3 else 1.0).then_inc(proj_out, 1)

            def qk_high(unit, part, pair=True):
                if part == Q_PROMPT:
                    act.wait_ge(proj_out, 9 * unit + 3)
                    last = act.activation(qh[:, 0:SEQ], qkv[:, 0, 0:SEQ], ACT.Copy)
                elif part == K_PROMPT:
                    act.wait_ge(proj_out, 9 * unit + 6)
                    last = act.activation(kh[:, 0:SEQ], qkv[:, 1, 0:SEQ], ACT.Copy)
                elif part == Q_SAMPLE and pair:
                    for h in range(2):
                        last = act.activation(sample_q(qsh, h), qkv[HD * h:HD * h + HD, 0, SEQ:T], ACT.Copy)
                elif part == Q_SAMPLE:
                    last = act.activation(qh[:, SEQ:TP], qkv[:, 0, SEQ:TP], ACT.Copy)
                elif part == K_SAMPLE:
                    last = act.activation(kh[:, SEQ:TP], qkv[:, 1, SEQ:TP], ACT.Copy)
                else:
                    act.wait_ge(cache_in, 32 * unit + 32)
                    last = act.activation(kh[:, TP:KCOLS], kvc[:, 0, :], ACT.Copy)
                last.then_inc(qk_hi, 1)

            def v_high(unit, part, v_out, bank=None):
                if part == V_CACHE:
                    act.wait_ge(cache_in, 32 * unit + 32)
                else:
                    act.wait_ge(vt_full, NVT * unit + part + 1)
                b, n, src = v_part(part, bank)
                act.activation(v_out(vh, b, n), v_in(v_out, src, n), ACT.Copy).then_inc(v_hi, 1)

            def next_evac(unit, f):
                if f == 0:
                    act.wait_ge(qk_lo, NQK * unit + K_PROMPT + 1)
                elif f == 2:
                    act.wait_ge(qk_lo, NQK * unit + Q_SAMPLE + 1)
                elif f == 3:
                    act.wait_ge(kv_stored, 32 * unit + 32)
                elif f == 5:
                    act.wait_ge(qk_lo, NQK * unit + K_SAMPLE + 1)
                elif f == 6:
                    act.wait_ge(vt_full, NVT * unit + NVT)
                proj_evac(unit + 1, f)

            def sb_unit(unit, mode):
                def sp_hi(unit, n):
                    act.wait_ge(sp_ready, NSTEP * unit + n + 1)
                    if 2 <= n < NBIG:
                        if STEPS[n - 2]["last"]:
                            act.wait_ge(s_full, NSTEP * unit + n - 1)
                        else:
                            act.wait_ge(carried, NCARRY * unit + CARRIES[n - 2] + 1)
                    act.activation(sph_of(n), u_of(n), ACT.Copy).then_inc(sph_ready, 1)

                def weight_exp(unit, n):
                    act.wait_ge(arg_ready, NSTEP * unit + n + 1)
                    act.activation(zs_of(n), zs_of(n), ACT.Exp).then_inc(wt_ready, 1)

                def soft_exp(unit, n):
                    act.wait_ge(u_ready, NSTEP * unit + n + 1)
                    act.activation(u_of(n), u_of(n), ACT.Exp).then_inc(e_ready, 1)

                def weight_hi(unit, n):
                    act.wait_ge(wt_ready, NSTEP * unit + n + 1)
                    if 2 <= n < NBIG:
                        act.wait_ge(av_done, NSTEP * unit + n - 1)
                    elif n < 2 and mode != FIRST:
                        act.wait_ge(av_done, NSTEP * (unit - 1) + NBIG - 2 + n + 1)
                    act.activation(wth_of(n), zs_of(n), ACT.Copy).then_inc(wth_ready, 1)

                def soft_ln(unit, n):
                    act.wait_ge(e_ready, NSTEP * unit + n + 1)
                    act.activation(u_of(n), u_of(n), ACT.Ln, bias=1.0).then_inc(l_ready, 1)

                for tick in ticks(mode):
                    if mode != TAIL and tick == 0:
                        proj_evac(unit, 8)
                    for lag, work in ((4, weight_hi), (1, soft_exp), (2, sp_hi), (1, soft_ln), (3, weight_exp)):
                        for a in stage(unit, mode, tick, lag):
                            work(*a)
                    if mode == TAIL:
                        continue
                    if tick == 1:
                        split_hi(Piece(PIECE_IN + 5, unit, 3))
                        v_high(unit, V_LOW, v_pair, VT)
                    elif tick == 2:
                        qk_high(unit, Q_SAMPLE)
                    elif tick == 3:
                        v_high(unit, V_HIGH, v_pair, VT)
                    elif tick == 4:
                        qk_high(unit, K_SAMPLE)
                    elif tick == 5:
                        v_high(unit, V_SAMPLE, v_pair, VT)
                    elif tick == 7:
                        v_high(unit, V_CACHE, v_pair)
                    elif tick == 8:
                        qk_high(unit, K_CACHE)
                    if tick and tick % 3 == 0:
                        next_evac(unit, tick // 3 - 1)
                    if tick and tick % 9 == 0:
                        split_hi(Piece(PIECE_IN + 3 + tick // 9 - 1, unit + 1, 3))
                    if tick == NBIG:
                        act.wait_ge(z_full, NSTEP * unit + NBIG)
                        qk_high(unit + 1, Q_PROMPT)
                        qk_high(unit + 1, K_PROMPT)

            def diff_unit(unit, head, filler):
                def exps(t):
                    s = t["i"] % 2
                    act.wait_ge(nm_ready, NTILE * head + t["i"] + 1)
                    for m in range(2):
                        act.activation(maps[:, s, m, 0:t["nk"]], maps[:, s, m, 0:t["nk"]], ACT.Exp, bias=nm[:, s, m:m + 1],
                                       accum_out=ls[:, s, m:m + 1]).then_inc(de_done, 1)

                def turned_hi(t, g, gn):
                    w = P * len(t["groups"][g])
                    act.wait_ge(dt_full, NGRP * head + gn + 1)
                    if gn >= 2:
                        act.wait_ge(dav_done, NGRP * head + gn - 1)
                    act.activation(dwh[:, gn % 2, 0:w], DT[:, 0:w], ACT.Copy).then_inc(dwh_ready, 1)

                gn = 0
                for tick in range(NTILE + 1):
                    if tick == 0:
                        proj_evac(unit, 8)
                        act.wait_ge(unit_done, head + 1)
                        v_high(unit, V_LOW, v_one, VT)
                        v_high(unit, V_HIGH, v_one, DT)
                        v_high(unit, V_SAMPLE, v_one, DVT)
                    elif tick == NTILE and filler:
                        act.wait_ge(ds_full, 2 * NTILE * head + 2 * NTILE)
                        qk_high(unit + 1, Q_PROMPT)
                        qk_high(unit + 1, K_PROMPT)
                    t = TILES[tick - 1] if tick else None
                    if t:
                        turned_hi(t, 0, gn)
                        gn += 1
                    if tick < NTILE:
                        exps(TILES[tick])
                    if t and len(t["groups"]) > 1:
                        turned_hi(t, 1, gn)
                        gn += 1
                    if tick == 0:
                        split_hi(Piece(PIECE_IN + 5, unit, 3))
                        qk_high(unit, Q_SAMPLE, pair=False)
                    elif tick == 1:
                        qk_high(unit, K_SAMPLE)
                        v_high(unit, V_CACHE, v_one)
                        qk_high(unit, K_CACHE)
                    if filler and 0 < tick < NTILE:
                        next_evac(unit, tick - 1)
                        if tick % 3 == 0:
                            split_hi(Piece(PIECE_IN + 3 + tick // 3 - 1, unit + 1, 3))

            for f in range(8):
                if f == 2:
                    act.wait_ge(spilled, 16 * KC)
                    act.wait_ge(zeroed, 5)
                proj_evac(0, f)
                if f % 3 == 2:
                    split_hi(Piece(PIECE_IN + 3 + f // 3))
                if f in (2, 5):
                    qk_high(0, f // 3)
            sb_unit(0, FIRST)
            with act.Fori(1, SB_UNITS) as i:
                sb_unit(i, MIDDLE)
            sb_unit(SB_UNITS, TAIL)
            with act.Fori(0, DIFF_UNITS - 1) as i:
                diff_unit(i + SB_UNITS, i, True)
            diff_unit(UNITS - 1, DIFF_UNITS - 1, False)
            act.wait_ge(do_done, NTILE * DIFF_UNITS)
            act.wait_ge(kv_stored, 32 * UNITS)

            def sub_square(e):
                act.activation(sq[:, e % 2, :], y[:, SB_UNITS + e, :], ACT.Square).then_inc(sub_sq, 1)

            sub_square(0)
            sub_square(1)
            for d in range(SB_UNITS):
                act.activation(xh[:, d, :], y[:, d, :], ACT.Copy).then_inc(xh_ready, 1)
            for e in range(DIFF_UNITS):
                act.wait_ge(sub_sum, e + 1)
                if e >= 1:
                    act.wait_ge(t_ready, T_SUB + e)
                act.activation(tiles3(rstd[:]), bank3((psA, psB)[e % 2]), ACT.Ln, scale=1.0 / P, bias=EPS).then_inc(sub_ln, 1)
                if e + 2 < DIFF_UNITS:
                    sub_square(e + 2)
                act.wait_ge(sub_ln, e + 1)
                act.activation(rstd[:], rstd[:], ACT.Exp, scale=-0.5).then_inc(sub_rstd, 1)
                act.wait_ge(t_ready, T_SUB + e + 1)
                act.activation(xh[:, SB_UNITS + e, :], tmp[:, e % 2, :], ACT.Copy).then_inc(xh_ready, 1)
            for d in range(KC):
                act.wait_ge(wo_full, d + 1)
                split_hi(Piece(PIECE_OUT + 3 + d))
            stats(3, y, wo_out, 0)
            stats(4, resid, r_ready, KC)
            x_hi(T_SPLIT_FF2)
            act.preload_act_table_set("silu_and_others")
            with act.Fori(0, FF_ITERS - 1) as i:
                ffn(PIECE_FF2, i, FF_ITERS)
            ffn(PIECE_FF2, FF_ITERS - 1, FF_ITERS, last=True)
            stats(5, y, y_done, 8 * 2 * FF_ITERS)
            stats(6, resid, r_ready, 2 * KC)

        @block.vector
        def _(dve):
            dve.sem_inc(y_done, 8)

            def split_lo(piece):
                dve.wait_ge(w_hi, piece.count)
                dve.tensor_tensor(wl[:, piece.slot, :, :], raw[:, piece.slot, :, :], wh[:, piece.slot, :, :].bitcast(F32),
                                  ALU.subtract).then_inc(w_ready, 1)

            def x_split(norm, g, x_base):
                dve.wait_ge(rstd_ready, norm + 1)

                def scaled(k):
                    if k >= 2:
                        dve.wait_ge(x_ready, x_base + k - 1)
                    dve.scalar_tensor_tensor(tmp[:, k % 2, :], resid[:, k, :], gains[:, KC * g + k:KC * g + k + 1],
                                             rstd[:], ALU.mult, ALU.mult).then_inc(t_ready, 1)

                def low(k):
                    dve.wait_ge(xh_ready, x_base + k + 1)
                    dve.tensor_tensor(xl[:, k, :], tmp[:, k % 2, :], xh[:, k, :].bitcast(F32), ALU.subtract).then_inc(x_ready, 1)

                for k in range(KC):
                    scaled(k)
                    if k >= 1:
                        low(k - 1)
                low(KC - 1)

            def post(norm, g, t_base, r_base):
                dve.wait_ge(rstd_ready, norm + 1)

                def add(k):
                    dve.wait_ge(t_ready, t_base + k + 1)
                    dve.scalar_tensor_tensor(resid[:, k, :], tmp[:, k % 2, :], gains[:, KC * g + k:KC * g + k + 1],
                                             resid[:, k, :], ALU.mult, ALU.add).then_inc(r_ready, 1)

                for k in range(KC):
                    if k >= 2:
                        dve.wait_ge(r_ready, r_base + k - 1)
                    dve.tensor_tensor(tmp[:, k % 2, :], y[:, k, :], rstd[:], ALU.mult).then_inc(t_ready, 1)
                    if k >= 1:
                        add(k - 1)
                add(KC - 1)

            def ffn(base, i, n_it, last=False):
                ii = i + n_it
                piece = [Piece(base + j, i, FF_PIECES) for j in range(2 * FF_PIECES)]

                def hidden(j):
                    dve.wait_ge(fullB, 6 * ii + j + 1)
                    for t in range(NT):
                        c = slice(t * TT, (t + 1) * TT)
                        dve.wait_ge(silu_done, 6 * ii + 3 * j + t + 1)
                        dve.tensor_tensor(tmp[:, j, c], psB[:, t, 0:TT], tmp[:, j, c], ALU.mult).then_inc(h_done, 1)
                    for t in range(NT):
                        c = slice(t * TT, (t + 1) * TT)
                        dve.wait_ge(hh_done, 6 * ii + 3 * j + t + 1)
                        dve.tensor_tensor(hl[:, j, c], tmp[:, j, c], hh[:, j, c].bitcast(F32), ALU.subtract).then_inc(hl_done, 1)

                split_lo(piece[3])
                hidden(0)
                split_lo(piece[4])
                split_lo(piece[5])
                hidden(1)
                if not last:
                    split_lo(piece[6])
                for d in range(KC):
                    ps, full = ((psA, fullA), (psB, fullB))[d % 2]
                    dve.wait_ge(full, 6 * ii + 2 + d // 2 + 1)
                    dve.wait_ge(y_done, 8 * ii + d + 1)
                    if d == 0:
                        dve.wait_ge(y_zero, 1 if n_it == 0 else 2)
                    dve.tensor_tensor(tiles3(y[:, d, :]), bank3(ps), tiles3(y[:, d, :]), ALU.add).then_inc(y_done, 1)
                if not last:
                    split_lo(piece[7])
                    split_lo(piece[8])

            dve.wait_ge(const_in, 32)
            dve.tensor_copy(tri[:], cst[:, 2:4, :]).then_inc(setup_v, 1)
            for g in (G_FF1_POST, G_FF2_POST):
                dve.tensor_scalar(gains[:, KC * g:KC * g + KC], gains[:, KC * g:KC * g + KC], 0.5, None, ALU.mult).then_inc(setup_v, 1)
            dve.tensor_scalar(gains[:, G_SUBLN:G_SUBLN + 1], gains[:, G_SUBLN:G_SUBLN + 1], 1.0 - LAM_INIT, None,
                              ALU.mult).then_inc(setup_v, 1)
            dve.wait_ge(setup_v, 4)
            for n in range(RING):
                split_lo(Piece(n))
            dve.wait_ge(lam_in, 16)
            dve.tensor_tensor(lamp[:], lamv[:, 0:2], lamv[:, 2:4], ALU.mult).then_inc(lam_prod, 1)
            x_split(0, G_FF1_PRE, 0)
            with dve.Fori(0, FF_ITERS) as i:
                ffn(PIECE_FF1, i, 0)
            post(1, G_FF1_POST, T_POST_FF1, 0)
            x_split(2, G_MIX_PRE, KC)
            dve.wait_ge(lam_exp, 1)
            dve.scalar_tensor_tensor(neglam[:], lame[:, 1:2], LAM_INIT, lame[:, 0:1], ALU.subtract, ALU.subtract).then_inc(lam_half, 1)

            def qk_low(unit, part, pair=True):
                dve.wait_ge(qk_hi, NQK * unit + part + 1)

                def low(o, src, hi):
                    return dve.tensor_tensor(o, src, hi.bitcast(F32), ALU.subtract)

                if part == Q_PROMPT:
                    last = low(ql[:, 0:SEQ], qkv[:, 0, 0:SEQ], qh[:, 0:SEQ])
                elif part == K_PROMPT:
                    last = low(kl[:, 0:SEQ], qkv[:, 1, 0:SEQ], kh[:, 0:SEQ])
                elif part == Q_SAMPLE and pair:
                    for h in range(2):
                        last = low(sample_q(qsl, h), qkv[HD * h:HD * h + HD, 0, SEQ:T], sample_q(qsh, h))
                elif part == Q_SAMPLE:
                    last = low(ql[:, SEQ:TP], qkv[:, 0, SEQ:TP], qh[:, SEQ:TP])
                elif part == K_SAMPLE:
                    last = low(kl[:, SEQ:TP], qkv[:, 1, SEQ:TP], kh[:, SEQ:TP])
                else:
                    last = low(kl[:, TP:KCOLS], kvc[:, 0, :], kh[:, TP:KCOLS])
                last.then_inc(qk_lo, 1)

            def v_low(unit, part, v_out, bank=None):
                dve.wait_ge(v_hi, NV * unit + part + 1)
                b, n, src = v_part(part, bank)
                dve.tensor_tensor(v_out(vl, b, n), v_in(v_out, src, n), v_out(vh, b, n).bitcast(F32),
                                  ALU.subtract).then_inc(v_lo, 1)

            def sb_unit(unit, mode):
                def masked(unit, n, first, out, table, op, whole, ready):
                    s = STEPS[n]
                    if not s["diag"]:
                        first.then_inc(ready, 1)
                        return
                    first.then_inc(whole, 1)
                    dve.wait_ge(whole, NMASKED * unit + MASKED[n] + 1)
                    heads = 1 if s["h"] is not None else 2
                    w = P if heads == 1 else DEC_SEQ
                    for x in range(heads):
                        last = dve.tensor_tensor(out[:, x * w:(x + 1) * w], out[:, x * w:(x + 1) * w], table[:, 0:w], op)
                    last.then_inc(ready, 1)

                def scores_out(unit, n):
                    dve.wait_ge(z_full, NSTEP * unit + n + 1)
                    if ZS <= n < NBIG:
                        dve.wait_ge(wtl_ready, NSTEP * unit + n - ZS + 1)
                    dve.tensor_copy(zs_of(n), Z[n % 2][:, 0:STEPS[n]["w"]]).then_inc(zs_ready, 1)

                def softplus(unit, n):
                    dve.wait_ge(l_ready, NSTEP * unit + n + 1)
                    masked(unit, n, dve.tensor_tensor(u_of(n), zs_of(n), u_of(n), ALU.max), u_of(n), m01, ALU.mult,
                           sp_whole, sp_ready)

                def argument(unit, n):
                    s = STEPS[n]
                    dve.wait_ge(s_full, NSTEP * unit + n + 1)
                    masked(unit, n, dve.tensor_tensor(zs_of(n), zs_of(n), S[s["bank"]][:, s["off"]:s["off"] + s["w"]],
                                                      ALU.subtract), zs_of(n), mneg, ALU.min, arg_whole, arg_ready)

                def sp_lo(unit, n):
                    dve.wait_ge(sph_ready, NSTEP * unit + n + 1)
                    dve.tensor_tensor(spl_of(n), u_of(n), sph_of(n).bitcast(F32), ALU.subtract).then_inc(spl_ready, 1)

                def weight_lo(unit, n):
                    dve.wait_ge(wth_ready, NSTEP * unit + n + 1)
                    dve.tensor_tensor(wtl_of(n), zs_of(n), wth_of(n).bitcast(F32), ALU.subtract).then_inc(wtl_ready, 1)

                def output(unit, n):
                    s = STEPS[n]
                    if s["last"] and s["h"] != 0:
                        dve.wait_ge(av_done, NSTEP * unit + n + 1)
                        w = 512 if s["h"] is not None else DEC_SEQ
                        dve.tensor_copy(y[:, bass.ds(unit, 1), s["g"] * 512:s["g"] * 512 + w],
                                        O[:, 0:w].rearrange("p (o c) -> p o c", o=1)).then_inc(o_done, 1)

                for tick in ticks(mode):
                    for lag, work in ((2, softplus), (3, argument), (0, scores_out), (2, sp_lo), (4, weight_lo)):
                        for a in stage(unit, mode, tick, lag):
                            work(*a)
                    if mode != TAIL:
                        if tick == 2:
                            v_low(unit, V_LOW, v_pair, VT)
                            split_lo(Piece(PIECE_IN + 5, unit, 3))
                        elif tick == 3:
                            qk_low(unit, Q_SAMPLE)
                        elif tick == 4:
                            v_low(unit, V_HIGH, v_pair, VT)
                        elif tick == 5:
                            qk_low(unit, K_SAMPLE)
                        elif tick == 6:
                            v_low(unit, V_SAMPLE, v_pair, VT)
                        elif tick == 8:
                            v_low(unit, V_CACHE, v_pair)
                        elif tick == 9:
                            qk_low(unit, K_CACHE)
                        elif tick == NBIG:
                            qk_low(unit + 1, Q_PROMPT)
                        elif tick == NBIG + 1:
                            qk_low(unit + 1, K_PROMPT)
                        if tick > 9 and tick % 9 == 1:
                            split_lo(Piece(PIECE_IN + 3 + tick // 9 - 1, unit + 1, 3))
                    for a in stage(unit, mode, tick, 5):
                        output(*a)

            def diff_unit(unit, head, filler):
                dve.wait_ge(dist_in, 16)
                dve.wait_ge(qk_lo, NQK * unit + K_PROMPT + 1)
                dve.tensor_scalar(dist[:], dist[:], 0.25, None, ALU.mult).then_inc(dist_ready, 1)
                dve.wait_ge(dist_ready, head + 1)

                def biased(t):
                    s = t["i"] % 2
                    if t["i"] >= 2:
                        dve.wait_ge(dw_ready, NTILE * head + t["i"] - 1)
                    for m in range(2):
                        dve.wait_ge(ds_full, 2 * NTILE * head + 2 * t["i"] + m + 1)
                        dve.sem_inc(held, 1)
                        dve.tensor_tensor_reduce(maps[:, s, m, 0:t["nk"]],
                                                 DS[m].rearrange("p a b -> p (a b)")[:, 0:t["nk"]],
                                                 dist[:, t["t0"]:t["t0"] + t["nk"]], 1.0, -3.0e38, ALU.add, ALU.max,
                                                 mx[:, s, m:m + 1]).then_inc(ds_read, 1)
                    dve.wait_ge(ds_read, 2 * NTILE * head + 2 * t["i"] + 2)
                    dve.tensor_scalar(nm[:, s, :], mx[:, s, :], -1.0, None, ALU.mult).then_inc(nm_ready, 1)

                def turned_lo(t, g, gn):
                    w = P * len(t["groups"][g])
                    dve.wait_ge(dwh_ready, NGRP * head + gn + 1)
                    dve.tensor_tensor(dwl[:, gn % 2, 0:w], DT[:, 0:w], dwh[:, gn % 2, 0:w].bitcast(F32),
                                      ALU.subtract).then_inc(dwl_ready, 1)

                def weights(t):
                    s, i = t["i"] % 2, t["i"]
                    dve.wait_ge(de_done, 2 * NTILE * head + 2 * i + 2)
                    dve.reciprocal(rl[:, s, :], ls[:, s, :]).then_inc(rl_ready, 1)
                    dve.wait_ge(rl_ready, NTILE * head + i + 1)
                    dve.tensor_tensor(c2[:, s, :], rl[:, s, 1:2], neglam[:], ALU.mult).then_inc(c2_ready, 1)
                    dve.wait_ge(c2_ready, NTILE * head + i + 1)
                    dve.tensor_scalar(maps[:, s, 1, 0:t["nk"]], maps[:, s, 1, 0:t["nk"]], c2[:, s, :], None,
                                      ALU.mult).then_inc(e2_ready, 1)
                    dve.wait_ge(e2_ready, NTILE * head + i + 1)
                    dve.scalar_tensor_tensor(maps[:, s, 0, 0:t["nk"]], maps[:, s, 0, 0:t["nk"]], rl[:, s, 0:1],
                                             maps[:, s, 1, 0:t["nk"]], ALU.mult, ALU.add).then_inc(dw_ready, 1)

                def output(t, gn):
                    dve.wait_ge(dav_done, NGRP * head + gn)
                    if t["i"] == 0 and not filler:
                        dve.wait_ge(qk_lo, NQK * unit + K_CACHE + 1)
                    dve.tensor_copy(y[:, bass.ds(unit, 1), t["q0"]:t["q0"] + t["nq"]],
                                    DO[:, (t["i"] % 2) * P:(t["i"] % 2) * P + t["nq"]].rearrange("p (o c) -> p o c", o=1)
                                    ).then_inc(do_done, 1)

                gn = 0
                for tick in range(NTILE + 2):
                    if tick == NTILE and filler:
                        qk_low(unit + 1, Q_PROMPT)
                        qk_low(unit + 1, K_PROMPT)
                    if tick >= 2:
                        output(TILES[tick - 2], gn)
                    if tick < NTILE:
                        biased(TILES[tick])
                    if tick == 0:
                        v_low(unit, V_LOW, v_one, VT)
                        v_low(unit, V_HIGH, v_one, DT)
                        v_low(unit, V_SAMPLE, v_one, DVT)
                    if 1 <= tick <= NTILE:
                        t = TILES[tick - 1]
                        for g in range(len(t["groups"])):
                            turned_lo(t, g, gn)
                            gn += 1
                    if tick < NTILE:
                        weights(TILES[tick])
                    if tick == 0:
                        split_lo(Piece(PIECE_IN + 5, unit, 3))
                        qk_low(unit, Q_SAMPLE, pair=False)
                    elif tick == 1:
                        qk_low(unit, K_SAMPLE)
                        v_low(unit, V_CACHE, v_one)
                        qk_low(unit, K_CACHE)
                    if filler and 0 < tick < NTILE and tick % 3 == 0:
                        split_lo(Piece(PIECE_IN + 3 + tick // 3 - 1, unit + 1, 3))

            dve.wait_ge(lam_half, 1)
            for j in range(2):
                split_lo(Piece(PIECE_IN + 3 + j))
                qk_low(0, j)
            sb_unit(0, FIRST)
            with dve.Fori(1, SB_UNITS) as i:
                sb_unit(i, MIDDLE)
            sb_unit(SB_UNITS, TAIL)
            with dve.Fori(0, DIFF_UNITS - 1) as i:
                diff_unit(i + SB_UNITS, i, True)
            diff_unit(UNITS - 1, DIFF_UNITS - 1, False)
            for d in range(SB_UNITS):
                dve.wait_ge(xh_ready, 2 * KC + d + 1)
                dve.tensor_tensor(xl[:, d, :], y[:, d, :], xh[:, d, :].bitcast(F32), ALU.subtract).then_inc(x_ready, 1)
            for e in range(DIFF_UNITS):
                d = SB_UNITS + e
                dve.wait_ge(sub_rstd, e + 1)
                if e >= 2:
                    dve.wait_ge(x_ready, 2 * KC + d - 1)
                dve.scalar_tensor_tensor(tmp[:, e % 2, :], y[:, d, :], gains[:, G_SUBLN:G_SUBLN + 1], rstd[:],
                                         ALU.mult, ALU.mult).then_inc(t_ready, 1)
                dve.wait_ge(xh_ready, 2 * KC + d + 1)
                dve.tensor_tensor(xl[:, d, :], tmp[:, e % 2, :], xh[:, d, :].bitcast(F32), ALU.subtract).then_inc(x_ready, 1)
            for d in range(KC):
                dve.wait_ge(wo_full, d + 1)
                dve.tensor_copy(tiles3(y[:, d, :]), bank3((psA, psB)[d % 2])).then_inc(wo_out, 1)
                split_lo(Piece(PIECE_OUT + 3 + d))
            dve.wait_ge(resid_in, 16 * KC)
            post(3, G_MIX_POST, T_POST_MIX, KC)
            x_split(4, G_FF2_PRE, 3 * KC)
            with dve.Fori(0, FF_ITERS - 1) as i:
                ffn(PIECE_FF2, i, FF_ITERS)
            ffn(PIECE_FF2, FF_ITERS - 1, FF_ITERS, last=True)
            post(5, G_FF2_POST, T_POST_FF2, 2 * KC)
            dve.wait_ge(rstd_ready, 7)
            for k in range(KC):
                dve.scalar_tensor_tensor(y[:, k, :], resid[:, k, :], gains[:, KC * G_FINAL + k:KC * G_FINAL + k + 1],
                                         rstd[:], ALU.mult, ALU.mult).then_inc(t_ready, 1)

        @block.gpsimd
        def _(pool):
            pool.memset(y[:], 0.0).then_inc(y_zero, 1)
            pool.wait_ge(spilled, 16 * KC)
            pool.memset(qkv[:, :, T:TP], 0.0).then_inc(zeroed, 1)
            for v in (vh, vl):
                gap = v[:, :].bitcast(F32).rearrange("p (b x d) -> p b x d", x=3, d=HD)[:, :, 1, :]
                pool.memset(gap, 0.0).then_inc(zeroed, 1)

            pool.wait_ge(setup_v, 4)
            for q in (qsh, qsl):
                pool.memset(q[:].bitcast(F32), 0.0).then_inc(zeroed, 1)

            def sb_unit(unit):
                for n in range(NSTEP):
                    pool.wait_ge(zs_ready, NSTEP * unit + n + 1)
                    pool.sem_inc(held, 1)
                    pool.tensor_scalar(u_of(n), zs_of(n), U_CLAMP, -3.0e38, ALU.min, ALU.max).then_inc(u_ready, 1)

            with pool.Fori(0, SB_UNITS) as i:
                sb_unit(i)
            pool.wait_ge(t_ready, T_POST_MIX + KC)
            pool.memset(y[:], 0.0).then_inc(y_zero, 1)


def consts():
    i = np.arange(P)
    k, q = i[:, None], i[None, :]
    before = k < q
    c = np.stack([k == q, np.ones((P, P)), k >= q, k < q, before, before], axis=1).astype(np.float32)
    c[:, 5, :] = np.where(before, 3.0e38, -1.0e30)
    huge = -1.0e30
    dist = np.zeros((P, KCOLS), np.float32)
    x = np.arange(SEQ)[None, :] - (SEQ - P)
    dist[:, :SEQ] = np.where(x // HD <= k // HD, -np.abs(k - x), huge)
    dist[:, SEQ:TP] = np.where(q < DEC_SEQ, -np.abs(k - q), huge)
    dist[:, TP:] = -(PAST + k - np.arange(PAST)[None, :])
    return c.reshape(P, 6 * P), dist


def kernel(**inputs):
    import concourse.bacc as bacc
    from concourse.bass_utils import run_bass_kernel_spmd

    a = {n: np.asarray(v) for n, v in inputs.items()}
    f32 = np.float32

    def in_pieces(w):
        return w.reshape(KC, P, -1, P).transpose(2, 1, 0, 3).reshape(-1, P, KC * P)

    c, dist = consts()
    w_in = in_pieces(a["w_in"][0])
    n_sb, n_d = SB_UNITS, DIFF_UNITS
    order = [j * n_sb + n for n in range(n_sb) for j in range(3)]
    order += [3 * n_sb + j * n_d + n for n in range(n_d) for j in range(3)]
    names = ["ff1_pre_g", "ff1_post_g", "mix_pre_g", "mix_post_g", "ff2_pre_g", "ff2_post_g", "final_g"]
    kc = np.concatenate([a["cache_sb_k"][0, 0].reshape(PAST, -1), a["cache_diff_k"][0, 0].reshape(PAST, -1)], axis=1)
    vc = np.concatenate([a["cache_sb_v"][0, 0].reshape(PAST, -1), a["cache_diff_v"][0, 0].reshape(PAST, -1)], axis=1)
    arrays = {
        "xT": np.concatenate([a["x_prompt"][0], a["x_sample"][0]]).T.reshape(KC, P, T),
        "wg1": in_pieces(a["ff1_w_gate"][0]),
        "wu1": in_pieces(a["ff1_w_up"][0]),
        "wd1": a["ff1_w_down"][0].reshape(-1, P, D_MODEL),
        "w_mix": np.concatenate([w_in[order], in_pieces(a["w_out"][0])]),
        "wg2": in_pieces(a["ff2_w_gate"][0]),
        "wu2": in_pieces(a["ff2_w_up"][0]),
        "wd2": a["ff2_w_down"][0].reshape(-1, P, D_MODEL),
        "k_cache": kc.T.reshape(UNITS, P, PAST),
        "v_cache": vc.reshape(PAST // P, P, UNITS, P).transpose(2, 1, 0, 3).reshape(UNITS, P, PAST),
        "gains": np.concatenate([a[n][0].reshape(KC, P).T for n in names] + [a["subln_g"][0].reshape(P, 1)], axis=1),
        "lam": np.stack([a[n][0] for n in ("lam_q1", "lam_q2", "lam_k1", "lam_k2")], axis=1),
        "consts": c,
        "dist_table": dist,
    }
    outs = {"yT": (KC, P, T), "kv": (2 * UNITS, P, T)}

    nc = bacc.Bacc("TRN2", target_bir_lowering=False, num_devices=1, dynamic_dma_scratch_size=1024)
    arrays = {f"in_{n}": np.ascontiguousarray(v) for n, v in arrays.items()}
    args = [nc.dram_tensor(n, v.shape, mybir.dt.from_np(v.dtype), kind="ExternalInput").ap() for n, v in arrays.items()]
    args += [nc.dram_tensor(f"out_{n}", s, F32, kind="ExternalOutput").ap() for n, s in outs.items()]
    build(nc, *args)
    r = run_bass_kernel_spmd(nc, [arrays], core_ids=[0]).results[0]

    yt = r["out_yT"].reshape(D_MODEL, T).T
    kv = r["out_kv"].reshape(UNITS, 2, P, T)

    def rows(units, which, tokens, heads, width):
        t = kv[units, which].reshape(-1, T).T[tokens]
        return np.ascontiguousarray(t).reshape(1, 1, -1, heads, width)

    sb, df = slice(0, SB_UNITS), slice(SB_UNITS, UNITS)
    out = [np.ascontiguousarray(yt[:SEQ])[None], np.ascontiguousarray(yt[SEQ:])[None]]
    for tokens in (slice(0, SEQ), slice(SEQ, T)):
        out += [rows(sb, 0, tokens, HEADS_SB, HD), rows(sb, 1, tokens, HEADS_SB, HD),
                rows(df, 0, tokens, HEADS_DIFF, 2 * HD), rows(df, 1, tokens, HEADS_DIFF, 2 * HD)]
    return tuple(out)
```

```python
import math
from contextlib import ExitStack

import numpy as np

import concourse.bass as bass
from concourse import mybir

P = 128
D_MODEL, SEQ, DEC_SEQ, PAST = 1024, 1024, 32, 256
D_FF = 2816
HEADS_SB, HEADS_DIFF, HD = 8, 4, 64
EPS = 1e-6
LAM_INIT = 0.8 - 0.6 * math.exp(-0.3 * 0)

T = SEQ + DEC_SEQ
NT, TT = 3, T // 3
KC = D_MODEL // P
FF_ITERS = D_FF // P // 2
FF_PIECES = 6
SB_UNITS = HEADS_SB * HD // P
DIFF_UNITS = HEADS_DIFF
UNITS = SB_UNITS + DIFF_UNITS
RING = 3
TP = SEQ + P
KCOLS = TP + PAST
KBLK = KCOLS // P
VW = 192
U_CLAMP = 30.0

F32, F32R = mybir.dt.float32, mybir.dt.float32r
ALU, ACT = mybir.AluOpType, mybir.ActivationFunctionType

PIECE_FF1 = 0
PIECE_IN = PIECE_FF1 + FF_PIECES * FF_ITERS
PIECE_OUT = PIECE_IN + 3 * UNITS
PIECE_FF2 = PIECE_OUT + KC

G_FF1_PRE, G_FF1_POST, G_MIX_PRE, G_MIX_POST, G_FF2_PRE, G_FF2_POST, G_FINAL = range(7)
G_SUBLN = 7 * KC


def sb_steps():
    steps = []
    for g in range(SEQ // 512):
        for kb in range(4 * g + 3, -1, -1):
            for h in range(2):
                c0 = max(kb * P, g * 512)
                steps.append(dict(g=g, h=h, kb=kb, c0=c0, w=(g + 1) * 512 - c0, off=c0 - g * 512,
                                  diag=kb >= 4 * g, first=kb == 4 * g + 3, last=kb == 0, bank=h))
    for kb in (8, 10, 9):
        steps.append(dict(g=SEQ // 512, h=None, kb=kb, c0=SEQ, w=2 * DEC_SEQ, off=0, diag=kb == 8,
                          first=kb == 8, last=kb == 9, bank=0))
    return steps


def diff_tiles():
    order = list(range(1, SEQ // P, 2)) + list(range(SEQ // P - 2, -1, -2))
    tiles = []
    for i in order:
        nk = (i + 1) * P
        tiles.append(dict(q0=i * P, nq=P, k0=0, nk=nk, t0=SEQ - nk))
    tiles.append(dict(q0=SEQ, nq=DEC_SEQ, k0=SEQ, nk=KCOLS - SEQ, t0=SEQ))
    for n, t in enumerate(tiles):
        t["i"] = n
        blocks = list(range(t["nk"] // P))
        t["groups"] = [blocks[b:b + 4] for b in range(0, len(blocks), 4)]
    return tiles


STEPS = sb_steps()
NSTEP = len(STEPS)
ZS, US = 5, 3
NBIG = sum(s["h"] is not None for s in STEPS)
NMASKED = sum(s["diag"] for s in STEPS)
MASKED = [sum(s["diag"] for s in STEPS[:n]) for n in range(NSTEP)]
NCARRY = sum(not s["last"] for s in STEPS)
CARRIES = [sum(not s["last"] for s in STEPS[:n]) for n in range(NSTEP)]
LAG = 5
FIRST, MIDDLE, TAIL = range(3)


def stage(unit, mode, tick, lag):
    back = tick < lag
    if (back and mode == FIRST) or (not back and mode == TAIL):
        return []
    return [(unit - 1 if back else unit, (tick - lag) % NSTEP)]


def ticks(mode):
    return range(LAG if mode == TAIL else NSTEP)


NQK, NV, NVT = 5, 4, 3
Q_PROMPT, K_PROMPT, Q_SAMPLE, K_SAMPLE, K_CACHE = range(NQK)
V_LOW, V_HIGH, V_SAMPLE, V_CACHE = range(NV)


TILES = diff_tiles()
NTILE = len(TILES)
NGRP = sum(len(t["groups"]) for t in TILES)

FINAL_DVE = 5
STORE_ORDER = [0, 1, FINAL_DVE, 2, 3, FINAL_DVE + 1, 4, FINAL_DVE + 2]

EARLY = 2
EARLY_TICK = 4
OUT_ORDER = [0, EARLY, 1] + list(range(EARLY + 1, KC))
SUB_TILES = NT * (DIFF_UNITS - 1)

SUMMED = KC - 2

POST_DVE = 2


def v_pair(t, b, n):
    return t.rearrange("p (b x d) -> p b x d", x=3, d=HD)[:, b:b + n, 0:3:2, :]


def v_one(t, b, n):
    return t[:, b * P:(b + n) * P]


def sample_q(t, h):
    return t[HD * h:HD * h + HD, DEC_SEQ * h:DEC_SEQ * h + DEC_SEQ]


def v_in(layout, src, n):
    return src.rearrange("p (b x d) -> p b x d", x=2, d=HD) if layout is v_pair else src


def build(nc, xT, wg1, wu1, wd1, w_mix, wg2, wu2, wd2, k_cache, v_cache, gains_d, lam_d, consts_d, dist_d,
          yT_out, kv_out):
    ctx = ExitStack()
    with ctx:
        where = [1152]

        def at(name, shape, dt, offset=None):
            size = 4 * int(np.prod(shape[1:]))
            if offset is None:
                offset = where[0]
                where[0] += -(-size // 32) * 32
            return nc.alloc_sbuf_tensor_at(name, shape, dt, offset=offset)

        xh = at("xh", [P, KC, T], F32R)
        xl = at("xl", [P, KC, T], F32R)
        roots, squares = (at(n, [P, DIFF_UNITS, T], F32, 1152 + 4 * T * (SB_UNITS + c)) for n, c in (("roots", 0), ("squares", KC)))
        y_at = where[0]
        y = at("y", [P, KC, T], F32)
        raw = at("raw", [P, RING, KC, P], F32)
        wh = at("wh", [P, RING, KC, P], F32R)
        wl = at("wl", [P, RING, KC, P], F32R)
        cst = at("cst", [P, 6, P], F32)
        tri_in = where[0] - 4 * 4 * P
        qsh = at("qsh", [P, 2 * DEC_SEQ], F32R, tri_in)
        qsl = at("qsl", [P, 2 * DEC_SEQ], F32R, tri_in + 8 * DEC_SEQ)
        tri = at("tri", [P, 2, P], F32R)
        gains = at("gains", [P, 7 * KC + 1], F32)
        lamv = at("lamv", [HD, 4], F32)
        lamp = at("lamp", [HD, 2], F32)
        lame = at("lame", [P, 2], F32)
        neglam = at("neglam", [P, 1], F32)
        mx = at("mx", [P, 2, 2], F32)
        nm = at("nm", [P, 2, 2], F32)
        ls = at("ls", [P, 2, 2], F32)
        rl = at("rl", [P, 2, 2], F32)
        c2 = at("c2", [P, 2, 1], F32)
        ident, ones, m01, mneg = cst[:, 0, :], cst[:, 1, :], cst[:, 4, :], cst[:, 5, :]
        shared = where[0]

        resid = at("resid", [P, KC, T], F32)
        rstd = at("rstd", [P, T], F32)
        sq = at("sq", [P, 2, T], F32)
        tmp = at("tmp", [P, 2, T], F32)
        hh = at("hh", [P, 2, T], F32R)
        hl = at("hl", [P, 2, T], F32R)

        where[0] = shared
        kh = at("kh", [P, KCOLS], F32R)
        kl = at("kl", [P, KCOLS], F32R)
        qh = at("qh", [P, TP], F32R)
        ql = at("ql", [P, TP], F32R)
        vh = at("vh", [P, KBLK * VW], F32R)
        v_raw = at("v_raw", [P, KBLK * VW], F32, where[0])
        vl = at("vl", [P, KBLK * VW], F32R)
        qkv = at("qkv", [P, 3, TP], F32)
        kc = at("kc", [P, PAST], F32)
        mix_rstd = at("mix_rstd", [P, T], F32, y_at + 4 * (KC - 1) * T)
        temps = where[0]
        zs = at("zs", [P, ZS, 512], F32)
        u = at("u", [P, US, 512], F32)
        sph = at("sph", [P, 2, 512], F32R)
        spl = at("spl", [P, 2, 512], F32R)
        wth = at("wth", [P, 2, 512], F32R)
        wtl = at("wtl", [P, 2, 512], F32R)
        small = 4 * 2 * DEC_SEQ
        small_at = y_at + 4 * (KC - 3) * T

        def with_small(big, slots, index, dt):
            little = at(f"small{index}", [P, NSTEP - NBIG, 2 * DEC_SEQ], dt, small_at + (NSTEP - NBIG) * small * index)
            return lambda n: (big[:, n % slots, 0:STEPS[n]["w"]] if n < NBIG else little[:, n - NBIG, :])

        zs_of = with_small(zs, ZS, 0, F32)
        u_of = with_small(u, US, 1, F32)
        sph_of, spl_of = with_small(sph, 2, 2, F32R), with_small(spl, 2, 3, F32R)
        wth_of, wtl_of = with_small(wth, 2, 4, F32R), with_small(wtl, 2, 5, F32R)
        where[0] = temps
        maps = at("maps", [P, 2, 2, SEQ], F32)
        dist = at("dist", [P, SEQ + KCOLS - SEQ], F32)
        dwh = at("dwh", [P, 2, 512], F32R)
        dwl = at("dwl", [P, 2, 512], F32R)

        resid_dram = nc.dram_tensor("resid_scratch", [KC, P, T], F32).ap()

        psA = ctx.enter_context(nc.psum_tensor("psA", [P, 3, 512], F32))
        psB = ctx.enter_context(nc.psum_tensor("psB", [P, 3, 512], F32))
        psC = ctx.enter_context(nc.psum_tensor("psC", [P, 2, 512], F32))
        Z = [psA[:, 2, :], psB[:, 0, :]]
        S = [psB[:, 1, :], psB[:, 2, :]]
        O = psC[:, 0, :]
        spare = psB[:, 0, 512 - DEC_SEQ:512]
        VT = psC[:, 1, :]
        DS = [psB[:, 0:2, :], psC[:, 0:2, :]]
        DT, DO = psA[:, 2, :], psB[:, 2, :]
        DVT = psB[:, 1, 0:P]

        def sem(name):
            return ctx.enter_context(nc.semaphore(name))

        const_in, lam_in = sem("const_in"), sem("lam_in")
        x_in = [sem(f"x_in{k}") for k in range(KC)]
        raw_in = [sem(f"raw_in{s}") for s in range(RING)]
        cache_in, cache_v_in, dist_in, resid_in = sem("cache_in"), sem("cache_v_in"), sem("dist_in"), sem("resid_in")
        spilled, kv_stored, y_stored = sem("spilled"), sem("kv_stored"), sem("y_stored")
        w_hi, w_ready = sem("w_hi"), sem("w_ready")
        setup_v, lam_prod, lam_sum, lam_exp, lam_half = (
            sem("setup_v"), sem("lam_prod"), sem("lam_sum"), sem("lam_exp"), sem("lam_half"))
        zeroed, y_zero = sem("zeroed"), sem("y_zero")
        sq_ready, sums, ln_done, rstd_ready = sem("sq_ready"), sem("sums"), sem("ln_done"), sem("rstd_ready")
        xh_ready, x_ready, r_ready = sem("xh_ready"), sem("x_ready"), sem("r_ready")
        out_sq, out_sum, out_sums, scaled_v, scaled_p = (
            sem("out_sq"), sem("out_sum"), sem("out_sums"), sem("scaled_v"), sem("scaled_p"))
        sample_ln, gate_done, scaled_silu = sem("sample_ln"), sem("gate_done"), sem("scaled_silu")
        fullA, fullB, silu_done, h_done, hh_done, hl_done, y_done = (
            sem("fullA"), sem("fullB"), sem("silu_done"), sem("h_done"), sem("hh_done"), sem("hl_done"), sem("y_done"))
        proj_full, proj_raw, proj_out, vt_full, unit_done = (
            sem("proj_full"), sem("proj_raw"), sem("proj_out"), sem("vt_full"), sem("unit_done"))
        qk_hi, qk_lo, v_hi, v_lo = sem("qk_hi"), sem("qk_lo"), sem("v_hi"), sem("v_lo")
        z_full, zs_ready, u_ready, e_ready, l_ready, sp_whole, arg_whole, sp_ready, sph_ready, spl_ready = (
            sem("z_full"), sem("zs_ready"), sem("u_ready"), sem("e_ready"), sem("l_ready"), sem("sp_whole"),
            sem("arg_whole"),
            sem("sp_ready"), sem("sph_ready"), sem("spl_ready"))
        s_full, arg_ready, carried, wt_ready, wth_ready, wtl_ready, av_done, o_done = (
            sem("s_full"), sem("arg_ready"), sem("carried"), sem("wt_ready"), sem("wth_ready"), sem("wtl_ready"),
            sem("av_done"), sem("o_done"))
        dist_ready, ds_full, ds_read, nm_ready, de_done, rl_ready, c2_ready, e2_ready, dw_ready = (
            sem("dist_ready"), sem("ds_full"), sem("ds_read"), sem("nm_ready"), sem("de_done"), sem("rl_ready"),
            sem("c2_ready"), sem("e2_ready"), sem("dw_ready"))
        dt_full, dwh_ready, dwl_ready, dav_done, do_done = (
            sem("dt_full"), sem("dwh_ready"), sem("dwl_ready"), sem("dav_done"), sem("do_done"))
        final_g, final_v, final_p = sem("final_g"), sem("final_v"), sem("final_p")
        sub_sq, sub_sum, sub_ln, sub_rstd, sub_scaled = (
            sem("sub_sq"), sem("sub_sum"), sem("sub_ln"), sem("sub_rstd"), sem("sub_scaled"))
        early_full, early_out, wo_full, wo_out = (
            sem("early_full"), sem("early_out"), sem("wo_full"), sem("wo_out"))
        held = sem("held")

        block = ctx.enter_context(nc.Block())

        def v_part(part, v_out, bank):
            if part == V_CACHE:
                return SEQ // P + 1, 2, v_out(v_raw, SEQ // P + 1, 2)
            n = 1 if part == V_SAMPLE else 4
            return 4 * part, n, v_in(v_out, bank[:, 0:n * P], n)

        def sub_squares(e):
            return squares[:, e, :]

        def sub_rstd_of(e):
            return roots[:, e, :]

        def sub_bank(m):
            return psA[:, m % 2, 0:TT] if m < SUB_TILES else (psC[:, 0, 0:TT], psC[:, 1, 0:TT], psA[:, 2, 0:TT])[m - SUB_TILES]

        def tile(t):
            return slice(t * TT, (t + 1) * TT)

        def bank3(ps):
            return ps[:, :, 0:TT]

        def tiles3(ap):
            return ap.rearrange("p (t c) -> p t c", t=NT)

        class Piece:
            def __init__(self, n, i=0, per=0):
                self.slot = n % RING
                self.landed = 16 * (n // RING + 1) + (16 * (per // RING)) * i
                self.count = n + 1 + per * i

        @block.sync
        def _(sp):
            def load_piece(src, piece, n_static=None):
                if n_static is None or n_static >= RING:
                    sp.wait_ge(w_ready, piece.count - RING)
                sp.dma_start(raw[:, piece.slot, :, :].rearrange("p k c -> p (k c)"), src).then_inc(raw_in[piece.slot], 16)

            def ff_sources(gate, up, down, i):
                for j in range(2):
                    yield gate, 2 * i + j
                    yield up, 2 * i + j
                for j in range(2):
                    yield down, 2 * i + j

            def one(w, n):
                return w[bass.ds(n, 1), :, :].rearrange("o p c -> (o p) c")

            sp.dma_start(cst[:].rearrange("p a b -> p (a b)"), consts_d).then_inc(const_in, 16)
            sp.dma_start(gains[:], gains_d).then_inc(const_in, 16)
            sp.dma_start(lamv[:], lam_d).then_inc(lam_in, 16)
            for j, (w, n) in enumerate(ff_sources(wg1, wu1, wd1, 0)):
                load_piece(w[n, :, :], Piece(PIECE_FF1 + j), j)
                if j == 0:
                    for k in range(KC):
                        sp.dma_start(resid[:, k, :], xT[k, :, :]).then_inc(x_in[k], 16)
            with sp.Fori(1, FF_ITERS) as i:
                for j, (w, n) in enumerate(ff_sources(wg1, wu1, wd1, i)):
                    load_piece(one(w, n), Piece(PIECE_FF1 + j, i, FF_PIECES))
            for j in range(3):
                load_piece(w_mix[j, :, :], Piece(PIECE_IN + j))
            for k in range(KC):
                sp.wait_ge(r_ready, k + 1)
                sp.dma_start(resid_dram[k, :, :], resid[:, k, :]).then_inc(spilled, 16)
            for j in range(3, 6):
                load_piece(w_mix[j, :, :], Piece(PIECE_IN + j))
            sp.wait_ge(spilled, 16 * KC)

            def load_keys(unit):
                sp.dma_start(kc[:], one(k_cache, unit)).then_inc(cache_in, 16)

            def unit_dmas(unit, v_out, last=False):
                for j in range(2):
                    load_piece(one(w_mix, 3 * unit + 6 + j), Piece(PIECE_IN + 6 + j, unit, 3))
                sp.wait_ge(proj_out, 9 * unit + 9)
                for j in range(2):
                    sp.dma_start(kv_out[bass.ds(2 * unit + j, 1), :, :].rearrange("o p c -> (o p) c"),
                                 qkv[:, 1 + j, 0:T]).then_inc(kv_stored, 16)
                sp.wait_ge(v_hi, NV * unit + V_SAMPLE + 1)
                for b in range(PAST // P):
                    sp.dma_start(v_out(v_raw, SEQ // P + 1 + b, 1),
                                 v_in(v_out, one(v_cache, unit)[:, b * P:(b + 1) * P], 1)).then_inc(cache_v_in, 16)
                load_piece(one(w_mix, 3 * unit + 8), Piece(PIECE_IN + 8, unit, 3))
                if not last:
                    sp.wait_ge(qk_lo, NQK * unit + K_CACHE + 1)
                    load_keys(unit + 1)

            load_keys(0)
            with sp.Fori(0, SB_UNITS) as i:
                unit_dmas(i, v_pair)
            sp.wait_ge(unit_done, 1)
            sp.dma_start(dist[:], dist_d).then_inc(dist_in, 16)
            with sp.Fori(SB_UNITS, UNITS - 1) as i:
                unit_dmas(i, v_one)
            unit_dmas(UNITS - 1, v_one, last=True)
            sp.wait_ge(unit_done, 1 + DIFF_UNITS)
            for k in range(KC):
                sp.dma_start(resid[:, k, :], resid_dram[k, :, :]).then_inc(resid_in, 16)
            for j in range(6, KC):
                load_piece(w_mix[3 * UNITS + j, :, :], Piece(PIECE_OUT + j))
            with sp.Fori(0, FF_ITERS) as i:
                for j, (w, n) in enumerate(ff_sources(wg2, wu2, wd2, i)):
                    load_piece(one(w, n), Piece(PIECE_FF2 + j, i, FF_PIECES))
            for k in STORE_ORDER:
                if k < FINAL_DVE:
                    sp.wait_ge(final_v, k + 1)
                else:
                    sp.wait_ge(final_p, k - FINAL_DVE + 1)
                sp.dma_start(yT_out[k, :, :], y[:, k, :]).then_inc(y_stored, 16)
            sp.wait_ge(y_stored, 16 * KC)
            sp.wait_ge(kv_stored, 32 * UNITS)

        def split3(pe, out, wa, wb, xa, xb, start, stop, group=True):
            pe.matmul(out, wa, xa, start=start, stop=False, skip_group_check=not group)
            pe.matmul(out, wa, xb, start=False, stop=False, skip_group_check=not group)
            return pe.matmul(out, wb, xa, start=False, stop=stop, skip_group_check=not group)

        @block.tensor
        def _(pe):
            def dense(ps, piece, rh, rl_):
                pe.wait_ge(w_ready, piece.count)
                for k in range(KC):
                    for wa, ra in ((wh, rh), (wh, rl_), (wl, rh)):
                        for t in range(NT):
                            last = pe.matmul(ps[:, t, 0:TT], wa[:, piece.slot, k, :], ra[:, k, t * TT:(t + 1) * TT],
                                             start=(k == 0 and wa is wh and ra is rh),
                                             stop=(k == KC - 1 and wa is wl))
                return last

            def ones_product(squares, start, stop):
                for t in range(NT):
                    last = pe.matmul(psA[:, t, 0:TT], ones, squares[:, tile(t)], start=start, stop=stop)
                return last

            def stats(norm):
                for k in range(KC):
                    pe.wait_ge(sq_ready, KC * (norm // 2) + k + 1)
                    ones_product(sq[:, k % 2, :], k == 0, k == KC - 1).then_inc(sums, 1)

            def out_stats(norm):
                n = norm // 2
                pe.wait_ge(out_sum, (SUMMED - 1) * (n + 1))
                ones_product(sq[:, 0, :], True, False)
                pe.wait_ge(out_sq, KC * n + KC - 1)
                ones_product(sq[:, 1, :], False, False)
                pe.wait_ge(out_sq, KC * n + KC)
                ones_product(tmp[:, 0, :], False, True).then_inc(out_sums, 1)

            def first_product(piece, norm, x_base):
                pe.wait_ge(w_ready, piece.count)
                for k in range(KC):
                    pe.wait_ge(sq_ready, KC * (norm // 2) + k + 1)
                    for out, c in ((psC[:, 0, :], slice(0, 512)), (psC[:, 1, :], slice(512, SEQ)), (spare, slice(SEQ, T))):
                        last = pe.matmul(out, ones, sq[:, k % 2, c], start=k == 0, stop=k == KC - 1)
                    last.then_inc(sums, 1)
                    pe.wait_ge(x_ready, x_base + k + 1)
                    for n, (wa, ra) in enumerate(((wh, xh), (wh, xl), (wl, xh))):
                        for t in range(NT):
                            last = pe.matmul(psA[:, t, 0:TT], wa[:, piece.slot, k, :], ra[:, k, tile(t)],
                                             start=(k, n) == (0, 0), stop=(k, n) == (KC - 1, 2))
                return last

            def ffn(base, i, n_it, norm=None, x_base=None):
                ii = i + n_it
                piece = [Piece(base + j, i, FF_PIECES) for j in range(FF_PIECES)]
                for j in range(2):
                    if j == 0:
                        pe.wait_ge(y_done, 8 * ii + 7)
                    else:
                        pe.wait_ge(gate_done, 6 * ii + 3)
                    if j == 0 and norm is not None:
                        first_product(piece[0], norm, x_base).then_inc(fullA, 1)
                        pe.wait_ge(sample_ln, norm // 2 + 1)
                    else:
                        dense(psA, piece[2 * j], xh, xl).then_inc(fullA, 1)
                    if j == 0:
                        pe.wait_ge(y_done, 8 * ii + 8)
                    else:
                        pe.wait_ge(h_done, 6 * ii + 3)
                    dense(psB, piece[2 * j + 1], xh, xl).then_inc(fullB, 1)
                for d in range(KC):
                    ps, full = ((psA, fullA), (psB, fullB))[d % 2]
                    if d == 0:
                        pe.wait_ge(gate_done, 6 * ii + 6)
                        pe.wait_ge(hl_done, 6 * ii + 3)
                        pe.wait_ge(w_ready, piece[5].count)
                    elif d == 1:
                        pe.wait_ge(h_done, 6 * ii + 6)
                    else:
                        pe.wait_ge(y_done, 8 * ii + 8 + d - 1)
                    for j in range(2):
                        for t in range(NT):
                            if d == 0 and j == 1:
                                pe.wait_ge(hl_done, 6 * ii + 3 + t + 1)
                            s = piece[4 + j].slot
                            c = slice(t * TT, (t + 1) * TT)
                            last = split3(pe, ps[:, t, 0:TT], wh[:, s, d, :], wl[:, s, d, :], hh[:, j, c], hl[:, j, c],
                                          start=j == 0, stop=j == 1)
                    last.then_inc(full, 1)

            def proj_part(unit, f, part, parts):
                piece = Piece(PIECE_IN + f // 3, unit, 3)
                bank = psA[:, f % 2, 0:TT]
                if part == 0:
                    if f % 3 == 0:
                        pe.wait_ge(w_ready, piece.count)
                    if f >= 2:
                        pe.wait_ge(proj_raw, 9 * unit + f - 1)
                    elif f == 0 and not (isinstance(unit, int) and unit == 0):
                        pe.wait_ge(proj_raw, 9 * unit)
                todo = [(k, n) for k in range(KC) for n in range(3)]
                for k, n in todo[part * len(todo) // parts:(part + 1) * len(todo) // parts]:
                    wa, xa = ((wh, xh), (wh, xl), (wl, xh))[n]
                    last = pe.matmul(bank, wa[:, piece.slot, k, :], xa[:, k, (f % 3) * TT:(f % 3 + 1) * TT],
                                     start=(k, n) == todo[0], stop=(k, n) == todo[-1])
                if part == parts - 1:
                    last.then_inc(proj_full, 1)

            def sub_sums(e, tiles=range(NT)):
                pe.wait_ge(sub_sq, e + 1)
                for t in tiles:
                    m = NT * e + t
                    if 2 <= m < SUB_TILES:
                        pe.wait_ge(sub_ln, m - 1)
                    pe.matmul(sub_bank(m), ones, sub_squares(e)[:, tile(t)], start=True, stop=True).then_inc(sub_sum, 1)

            def early_bank(w):
                return psA[:, (SUB_TILES + w) % 2, 0:TT]

            def out_products(bank, d, t, chunks, start, stop):
                slot = Piece(PIECE_OUT + d).slot
                for k in chunks:
                    for n, (wa, xa) in enumerate(((wh, xh), (wh, xl), (wl, xh))):
                        last = pe.matmul(bank, wa[:, slot, k, :], xa[:, k, tile(t)],
                                         start=start and (k, n) == (0, 0), stop=stop and (k, n) == (chunks[-1], 2))
                return last

            def last_head(bank, d, t):
                return split3(pe, bank, wh[:, Piece(PIECE_OUT + d).slot, KC - 1, :], wl[:, Piece(PIECE_OUT + d).slot, KC - 1, :],
                              xh[:, KC - 1, tile(t)], xl[:, KC - 1, tile(t)], True, True)

            def out_part(w, part, parts):
                n = KC - 1
                if w == 0:
                    pe.wait_ge(x_ready, 2 * KC + (part + 1) * n // parts)
                if part == 0:
                    pe.wait_ge(w_ready, Piece(PIECE_OUT + w // NT).count)
                    if w < 2:
                        pe.wait_ge(sub_ln, SUB_TILES + w - 1)
                    else:
                        pe.wait_ge(early_out, w - 1)
                last = out_products(early_bank(w), w // NT, w % NT, range(part * n // parts, (part + 1) * n // parts),
                                    part == 0, part == parts - 1)
                if part == parts - 1:
                    last.then_inc(early_full, 1)

            def turn_values(bank, unit, b0, n):
                for b in range(n):
                    last = pe.transpose(bank[:, b * P:(b + 1) * P], qkv[:, 2, (b0 + b) * P:(b0 + b + 1) * P], ident)
                last.then_inc(vt_full, 1)

            def sb_unit(unit, mode):
                def scores(unit, n):
                    s = STEPS[n]
                    if n >= 2:
                        pe.wait_ge(zs_ready, NSTEP * unit + n - 1)
                    elif n == 0 and mode != FIRST:
                        pe.wait_ge(zs_ready, NSTEP * unit)
                    if n == 0:
                        pe.wait_ge(qk_lo, NQK * unit + K_PROMPT + 1)
                    elif n == NBIG:
                        pe.wait_ge(qk_lo, NQK * unit + K_CACHE + 1)
                    kc = slice(s["kb"] * P, (s["kb"] + 1) * P)
                    out = Z[n % 2][:, 0:s["w"]]
                    if s["h"] is None:
                        last = split3(pe, out, kh[:, kc], kl[:, kc], qsh[:], qsl[:], start=True, stop=True)
                    else:
                        r = slice(HD * s["h"], HD * s["h"] + HD)
                        qc = slice(s["c0"], s["c0"] + s["w"])
                        last = split3(pe, out, kh[r, kc], kl[r, kc], qh[r, qc], ql[r, qc], start=True, stop=True)
                    last.then_inc(z_full, 1)

                def add_tri(n, which, start):
                    s = STEPS[n]
                    out = S[s["bank"]][:, s["off"]:s["off"] + s["w"]]
                    pe.matmul(out, tri[:, which, :], sph_of(n), start=start, stop=False, skip_group_check=True)
                    return pe.matmul(out, tri[:, which, :], spl_of(n), start=False, stop=False, skip_group_check=True)

                def suffix(unit, n):
                    pe.wait_ge(spl_ready, NSTEP * unit + n + 1)
                    add_tri(n, 0, STEPS[n]["first"]).then_inc(s_full, 1)

                def carry_on(unit, n):
                    pe.wait_ge(arg_ready, NSTEP * unit + n + 1)
                    if not STEPS[n]["last"]:
                        add_tri(n, 1, False).then_inc(carried, 1)

                def values(unit, n):
                    s = STEPS[n]
                    pe.wait_ge(wtl_ready, NSTEP * unit + n + 1)
                    if s["first"] and s["h"] != 1:
                        pe.wait_ge(v_lo, NV * unit + (V_LOW, V_HIGH, V_CACHE)[s["g"]] + 1)
                        if s["g"] > 0:
                            pe.wait_ge(o_done, 3 * unit + s["g"])
                        elif mode != FIRST:
                            pe.wait_ge(o_done, 3 * unit)
                    heads = (s["h"],) if s["h"] is not None else (0, 1)
                    wt_hi, wt_lo = wth_of(n), wtl_of(n)
                    for x, h in enumerate(heads):
                        w = s["w"] // len(heads)
                        vc = slice(s["kb"] * VW + HD * h, s["kb"] * VW + HD * h + P)
                        wc = slice(x * w, (x + 1) * w)
                        last = split3(pe, O[:, s["off"]:s["off"] + w], vh[:, vc], vl[:, vc], wt_hi[:, wc], wt_lo[:, wc],
                                      start=s["first"] and h == 0, stop=False, group=False)
                    last.then_inc(av_done, 1)

                for tick in ticks(mode):
                    for a in stage(unit, mode, tick, 3):
                        suffix(*a)
                    for a in stage(unit, mode, tick, 0):
                        scores(*a)
                    for a in stage(unit, mode, tick, 5):
                        values(*a)
                    if mode != TAIL:
                        if tick == 1:
                            pe.wait_ge(proj_out, 9 * unit + 9)
                            turn_values(VT, unit, 0, 4)
                        elif tick == 3:
                            pe.wait_ge(v_lo, NV * unit + V_LOW + 1)
                            turn_values(VT, unit, 4, 4)
                        elif tick == 5:
                            pe.wait_ge(v_lo, NV * unit + V_HIGH + 1)
                            turn_values(VT, unit, SEQ // P, 1)
                        proj_part(unit + 1, tick // 3, tick % 3, 3)
                    for a in stage(unit, mode, tick, 3):
                        carry_on(*a)

            def diff_unit(unit, head, filler):
                def scores(t):
                    if t["i"] == 0:
                        pe.wait_ge(qk_lo, NQK * unit + K_PROMPT + 1)
                    elif t["k0"]:
                        pe.wait_ge(qk_lo, NQK * unit + K_CACHE + 1)
                    for m in range(2):
                        if t["i"] >= 1:
                            pe.wait_ge(ds_read, 2 * NTILE * head + 2 * (t["i"] - 1) + m + 1)
                        r = slice(HD * m, HD * m + HD)
                        for c in range(0, t["nk"], 512):
                            w = min(512, t["nk"] - c)
                            qc, kc = slice(t["q0"], t["q0"] + P), slice(t["k0"] + c, t["k0"] + c + w)
                            last = split3(pe, DS[m][:, c // 512, 0:w], qh[r, qc], ql[r, qc], kh[r, kc], kl[r, kc],
                                          start=True, stop=True)
                        last.then_inc(ds_full, 1)

                def turn(t, g, gn):
                    if g == 0:
                        pe.wait_ge(dw_ready, NTILE * head + t["i"] + 1)
                    if gn >= 1:
                        pe.wait_ge(dwl_ready, NGRP * head + gn)
                    else:
                        pe.wait_ge(v_lo, NV * unit + V_HIGH + 1)
                    for x, b in enumerate(t["groups"][g]):
                        last = pe.transpose(DT[:, x * P:(x + 1) * P], maps[:, t["i"] % 2, 0, b * P:(b + 1) * P], ident)
                    last.then_inc(dt_full, 1)

                def values(t, g, gn):
                    pe.wait_ge(dwl_ready, NGRP * head + gn + 1)
                    if t["k0"]:
                        pe.wait_ge(v_lo, NV * unit + V_CACHE + 1)
                    if g == 0 and t["i"] >= 2:
                        pe.wait_ge(do_done, NTILE * head + t["i"] - 1)
                    out = DO[:, (t["i"] % 2) * P:(t["i"] % 2) * P + t["nq"]]
                    for x, b in enumerate(t["groups"][g]):
                        kb = t["k0"] // P + b
                        vc, wc = slice(kb * P, (kb + 1) * P), slice(x * P, x * P + t["nq"])
                        last = split3(pe, out, vh[:, vc], vl[:, vc], dwh[:, gn % 2, wc], dwl[:, gn % 2, wc],
                                      start=g == 0 and x == 0, stop=b == t["groups"][-1][-1])
                    last.then_inc(dav_done, 1)

                def fill(tick, half):
                    if filler:
                        if tick < NTILE:
                            proj_part(unit + 1, tick, half, 2)
                    elif 0 < tick < DIFF_UNITS:
                        sub_sums(tick - 1, range(2 * half, min(NT, 2 * half + 2)))
                    elif tick >= EARLY_TICK:
                        out_part(tick - EARLY_TICK, half, 2)

                gn = 0
                for tick in range(NTILE + 1):
                    if tick < NTILE:
                        scores(TILES[tick])
                    if tick == 0:
                        fill(0, 0)
                        pe.wait_ge(proj_out, 9 * unit + 9)
                        turn_values(VT, unit, 0, 4)
                        turn_values(DT, unit, 4, 4)
                        turn_values(DVT, unit, SEQ // P, 1)
                    t = TILES[tick - 1] if tick else None
                    if t:
                        turn(t, 0, gn)
                    if tick:
                        fill(tick, 0)
                    if t:
                        values(t, 0, gn)
                        gn += 1
                        if len(t["groups"]) > 1:
                            turn(t, 1, gn)
                    fill(tick, 1)
                    if t and len(t["groups"]) > 1:
                        values(t, 1, gn)
                        gn += 1
                pe.drain().then_inc(unit_done, 1)

            pe.wait_ge(const_in, 32)
            pe.wait_ge(lam_prod, 1)
            pe.matmul(psC[:, 0, 0:2], ones[0:HD, :], lamp[:], start=True, stop=True).then_inc(lam_sum, 1)
            ffn(PIECE_FF1, 0, 0, 0, 0)
            with pe.Fori(1, FF_ITERS) as i:
                ffn(PIECE_FF1, i, 0)
            pe.wait_ge(y_done, 8 * FF_ITERS + 7)
            out_stats(1)
            first_product(Piece(PIECE_IN), 2, KC).then_inc(proj_full, 3)
            pe.wait_ge(sample_ln, 2)
            dense(psB, Piece(PIECE_IN + 1), xh, xl).then_inc(proj_full, 3)
            for f in range(6, 9):
                proj_part(0, f, 0, 1)
            sb_unit(0, FIRST)
            with pe.Fori(1, SB_UNITS) as i:
                sb_unit(i, MIDDLE)
            sb_unit(SB_UNITS, TAIL)
            pe.drain().then_inc(unit_done, 1)
            pe.wait_ge(o_done, 3 * SB_UNITS)
            with pe.Fori(0, DIFF_UNITS - 1) as i:
                diff_unit(i + SB_UNITS, i, True)
            diff_unit(UNITS - 1, DIFF_UNITS - 1, False)
            for w in range(NTILE + 1 - EARLY_TICK, NT * EARLY):
                out_part(w, 0, 1)
            for t in range(NT):
                if t == 0:
                    pe.wait_ge(w_ready, Piece(PIECE_OUT + EARLY).count)
                    pe.wait_ge(do_done, NTILE * DIFF_UNITS)
                elif t == 1:
                    sub_sums(DIFF_UNITS - 1)
                out_products(psB[:, t, 0:TT], EARLY, t, range(KC - 1), True, False)
            pe.wait_ge(x_ready, 3 * KC)
            for n, d in enumerate(OUT_ORDER):
                ps = (psA, psB)[n % 2]
                if n == 0:
                    pe.wait_ge(early_out, NT * EARLY)
                    pe.wait_ge(sub_ln, NT * DIFF_UNITS)
                elif n >= 2:
                    pe.wait_ge(wo_out, n - 1)
                if d <= EARLY:
                    for t in range(NT):
                        last = out_products(ps[:, t, 0:TT], d, t, [KC - 1], False, True) if d == EARLY else \
                            last_head(ps[:, t, 0:TT], d, t)
                    last.then_inc(wo_full, 1)
                else:
                    dense(ps, Piece(PIECE_OUT + d), xh, xl).then_inc(wo_full, 1)
            pe.wait_ge(wo_out, KC - 1)
            out_stats(3)
            ffn(PIECE_FF2, 0, FF_ITERS, 4, 3 * KC)
            with pe.Fori(1, FF_ITERS) as i:
                ffn(PIECE_FF2, i, FF_ITERS)
            pe.wait_ge(y_done, 8 * 2 * FF_ITERS + 7)
            out_stats(5)
            stats(6)

        @block.scalar
        def _(act):
            def split_hi(piece):
                act.wait_ge(raw_in[piece.slot], piece.landed)
                act.activation(wh[:, piece.slot, :, :], raw[:, piece.slot, :, :], ACT.Copy).then_inc(w_hi, 1)

            def root(norm):
                act.activation(tiles3(rstd[:]), bank3(psA), ACT.Ln, scale=1.0 / D_MODEL, bias=EPS).then_inc(ln_done, 1)
                act.wait_ge(ln_done, norm + 1)
                act.activation(rstd[:], rstd[:], ACT.Exp, scale=-0.5).then_inc(rstd_ready, 1)

            def square(norm, k):
                if norm > 0 or k >= 2:
                    act.wait_ge(sums, KC * (norm // 2) + k - 1)
                act.activation(sq[:, k % 2, :], resid[:, k, :], ACT.Square).then_inc(sq_ready, 1)

            def input_hi(norm, g, k):
                square(norm, k)
                act.activation(xh[:, k, :], resid[:, k, :], ACT.Copy,
                               scale=gains[:, KC * g + k:KC * g + k + 1]).then_inc(xh_ready, 1)

            def input_root(norm, rstd=rstd):
                act.wait_ge(sums, KC * (norm // 2 + 1))
                act.activation(rstd[:, SEQ:T], spare, ACT.Ln, scale=1.0 / D_MODEL, bias=EPS).then_inc(sample_ln, 1)
                act.activation(rstd[:, 0:SEQ], psC[:].rearrange("p a b -> p (a b)"), ACT.Ln, scale=1.0 / D_MODEL,
                               bias=EPS).then_inc(ln_done, 1)
                act.wait_ge(ln_done, norm + 1)
                act.activation(rstd[:], rstd[:], ACT.Exp, scale=-0.5).then_inc(rstd_ready, 1)

            def out_square(norm, k, chunk=None):
                if 2 <= k < KC - 1:
                    act.wait_ge(out_sum, (SUMMED - 1) * (norm // 2) + k - 1)
                act.activation(tmp[:, 0, :] if k == KC - 1 else sq[:, min(k, 1), :], y[:, k if chunk is None else chunk, :], ACT.Square).then_inc(out_sq, 1)

            def out_root(norm):
                act.wait_ge(out_sums, norm // 2 + 1)
                root(norm)

            def ffn_norm(norm):
                act.preload_act_table_set("natural_log_exp_and_others")
                for k in range(KC):
                    act.wait_ge(y_done, 8 * (norm // 4 + 1) * FF_ITERS + k + 1)
                    out_square(norm, k)

            def ffn(base, i, n_it, last=False, late=True):
                ii = i + n_it
                piece = [Piece(base + j, i, FF_PIECES) for j in range(2 * FF_PIECES)]

                def silu(j):
                    for t in range(NT):
                        act.wait_ge(gate_done, 6 * ii + 3 * j + t + 1)
                        act.activation(tmp[:, j, tile(t)], tmp[:, j, tile(t)], ACT.Silu).then_inc(silu_done, 1)

                def hidden_hi(j):
                    for t in range(NT):
                        c = slice(t * TT, (t + 1) * TT)
                        act.wait_ge(h_done, 6 * ii + 3 * j + t + 1)
                        act.activation(hh[:, j, c], tmp[:, j, c], ACT.Copy).then_inc(hh_done, 1)

                silu(0)
                split_hi(piece[3])
                hidden_hi(0)
                split_hi(piece[4])
                silu(1)
                split_hi(piece[5])
                hidden_hi(1)
                if not last:
                    split_hi(piece[6])
                if not last and late:
                    act.wait_ge(fullB, 6 * ii + 6)
                    split_hi(piece[7])
                    split_hi(piece[8])

            act.preload_act_table_set("natural_log_exp_and_others")
            act.wait_ge(lam_sum, 1)
            act.activation(lame[:], psC[:, 0, 0:2], ACT.Exp).then_inc(lam_exp, 1)
            split_hi(Piece(0))
            act.wait_ge(const_in, 32)
            for k in range(KC):
                act.wait_ge(x_in[k], 16)
                input_hi(0, G_FF1_PRE, k)
            split_hi(Piece(1))
            input_root(0)
            act.preload_act_table_set("silu_and_others")
            split_hi(Piece(2))
            with act.Fori(0, FF_ITERS - 1) as i:
                ffn(PIECE_FF1, i, 0)
            ffn(PIECE_FF1, FF_ITERS - 1, 0, late=False)
            ffn_norm(1)
            split_hi(Piece(PIECE_IN + 1))
            out_root(1)
            split_hi(Piece(PIECE_IN + 2))
            for k in range(KC):
                act.wait_ge(r_ready, k + 1)
                input_hi(2, G_MIX_PRE, k)
            input_root(2, mix_rstd)

            def proj_evac(unit, f, bank=None):
                act.wait_ge(proj_full, 9 * unit + f + 1)
                bank = psA[:, f % 2, 0:TT] if bank is None else bank
                act.activation(qkv[:, f // 3, (f % 3) * TT:(f % 3 + 1) * TT], bank, ACT.Copy,
                               scale=HD ** -0.5 if f < 3 else 1.0).then_inc(proj_raw, 1)

            def qk_high(unit, part, pair=True):
                if part == Q_PROMPT:
                    act.wait_ge(proj_out, 9 * unit + 3)
                    last = act.activation(qh[:, 0:SEQ], qkv[:, 0, 0:SEQ], ACT.Copy)
                elif part == K_PROMPT:
                    act.wait_ge(proj_out, 9 * unit + 6)
                    last = act.activation(kh[:, 0:SEQ], qkv[:, 1, 0:SEQ], ACT.Copy)
                elif part == Q_SAMPLE and pair:
                    for h in range(2):
                        last = act.activation(sample_q(qsh, h), qkv[HD * h:HD * h + HD, 0, SEQ:T], ACT.Copy)
                elif part == Q_SAMPLE:
                    last = act.activation(qh[:, SEQ:TP], qkv[:, 0, SEQ:TP], ACT.Copy)
                elif part == K_SAMPLE:
                    last = act.activation(kh[:, SEQ:TP], qkv[:, 1, SEQ:TP], ACT.Copy)
                else:
                    act.wait_ge(cache_in, 16 * unit + 16)
                    last = act.activation(kh[:, TP:KCOLS], kc[:], ACT.Copy)
                last.then_inc(qk_hi, 1)

            def v_high(unit, part, v_out, bank=None):
                if part == V_CACHE:
                    act.wait_ge(cache_v_in, 32 * unit + 32)
                else:
                    act.wait_ge(vt_full, NVT * unit + part + 1)
                b, n, src = v_part(part, v_out, bank)
                act.activation(v_out(vh, b, n), src, ACT.Copy).then_inc(v_hi, 1)

            def next_evac(unit, f):
                if f == 0:
                    act.wait_ge(qk_lo, NQK * unit + K_PROMPT + 1)
                elif f == 2:
                    act.wait_ge(qk_lo, NQK * unit + Q_SAMPLE + 1)
                elif f == 3:
                    act.wait_ge(kv_stored, 32 * unit + 32)
                elif f == 5:
                    act.wait_ge(qk_lo, NQK * unit + K_SAMPLE + 1)
                elif f == 6:
                    act.wait_ge(vt_full, NVT * unit + NVT)
                proj_evac(unit + 1, f)

            def sb_unit(unit, mode):
                def sp_hi(unit, n):
                    act.wait_ge(sp_ready, NSTEP * unit + n + 1)
                    if 2 <= n < NBIG:
                        if STEPS[n - 2]["last"]:
                            act.wait_ge(s_full, NSTEP * unit + n - 1)
                        else:
                            act.wait_ge(carried, NCARRY * unit + CARRIES[n - 2] + 1)
                    act.activation(sph_of(n), u_of(n), ACT.Copy).then_inc(sph_ready, 1)

                def weight_exp(unit, n):
                    act.wait_ge(arg_ready, NSTEP * unit + n + 1)
                    act.activation(zs_of(n), zs_of(n), ACT.Exp).then_inc(wt_ready, 1)

                def soft_exp(unit, n):
                    act.wait_ge(u_ready, NSTEP * unit + n + 1)
                    act.activation(u_of(n), u_of(n), ACT.Exp).then_inc(e_ready, 1)

                def weight_hi(unit, n):
                    act.wait_ge(wt_ready, NSTEP * unit + n + 1)
                    if 2 <= n < NBIG:
                        act.wait_ge(av_done, NSTEP * unit + n - 1)
                    elif n < 2 and mode != FIRST:
                        act.wait_ge(av_done, NSTEP * (unit - 1) + NBIG - 2 + n + 1)
                    act.activation(wth_of(n), zs_of(n), ACT.Copy).then_inc(wth_ready, 1)

                def soft_ln(unit, n):
                    act.wait_ge(e_ready, NSTEP * unit + n + 1)
                    act.activation(u_of(n), u_of(n), ACT.Ln, bias=1.0).then_inc(l_ready, 1)

                for tick in ticks(mode):
                    if mode != TAIL and tick == 0:
                        proj_evac(unit, 8)
                    for lag, work in ((4, weight_hi), (1, soft_exp), (2, sp_hi), (1, soft_ln), (3, weight_exp)):
                        for a in stage(unit, mode, tick, lag):
                            work(*a)
                    if mode == TAIL:
                        continue
                    if tick == 1:
                        split_hi(Piece(PIECE_IN + 5, unit, 3))
                        v_high(unit, V_LOW, v_pair, VT)
                    elif tick == 2:
                        qk_high(unit, Q_SAMPLE)
                    elif tick == 3:
                        v_high(unit, V_HIGH, v_pair, VT)
                    elif tick == 4:
                        qk_high(unit, K_SAMPLE)
                    elif tick == 5:
                        v_high(unit, V_SAMPLE, v_pair, VT)
                    elif tick == 7:
                        v_high(unit, V_CACHE, v_pair)
                    elif tick == 8:
                        qk_high(unit, K_CACHE)
                    if tick and tick % 3 == 0:
                        next_evac(unit, tick // 3 - 1)
                    if tick and tick % 9 == 0:
                        split_hi(Piece(PIECE_IN + 3 + tick // 9 - 1, unit + 1, 3))
                    if tick == NBIG:
                        act.wait_ge(z_full, NSTEP * unit + NBIG)
                        qk_high(unit + 1, Q_PROMPT)
                        qk_high(unit + 1, K_PROMPT)

            def sub_square(e):
                act.activation(sub_squares(e), y[:, SB_UNITS + e, :], ACT.Square).then_inc(sub_sq, 1)

            def sub_root(e):
                for t in range(NT):
                    act.wait_ge(sub_sum, NT * e + t + 1)
                    act.activation(sub_rstd_of(e)[:, tile(t)], sub_bank(NT * e + t), ACT.Ln, scale=1.0 / P,
                                   bias=EPS).then_inc(sub_ln, 1)
                act.wait_ge(sub_ln, NT * e + NT)
                act.activation(sub_rstd_of(e), sub_rstd_of(e), ACT.Exp, scale=-0.5).then_inc(sub_rstd, 1)

            def out_hi(d):
                act.activation(xh[:, d, :], y[:, d, :], ACT.Copy).then_inc(xh_ready, 1)

            def sub_hi(e):
                act.wait_ge(sub_scaled, e + 1)
                act.activation(xh[:, SB_UNITS + e, :], y[:, SB_UNITS + e, :], ACT.Copy).then_inc(xh_ready, 1)

            def early_evac(w):
                act.wait_ge(early_full, w + 1)
                act.activation(y[:, w // NT, tile(w % NT)], psA[:, (SUB_TILES + w) % 2, 0:TT], ACT.Copy).then_inc(early_out, 1)

            def diff_unit(unit, head, filler):
                def exps(t):
                    s = t["i"] % 2
                    act.wait_ge(nm_ready, NTILE * head + t["i"] + 1)
                    for m in range(2):
                        act.activation(maps[:, s, m, 0:t["nk"]], maps[:, s, m, 0:t["nk"]], ACT.Exp, bias=nm[:, s, m:m + 1],
                                       accum_out=ls[:, s, m:m + 1]).then_inc(de_done, 1)

                def turned_hi(t, g, gn):
                    w = P * len(t["groups"][g])
                    act.wait_ge(dt_full, NGRP * head + gn + 1)
                    if gn >= 2:
                        act.wait_ge(dav_done, NGRP * head + gn - 1)
                    act.activation(dwh[:, gn % 2, 0:w], DT[:, 0:w], ACT.Copy).then_inc(dwh_ready, 1)

                gn = 0
                for tick in range(NTILE + 1):
                    if tick == 0:
                        proj_evac(unit, 8)
                        act.wait_ge(unit_done, head + 1)
                        v_high(unit, V_LOW, v_one, VT)
                        v_high(unit, V_HIGH, v_one, DT)
                        v_high(unit, V_SAMPLE, v_one, DVT)
                    elif tick == NTILE and filler:
                        act.wait_ge(ds_full, 2 * NTILE * head + 2 * NTILE)
                        qk_high(unit + 1, Q_PROMPT)
                        qk_high(unit + 1, K_PROMPT)
                    t = TILES[tick - 1] if tick else None
                    if t:
                        turned_hi(t, 0, gn)
                        gn += 1
                    if tick < NTILE:
                        exps(TILES[tick])
                    if t and len(t["groups"]) > 1:
                        turned_hi(t, 1, gn)
                        gn += 1
                    if tick == 0:
                        split_hi(Piece(PIECE_IN + 5, unit, 3))
                        qk_high(unit, Q_SAMPLE, pair=False)
                    elif tick == 1:
                        qk_high(unit, K_SAMPLE)
                        qk_high(unit, K_CACHE)
                    elif tick == 3:
                        v_high(unit, V_CACHE, v_one)
                    if filler and 0 < tick < NTILE:
                        next_evac(unit, tick - 1)
                        if tick % 3 == 0:
                            split_hi(Piece(PIECE_IN + 3 + tick // 3 - 1, unit + 1, 3))
                    if not filler:
                        if tick == 0:
                            act.wait_ge(do_done, NTILE * (DIFF_UNITS - 1))
                            act.wait_ge(o_done, 3 * SB_UNITS)
                        elif tick < DIFF_UNITS:
                            sub_root(tick - 1)
                        if tick < 2:
                            out_hi(2 * tick)
                            out_hi(2 * tick + 1)
                        if 2 <= tick <= DIFF_UNITS:
                            sub_hi(tick - 2)
                        if tick > EARLY_TICK:
                            early_evac(tick - EARLY_TICK - 1)

            for f in range(8):
                if f == 2:
                    act.wait_ge(spilled, 16 * KC)
                    act.wait_ge(zeroed, 5)
                proj_evac(0, f, (psA, psB)[f // 3][:, f % 3, 0:TT] if f < 6 else None)
                if f % 3 == 2:
                    split_hi(Piece(PIECE_IN + 3 + f // 3))
                if f in (2, 5):
                    qk_high(0, f // 3)
            sb_unit(0, FIRST)
            with act.Fori(1, SB_UNITS) as i:
                sb_unit(i, MIDDLE)
            sb_unit(SB_UNITS, TAIL)
            with act.Fori(0, DIFF_UNITS - 1) as i:
                diff_unit(i + SB_UNITS, i, True)
            diff_unit(UNITS - 1, DIFF_UNITS - 1, False)
            act.wait_ge(do_done, NTILE * DIFF_UNITS)
            sub_square(DIFF_UNITS - 1)
            for w in range(NTILE - EARLY_TICK, NT * EARLY):
                early_evac(w)
            sub_root(DIFF_UNITS - 1)
            sub_hi(DIFF_UNITS - 1)
            act.wait_ge(kv_stored, 32 * UNITS)
            for n, d in enumerate(OUT_ORDER):
                act.wait_ge(wo_full, max(n, OUT_ORDER.index(n)) + 1)
                split_hi(Piece(PIECE_OUT + 3 + n))
                act.wait_ge(wo_out, n + 1)
                out_square(3, n, d)
            out_root(3)
            for k in range(KC):
                act.wait_ge(r_ready, KC + k + 1)
                input_hi(4, G_FF2_PRE, k)
            input_root(4)
            act.preload_act_table_set("silu_and_others")
            with act.Fori(0, FF_ITERS - 1) as i:
                ffn(PIECE_FF2, i, FF_ITERS)
            ffn(PIECE_FF2, FF_ITERS - 1, FF_ITERS, last=True)
            ffn_norm(5)
            out_root(5)
            for k in range(KC):
                act.wait_ge(r_ready, 2 * KC + k + 1)
                square(6, k)
                act.activation(y[:, k, :], resid[:, k, :], ACT.Copy,
                               scale=gains[:, KC * G_FINAL + k:KC * G_FINAL + k + 1]).then_inc(final_g, 1)
            act.wait_ge(sums, KC * 4)
            root(6)

        @block.vector
        def _(dve):
            dve.sem_inc(y_done, 8)

            def split_lo(piece):
                dve.wait_ge(w_hi, piece.count)
                dve.tensor_tensor(wl[:, piece.slot, :, :], raw[:, piece.slot, :, :], wh[:, piece.slot, :, :].bitcast(F32),
                                  ALU.subtract).then_inc(w_ready, 1)

            def square_sum(norm, k):
                n = norm // 2
                dve.wait_ge(out_sq, KC * n + k + 1)
                if k >= 2:
                    dve.wait_ge(out_sum, (SUMMED - 1) * n + k - 1)
                dve.tensor_tensor(sq[:, 0, :], sq[:, 0, :], sq[:, 1, :], ALU.add).then_inc(out_sum, 1)

            def input_lo(g, x_base, k):
                dve.wait_ge(xh_ready, x_base + k + 1)
                dve.scalar_tensor_tensor(xl[:, k, :], resid[:, k, :], gains[:, KC * g + k:KC * g + k + 1],
                                         xh[:, k, :].bitcast(F32), ALU.mult, ALU.subtract).then_inc(x_ready, 1)

            def post(norm, g, low=None):
                n = norm // 2
                dve.wait_ge(rstd_ready, norm + 1)

                def add(k):
                    if k < POST_DVE:
                        dve.wait_ge(scaled_v, POST_DVE * n + k + 1)
                    else:
                        dve.wait_ge(scaled_p, (KC - POST_DVE) * n + k - POST_DVE + 1)
                    dve.scalar_tensor_tensor(resid[:, k, :], y[:, k, :], gains[:, KC * g + k:KC * g + k + 1],
                                             resid[:, k, :], ALU.mult, ALU.add).then_inc(r_ready, 1)

                for k in range(KC):
                    if k < POST_DVE:
                        dve.tensor_tensor(y[:, k, :], y[:, k, :], rstd[:], ALU.mult).then_inc(scaled_v, 1)
                    add(k)
                    if k >= 1 and low:
                        low(k - 1)
                if low:
                    low(KC - 1)

            def ffn(base, i, n_it, last=False, norm=None):
                ii = i + n_it
                piece = [Piece(base + j, i, FF_PIECES) for j in range(2 * FF_PIECES)]

                def gate(j):
                    dve.wait_ge(fullA, 6 * ii + j + 1)
                    for t in range(NT):
                        dve.tensor_tensor(tmp[:, j, tile(t)], psA[:, t, 0:TT], rstd[:, tile(t)], ALU.mult).then_inc(gate_done, 1)

                def hidden(j):
                    dve.wait_ge(fullB, 6 * ii + j + 1)
                    for t in range(NT):
                        c = slice(t * TT, (t + 1) * TT)
                        dve.wait_ge(scaled_silu, 6 * ii + 3 * j + t + 1)
                        dve.tensor_tensor(tmp[:, j, c], psB[:, t, 0:TT], tmp[:, j, c], ALU.mult).then_inc(h_done, 1)
                    for t in range(NT):
                        c = slice(t * TT, (t + 1) * TT)
                        dve.wait_ge(hh_done, 6 * ii + 3 * j + t + 1)
                        dve.tensor_tensor(hl[:, j, c], tmp[:, j, c], hh[:, j, c].bitcast(F32), ALU.subtract).then_inc(hl_done, 1)

                gate(0)
                split_lo(piece[3])
                hidden(0)
                split_lo(piece[4])
                gate(1)
                split_lo(piece[5])
                hidden(1)
                if not last:
                    split_lo(piece[6])
                for d in range(KC):
                    ps, full = ((psA, fullA), (psB, fullB))[d % 2]
                    dve.wait_ge(full, 6 * ii + 2 + d // 2 + 1)
                    dve.wait_ge(y_done, 8 * ii + d + 1)
                    if d == 0:
                        dve.wait_ge(y_zero, 1 if n_it == 0 else 2)
                    dve.tensor_tensor(tiles3(y[:, d, :]), bank3(ps), tiles3(y[:, d, :]), ALU.add).then_inc(y_done, 1)
                    if norm is not None and 2 <= d <= SUMMED:
                        square_sum(norm, d - 1)
                if norm is None:
                    split_lo(piece[7])
                    split_lo(piece[8])

            dve.wait_ge(lam_in, 16)
            dve.tensor_tensor(lamp[:], lamv[:, 0:2], lamv[:, 2:4], ALU.mult).then_inc(lam_prod, 1)
            dve.wait_ge(lam_exp, 1)
            dve.scalar_tensor_tensor(neglam[:], lame[:, 1:2], LAM_INIT, lame[:, 0:1], ALU.subtract, ALU.subtract).then_inc(lam_half, 1)

            dve.wait_ge(const_in, 32)
            dve.tensor_copy(tri[:], cst[:, 2:4, :]).then_inc(setup_v, 1)
            for g in (G_FF1_POST, G_FF2_POST):
                dve.tensor_scalar(gains[:, KC * g:KC * g + KC], gains[:, KC * g:KC * g + KC], 0.5, None, ALU.mult).then_inc(setup_v, 1)
            dve.tensor_scalar(gains[:, G_SUBLN:G_SUBLN + 1], gains[:, G_SUBLN:G_SUBLN + 1], 1.0 - LAM_INIT, None,
                              ALU.mult).then_inc(setup_v, 1)
            dve.wait_ge(setup_v, 4)
            split_lo(Piece(0))
            for k in range(KC):
                input_lo(G_FF1_PRE, 0, k)
            split_lo(Piece(1))
            split_lo(Piece(2))
            dve.wait_ge(rstd_ready, 1)
            with dve.Fori(0, FF_ITERS - 1) as i:
                ffn(PIECE_FF1, i, 0)
            ffn(PIECE_FF1, FF_ITERS - 1, 0, norm=1)
            split_lo(Piece(PIECE_IN + 1))
            post(1, G_FF1_POST, lambda k: input_lo(G_MIX_PRE, KC, k))
            split_lo(Piece(PIECE_IN + 2))

            def qk_low(unit, part, pair=True):
                dve.wait_ge(qk_hi, NQK * unit + part + 1)

                def low(o, src, hi):
                    return dve.tensor_tensor(o, src, hi.bitcast(F32), ALU.subtract)

                if part == Q_PROMPT:
                    last = low(ql[:, 0:SEQ], qkv[:, 0, 0:SEQ], qh[:, 0:SEQ])
                elif part == K_PROMPT:
                    last = low(kl[:, 0:SEQ], qkv[:, 1, 0:SEQ], kh[:, 0:SEQ])
                elif part == Q_SAMPLE and pair:
                    for h in range(2):
                        last = low(sample_q(qsl, h), qkv[HD * h:HD * h + HD, 0, SEQ:T], sample_q(qsh, h))
                elif part == Q_SAMPLE:
                    last = low(ql[:, SEQ:TP], qkv[:, 0, SEQ:TP], qh[:, SEQ:TP])
                elif part == K_SAMPLE:
                    last = low(kl[:, SEQ:TP], qkv[:, 1, SEQ:TP], kh[:, SEQ:TP])
                else:
                    last = low(kl[:, TP:KCOLS], kc[:], kh[:, TP:KCOLS])
                last.then_inc(qk_lo, 1)

            def v_low(unit, part, v_out, bank=None):
                dve.wait_ge(v_hi, NV * unit + part + 1)
                b, n, src = v_part(part, v_out, bank)
                dve.tensor_tensor(v_out(vl, b, n), src, v_out(vh, b, n).bitcast(F32),
                                  ALU.subtract).then_inc(v_lo, 1)

            def sb_unit(unit, mode):
                def masked(unit, n, first, out, table, op, whole, ready):
                    s = STEPS[n]
                    if not s["diag"]:
                        first.then_inc(ready, 1)
                        return
                    first.then_inc(whole, 1)
                    dve.wait_ge(whole, NMASKED * unit + MASKED[n] + 1)
                    heads = 1 if s["h"] is not None else 2
                    w = P if heads == 1 else DEC_SEQ
                    for x in range(heads):
                        last = dve.tensor_tensor(out[:, x * w:(x + 1) * w], out[:, x * w:(x + 1) * w], table[:, 0:w], op)
                    last.then_inc(ready, 1)

                def scores_out(unit, n):
                    dve.wait_ge(z_full, NSTEP * unit + n + 1)
                    if ZS <= n < NBIG:
                        dve.wait_ge(wtl_ready, NSTEP * unit + n - ZS + 1)
                    dve.tensor_copy(zs_of(n), Z[n % 2][:, 0:STEPS[n]["w"]]).then_inc(zs_ready, 1)

                def softplus(unit, n):
                    dve.wait_ge(l_ready, NSTEP * unit + n + 1)
                    masked(unit, n, dve.tensor_tensor(u_of(n), zs_of(n), u_of(n), ALU.max), u_of(n), m01, ALU.mult,
                           sp_whole, sp_ready)

                def argument(unit, n):
                    s = STEPS[n]
                    dve.wait_ge(s_full, NSTEP * unit + n + 1)
                    masked(unit, n, dve.tensor_tensor(zs_of(n), zs_of(n), S[s["bank"]][:, s["off"]:s["off"] + s["w"]],
                                                      ALU.subtract), zs_of(n), mneg, ALU.min, arg_whole, arg_ready)

                def sp_lo(unit, n):
                    dve.wait_ge(sph_ready, NSTEP * unit + n + 1)
                    dve.tensor_tensor(spl_of(n), u_of(n), sph_of(n).bitcast(F32), ALU.subtract).then_inc(spl_ready, 1)

                def weight_lo(unit, n):
                    dve.wait_ge(wth_ready, NSTEP * unit + n + 1)
                    dve.tensor_tensor(wtl_of(n), zs_of(n), wth_of(n).bitcast(F32), ALU.subtract).then_inc(wtl_ready, 1)

                def output(unit, n):
                    s = STEPS[n]
                    if s["last"] and s["h"] != 0:
                        dve.wait_ge(av_done, NSTEP * unit + n + 1)
                        w = 512 if s["h"] is not None else DEC_SEQ
                        dve.tensor_copy(y[:, bass.ds(unit, 1), s["g"] * 512:s["g"] * 512 + w],
                                        O[:, 0:w].rearrange("p (o c) -> p o c", o=1)).then_inc(o_done, 1)

                for tick in ticks(mode):
                    for lag, work in ((2, softplus), (3, argument), (0, scores_out), (2, sp_lo), (4, weight_lo)):
                        for a in stage(unit, mode, tick, lag):
                            work(*a)
                    if mode != TAIL:
                        if tick == 2:
                            v_low(unit, V_LOW, v_pair, VT)
                        elif tick == 3:
                            qk_low(unit, Q_SAMPLE)
                        elif tick == 4:
                            v_low(unit, V_HIGH, v_pair, VT)
                        elif tick == 5:
                            qk_low(unit, K_SAMPLE)
                        elif tick == 6:
                            v_low(unit, V_SAMPLE, v_pair, VT)
                        elif tick == 8:
                            v_low(unit, V_CACHE, v_pair)
                        elif tick == 9:
                            qk_low(unit, K_CACHE)
                    for a in stage(unit, mode, tick, 5):
                        output(*a)

            def sub_scale(e):
                d = SB_UNITS + e
                dve.wait_ge(sub_rstd, e + 1)
                dve.scalar_tensor_tensor(y[:, d, :], y[:, d, :], gains[:, G_SUBLN:G_SUBLN + 1], sub_rstd_of(e),
                                         ALU.mult, ALU.mult).then_inc(sub_scaled, 1)

            def out_lo(d):
                dve.wait_ge(xh_ready, 2 * KC + d + 1)
                dve.tensor_tensor(xl[:, d, :], y[:, d, :], xh[:, d, :].bitcast(F32), ALU.subtract).then_inc(x_ready, 1)

            def next_slope():
                dve.tensor_scalar(dist[:], dist[:], 0.25, None, ALU.mult).then_inc(dist_ready, 1)

            def diff_unit(unit, head, filler):
                dve.wait_ge(dist_ready, head + 1)

                def biased(t):
                    s = t["i"] % 2
                    if t["i"] >= 2:
                        dve.wait_ge(dw_ready, NTILE * head + t["i"] - 1)
                    for m in range(2):
                        dve.wait_ge(ds_full, 2 * NTILE * head + 2 * t["i"] + m + 1)
                        dve.sem_inc(held, 1)
                        dve.tensor_tensor_reduce(maps[:, s, m, 0:t["nk"]],
                                                 DS[m].rearrange("p a b -> p (a b)")[:, 0:t["nk"]],
                                                 dist[:, t["t0"]:t["t0"] + t["nk"]], 1.0, -3.0e38, ALU.add, ALU.max,
                                                 mx[:, s, m:m + 1]).then_inc(ds_read, 1)
                    dve.wait_ge(ds_read, 2 * NTILE * head + 2 * t["i"] + 2)
                    dve.tensor_scalar(nm[:, s, :], mx[:, s, :], -1.0, None, ALU.mult).then_inc(nm_ready, 1)

                def turned_lo(t, g, gn):
                    w = P * len(t["groups"][g])
                    dve.wait_ge(dwh_ready, NGRP * head + gn + 1)
                    dve.tensor_tensor(dwl[:, gn % 2, 0:w], DT[:, 0:w], dwh[:, gn % 2, 0:w].bitcast(F32),
                                      ALU.subtract).then_inc(dwl_ready, 1)

                def weights(t):
                    s, i = t["i"] % 2, t["i"]
                    dve.wait_ge(de_done, 2 * NTILE * head + 2 * i + 2)
                    dve.reciprocal(rl[:, s, :], ls[:, s, :]).then_inc(rl_ready, 1)
                    dve.wait_ge(rl_ready, NTILE * head + i + 1)
                    dve.tensor_tensor(c2[:, s, :], rl[:, s, 1:2], neglam[:], ALU.mult).then_inc(c2_ready, 1)
                    dve.wait_ge(c2_ready, NTILE * head + i + 1)
                    dve.tensor_scalar(maps[:, s, 1, 0:t["nk"]], maps[:, s, 1, 0:t["nk"]], c2[:, s, :], None,
                                      ALU.mult).then_inc(e2_ready, 1)
                    dve.wait_ge(e2_ready, NTILE * head + i + 1)
                    dve.scalar_tensor_tensor(maps[:, s, 0, 0:t["nk"]], maps[:, s, 0, 0:t["nk"]], rl[:, s, 0:1],
                                             maps[:, s, 1, 0:t["nk"]], ALU.mult, ALU.add).then_inc(dw_ready, 1)

                def output(t, gn):
                    dve.wait_ge(dav_done, NGRP * head + gn)
                    if t["i"] == 0 and not filler:
                        dve.wait_ge(proj_out, 9 * UNITS)
                    dve.tensor_copy(y[:, bass.ds(unit, 1), t["q0"]:t["q0"] + t["nq"]],
                                    DO[:, (t["i"] % 2) * P:(t["i"] % 2) * P + t["nq"]].rearrange("p (o c) -> p o c", o=1)
                                    ).then_inc(do_done, 1)

                gn = 0
                for tick in range(NTILE + 2):
                    if tick == NTILE and filler:
                        dve.wait_ge(ds_read, 2 * NTILE * head + 2 * NTILE)
                        next_slope()
                    if tick >= 2:
                        output(TILES[tick - 2], gn)
                    if tick < NTILE:
                        biased(TILES[tick])
                    if tick == 0:
                        v_low(unit, V_LOW, v_one, VT)
                        v_low(unit, V_HIGH, v_one, DT)
                        v_low(unit, V_SAMPLE, v_one, DVT)
                    if 1 <= tick <= NTILE:
                        t = TILES[tick - 1]
                        for g in range(len(t["groups"])):
                            turned_lo(t, g, gn)
                            gn += 1
                    if tick == NTILE and filler:
                        qk_low(unit + 1, K_PROMPT)
                    if tick < NTILE:
                        weights(TILES[tick])
                    if tick == 0:
                        qk_low(unit, Q_SAMPLE, pair=False)
                    elif tick == 1:
                        qk_low(unit, K_SAMPLE)
                        qk_low(unit, K_CACHE)
                    elif tick == 3:
                        v_low(unit, V_CACHE, v_one)
                    if not filler:
                        if 1 <= tick < DIFF_UNITS:
                            sub_scale(tick - 1)

            dve.wait_ge(lam_half, 1)
            for j in range(2):
                split_lo(Piece(PIECE_IN + 3 + j))
                qk_low(0, j)
            sb_unit(0, FIRST)
            with dve.Fori(1, SB_UNITS) as i:
                sb_unit(i, MIDDLE)
            sb_unit(SB_UNITS, TAIL)
            dve.wait_ge(dist_in, 16)
            next_slope()
            with dve.Fori(0, DIFF_UNITS - 1) as i:
                diff_unit(i + SB_UNITS, i, True)
            diff_unit(UNITS - 1, DIFF_UNITS - 1, False)
            sub_scale(DIFF_UNITS - 1)
            out_lo(KC - 1)
            for n, d in enumerate(OUT_ORDER):
                dve.wait_ge(wo_full, n + 1)
                if d < EARLY:
                    dve.wait_ge(early_out, NT * EARLY)
                    dve.tensor_tensor(tiles3(y[:, d, :]), bank3((psA, psB)[n % 2]), tiles3(y[:, d, :]), ALU.add).then_inc(wo_out, 1)
                else:
                    dve.tensor_copy(tiles3(y[:, d, :]), bank3((psA, psB)[n % 2])).then_inc(wo_out, 1)
                split_lo(Piece(PIECE_OUT + 3 + n))
                if 2 <= n <= SUMMED:
                    square_sum(3, n - 1)
            dve.wait_ge(resid_in, 16 * KC)
            post(3, G_MIX_POST, lambda k: input_lo(G_FF2_PRE, 3 * KC, k))
            dve.wait_ge(rstd_ready, 5)
            with dve.Fori(0, FF_ITERS - 1) as i:
                ffn(PIECE_FF2, i, FF_ITERS)
            ffn(PIECE_FF2, FF_ITERS - 1, FF_ITERS, last=True, norm=5)
            post(5, G_FF2_POST)
            dve.wait_ge(rstd_ready, 7)
            dve.wait_ge(final_g, KC)
            for k in range(FINAL_DVE):
                dve.tensor_tensor(y[:, k, :], y[:, k, :], rstd[:], ALU.mult).then_inc(final_v, 1)

        @block.gpsimd
        def _(pool):
            pool.memset(y[:], 0.0).then_inc(y_zero, 1)

            def post(norm):
                pool.wait_ge(rstd_ready, norm + 1)
                for k in range(POST_DVE, KC):
                    pool.tensor_tensor(y[:, k, :], y[:, k, :], rstd[:], ALU.mult).then_inc(scaled_p, 1)

            def scale_silu(i, n_it):
                for m in range(2 * NT):
                    c = tmp[:, m // NT, tile(m % NT)]
                    pool.wait_ge(silu_done, 6 * (i + n_it) + m + 1)
                    pool.tensor_tensor(c, c, rstd[:, tile(m % NT)], ALU.mult).then_inc(scaled_silu, 1)

            pool.wait_ge(rstd_ready, 1)
            with pool.Fori(0, FF_ITERS) as i:
                scale_silu(i, 0)
            post(1)
            pool.wait_ge(spilled, 16 * KC)
            pool.wait_ge(x_ready, 2 * KC)
            pool.wait_ge(rstd_ready, 3)
            pool.memset(qkv[:, :, T:TP], 0.0).then_inc(zeroed, 1)
            for v in (vh, vl):
                gap = v[:, :].bitcast(F32).rearrange("p (b x d) -> p b x d", x=3, d=HD)[:, :, 1, :]
                pool.memset(gap, 0.0).then_inc(zeroed, 1)

            pool.wait_ge(setup_v, 4)
            for q in (qsh, qsl):
                pool.memset(q[:].bitcast(F32), 0.0).then_inc(zeroed, 1)

            def scale_proj(unit, f):
                pool.wait_ge(proj_raw, 9 * unit + f + 1)
                o = qkv[:, f // 3, tile(f % 3)]
                pool.tensor_tensor(o, o, mix_rstd[:, tile(f % 3)], ALU.mult).then_inc(proj_out, 1)

            def split_lo(piece):
                pool.wait_ge(w_ready, piece.count - 1)
                pool.wait_ge(w_hi, piece.count)
                pool.tensor_tensor(wl[:, piece.slot, :, :], raw[:, piece.slot, :, :], wh[:, piece.slot, :, :].bitcast(F32),
                                   ALU.subtract).then_inc(w_ready, 1)

            def qk_low(unit, part):
                pool.wait_ge(qk_hi, NQK * unit + part + 1)
                lo, hi = ((ql, qh), (kl, kh))[part]
                pool.tensor_tensor(lo[:, 0:SEQ], qkv[:, part, 0:SEQ], hi[:, 0:SEQ].bitcast(F32), ALU.subtract).then_inc(qk_lo, 1)

            def sb_unit(unit):
                for n in range(NSTEP):
                    pool.wait_ge(zs_ready, NSTEP * unit + n + 1)
                    pool.sem_inc(held, 1)
                    pool.tensor_scalar(u_of(n), zs_of(n), U_CLAMP, -3.0e38, ALU.min, ALU.max).then_inc(u_ready, 1)
                    if n == 0:
                        scale_proj(unit, 8)
                    elif n > 3 and n % 3 == 1:
                        scale_proj(unit + 1, n // 3 - 1)
                    if n == 2:
                        split_lo(Piece(PIECE_IN + 5, unit, 3))
                    elif n > 9 and n % 9 == 2:
                        split_lo(Piece(PIECE_IN + 3 + n // 9 - 1, unit + 1, 3))
                    elif n == NBIG:
                        qk_low(unit + 1, Q_PROMPT)
                    elif n == NBIG + 1:
                        qk_low(unit + 1, K_PROMPT)

            for f in range(8):
                scale_proj(0, f)
            with pool.Fori(0, SB_UNITS) as i:
                sb_unit(i)
            with pool.Fori(SB_UNITS, UNITS - 1) as i:
                scale_proj(i, 8)
                split_lo(Piece(PIECE_IN + 5, i, 3))
                for f in range(8):
                    scale_proj(i + 1, f)
                    if f % 3 == 2:
                        split_lo(Piece(PIECE_IN + 3 + f // 3, i + 1, 3))
                qk_low(i + 1, Q_PROMPT)
            scale_proj(UNITS - 1, 8)
            pool.wait_ge(do_done, NTILE * (DIFF_UNITS - 1))
            pool.wait_ge(proj_out, 9 * UNITS)
            for e in range(DIFF_UNITS - 1):
                d = SB_UNITS + e
                pool.tensor_tensor(sub_squares(e), y[:, d, :], y[:, d, :], ALU.mult).then_inc(sub_sq, 1)
            split_lo(Piece(PIECE_IN + 5, UNITS - 1, 3))
            for d in range(KC - 1):
                pool.wait_ge(xh_ready, 2 * KC + d + 1)
                pool.tensor_tensor(xl[:, d, :], y[:, d, :], xh[:, d, :].bitcast(F32), ALU.subtract).then_inc(x_ready, 1)
            post(3)
            pool.wait_ge(r_ready, 2 * KC)
            pool.memset(y[:], 0.0).then_inc(y_zero, 1)
            pool.wait_ge(rstd_ready, 5)
            with pool.Fori(0, FF_ITERS) as i:
                scale_silu(i, FF_ITERS)
            post(5)
            pool.wait_ge(rstd_ready, 7)
            pool.wait_ge(final_g, KC)
            for k in range(FINAL_DVE, KC):
                pool.tensor_tensor(y[:, k, :], y[:, k, :], rstd[:], ALU.mult).then_inc(final_p, 1)


def consts():
    i = np.arange(P)
    k, q = i[:, None], i[None, :]
    before = k < q
    c = np.stack([k == q, np.ones((P, P)), k >= q, k < q, before, before], axis=1).astype(np.float32)
    c[:, 5, :] = np.where(before, 3.0e38, -1.0e30)
    huge = -1.0e30
    dist = np.zeros((P, KCOLS), np.float32)
    x = np.arange(SEQ)[None, :] - (SEQ - P)
    dist[:, :SEQ] = np.where(x // HD <= k // HD, -np.abs(k - x), huge)
    dist[:, SEQ:TP] = np.where(q < DEC_SEQ, -np.abs(k - q), huge)
    dist[:, TP:] = -(PAST + k - np.arange(PAST)[None, :])
    return c.reshape(P, 6 * P), dist


def kernel(**inputs):
    import concourse.bacc as bacc
    from concourse.bass_utils import run_bass_kernel_spmd

    a = {n: np.asarray(v) for n, v in inputs.items()}
    f32 = np.float32

    def in_pieces(w):
        return w.reshape(KC, P, -1, P).transpose(2, 1, 0, 3).reshape(-1, P, KC * P)

    c, dist = consts()
    w_in = in_pieces(a["w_in"][0])
    n_sb, n_d = SB_UNITS, DIFF_UNITS
    order = [j * n_sb + n for n in range(n_sb) for j in range(3)]
    order += [3 * n_sb + j * n_d + n for n in range(n_d) for j in range(3)]
    names = ["ff1_pre_g", "ff1_post_g", "mix_pre_g", "mix_post_g", "ff2_pre_g", "ff2_post_g", "final_g"]
    kc = np.concatenate([a["cache_sb_k"][0, 0].reshape(PAST, -1), a["cache_diff_k"][0, 0].reshape(PAST, -1)], axis=1)
    vc = np.concatenate([a["cache_sb_v"][0, 0].reshape(PAST, -1), a["cache_diff_v"][0, 0].reshape(PAST, -1)], axis=1)
    arrays = {
        "xT": np.concatenate([a["x_prompt"][0], a["x_sample"][0]]).T.reshape(KC, P, T),
        "wg1": in_pieces(a["ff1_w_gate"][0]),
        "wu1": in_pieces(a["ff1_w_up"][0]),
        "wd1": a["ff1_w_down"][0].reshape(-1, P, D_MODEL),
        "w_mix": np.concatenate([w_in[order], in_pieces(a["w_out"][0])]),
        "wg2": in_pieces(a["ff2_w_gate"][0]),
        "wu2": in_pieces(a["ff2_w_up"][0]),
        "wd2": a["ff2_w_down"][0].reshape(-1, P, D_MODEL),
        "k_cache": kc.T.reshape(UNITS, P, PAST),
        "v_cache": vc.reshape(PAST // P, P, UNITS, P).transpose(2, 1, 0, 3).reshape(UNITS, P, PAST),
        "gains": np.concatenate([a[n][0].reshape(KC, P).T for n in names] + [a["subln_g"][0].reshape(P, 1)], axis=1),
        "lam": np.stack([a[n][0] for n in ("lam_q1", "lam_q2", "lam_k1", "lam_k2")], axis=1),
        "consts": c,
        "dist_table": dist,
    }
    outs = {"yT": (KC, P, T), "kv": (2 * UNITS, P, T)}

    nc = bacc.Bacc("TRN2", target_bir_lowering=False, num_devices=1, dynamic_dma_scratch_size=1024)
    arrays = {f"in_{n}": np.ascontiguousarray(v) for n, v in arrays.items()}
    args = [nc.dram_tensor(n, v.shape, mybir.dt.from_np(v.dtype), kind="ExternalInput").ap() for n, v in arrays.items()]
    args += [nc.dram_tensor(f"out_{n}", s, F32, kind="ExternalOutput").ap() for n, s in outs.items()]
    build(nc, *args)
    r = run_bass_kernel_spmd(nc, [arrays], core_ids=[0]).results[0]

    yt = r["out_yT"].reshape(D_MODEL, T).T
    kv = r["out_kv"].reshape(UNITS, 2, P, T)

    def rows(units, which, tokens, heads, width):
        t = kv[units, which].reshape(-1, T).T[tokens]
        return np.ascontiguousarray(t).reshape(1, 1, -1, heads, width)

    sb, df = slice(0, SB_UNITS), slice(SB_UNITS, UNITS)
    out = [np.ascontiguousarray(yt[:SEQ])[None], np.ascontiguousarray(yt[SEQ:])[None]]
    for tokens in (slice(0, SEQ), slice(SEQ, T)):
        out += [rows(sb, 0, tokens, HEADS_SB, HD), rows(sb, 1, tokens, HEADS_SB, HD),
                rows(df, 0, tokens, HEADS_DIFF, 2 * HD), rows(df, 1, tokens, HEADS_DIFF, 2 * HD)]
    return tuple(out)
```
